# Optimizing a Trainium2 kernel written in Bass

```python
import jax
import jax.numpy as jnp
from jax import lax
import numpy as np

D_MODEL = 1024
BATCH = 1
SEQ = 512
DEPTH = 1
DEC_BATCH = 8
DEC_SEQ = 8
PAST_LEN = 2048
PAGE_SIZE = 128

N_HEADS = 8
HEAD_DIM = 64
N_KV_HEADS = 2
Q_PER_KV = N_HEADS // N_KV_HEADS
ATTN_WIDTH = N_HEADS * HEAD_DIM
CMP_BLOCK = 64
TOP_K_BLOCKS = 16
WINDOW = 512
WIN_QBLK = 128
SLC_QBLK = 32
FORCE_SCORE = 1.0e4
POOL_WIDTH = D_MODEL - ATTN_WIDTH
POOL_WINDOWS = (2, 4, 8, 16)
N_POOL_GROUPS = len(POOL_WINDOWS)
POOL_GROUP_WIDTH = POOL_WIDTH // N_POOL_GROUPS
POOL_BUF = max(POOL_WINDOWS) - 1
KV_COLS = 2 * N_KV_HEADS * HEAD_DIM
GATE_COLS = 3 * N_HEADS
IN_COLS = ATTN_WIDTH + 3 * KV_COLS + GATE_COLS + POOL_WIDTH
N_EXPERT_GROUPS = 4
EXPERTS_PER_GROUP = 4
N_EXPERTS = N_EXPERT_GROUPS * EXPERTS_PER_GROUP
D_EXPERT = 512
TOP_K_EXPERTS = 2
EPS = 1e-6
NEG = -1e30

kernel_name = 'hymba_nsa_pool_hmoe_step'

def rmsnorm(x, g):
    xf = x.astype(jnp.float32)
    y = xf * lax.rsqrt(jnp.mean(xf * xf, axis=-1, keepdims=True) + EPS)
    return (y * g.astype(jnp.float32)).astype(x.dtype)

def alibi_slopes():
    s = 2.0 ** (-8.0 * np.arange(1, N_HEADS + 1) / N_HEADS)
    return jnp.asarray(s, dtype=jnp.float32).reshape(N_KV_HEADS, Q_PER_KV)

def masked_softmax(logits, mask):
    z = jnp.where(mask, logits.astype(jnp.float32), NEG)
    m = jnp.max(z, axis=-1, keepdims=True)
    e = jnp.where(mask, jnp.exp(z - m), 0.0)
    den = jnp.sum(e, axis=-1, keepdims=True)
    return e / jnp.where(den > 0, den, 1.0)

def norm_keys(kv, g):
    return jnp.concatenate([rmsnorm(kv[:, :, :1], g), kv[:, :, 1:]], axis=2)

def in_projection(x, norm1_g, w_in, q_norm_g, k_norm_slc_g, k_norm_win_g):
    b, t, _ = x.shape
    p = jnp.einsum('btd,dc->btc', rmsnorm(x, norm1_g), w_in)
    o = [0]
    for w in (ATTN_WIDTH, KV_COLS, KV_COLS, KV_COLS, GATE_COLS, POOL_WIDTH):
        o.append(o[-1] + w)
    kv_shape = (b, t, 2, N_KV_HEADS, HEAD_DIM)
    q = rmsnorm(p[..., o[0]:o[1]].reshape(b, t, N_HEADS, HEAD_DIM), q_norm_g)
    kv_cmp = p[..., o[1]:o[2]].reshape(kv_shape)
    kv_slc = norm_keys(p[..., o[2]:o[3]].reshape(kv_shape), k_norm_slc_g)
    kv_win = norm_keys(p[..., o[3]:o[4]].reshape(kv_shape), k_norm_win_g)
    gates = jax.nn.sigmoid(p[..., o[4]:o[5]].astype(jnp.float32)).reshape(b, t, N_HEADS, 3)
    u_pool = p[..., o[5]:o[6]]
    return q, kv_cmp, kv_slc, kv_win, gates, u_pool

def pad_to_blocks(kv):
    b, t = kv.shape[:2]
    nb = -(-t // CMP_BLOCK)
    kv = jnp.pad(kv, ((0, 0), (0, nb * CMP_BLOCK - t), (0, 0), (0, 0), (0, 0)))
    return kv.reshape(b, nb, CMP_BLOCK, 2, N_KV_HEADS, HEAD_DIM)

def compress_blocks(kv_cmp, cmp_pos_emb, w_cmp_k, w_cmp_v, k_norm_cmp_g):
    blk = pad_to_blocks(kv_cmp) + cmp_pos_emb[None, None, :, None, None, :]
    kc = jnp.einsum('bnlkd,lde->bnke', blk[:, :, :, 0], w_cmp_k)
    vc = jnp.einsum('bnlkd,lde->bnke', blk[:, :, :, 1], w_cmp_v)
    return rmsnorm(kc, k_norm_cmp_g), vc

def compressed_attention(q, q_pos, kc, vc, slopes):
    b, tq = q.shape[:2]
    nb = kc.shape[1]
    qg = q.reshape(b, tq, N_KV_HEADS, Q_PER_KV, HEAD_DIM)
    s = jnp.einsum('bqkgd,bnkd->bkgqn', qg, kc).astype(jnp.float32) * (HEAD_DIM ** -0.5)
    block_end = jnp.arange(nb, dtype=jnp.int32) * CMP_BLOCK + (CMP_BLOCK - 1)
    dist_i = q_pos[:, None] - block_end[None, :]
    mask = dist_i >= 0
    p = masked_softmax(s - slopes[:, :, None, None] * dist_i.astype(jnp.float32), mask)
    o = jnp.einsum('bkgqn,bnkd->bqkgd', p.astype(vc.dtype), vc)
    return o.reshape(b, tq, N_HEADS, HEAD_DIM), p.sum(axis=2)

def select_blocks(p_kv, q_pos, nb):
    j = jnp.arange(nb, dtype=jnp.int32)[None, :]
    qp = q_pos[:, None]
    cand = j * CMP_BLOCK <= qp
    forced = (j == qp // CMP_BLOCK) | (j == 0)
    score = jnp.where(forced, FORCE_SCORE, jnp.where(cand, p_kv, -1.0))
    vals, idx = lax.top_k(score, min(TOP_K_BLOCKS, nb))
    return idx, vals > -0.5

def gather_rows(table, idx):
    return table[idx]

def selected_attention(q, q_pos, kv_blocks, idx, valid, slopes):
    b, tq = q.shape[:2]
    n_sel = idx.shape[-1]
    sel = jax.vmap(jax.vmap(gather_rows))(kv_blocks, idx.reshape(b, N_KV_HEADS, tq * n_sel))
    sel = sel.reshape(b, N_KV_HEADS, tq, n_sel * CMP_BLOCK, 2, HEAD_DIM)
    tok_pos = (idx[..., None] * CMP_BLOCK + jnp.arange(CMP_BLOCK, dtype=jnp.int32)).reshape(
        b, N_KV_HEADS, tq, n_sel * CMP_BLOCK)
    mask = jnp.repeat(valid, CMP_BLOCK, axis=-1) & (tok_pos <= q_pos[:, None])
    dist = (q_pos[:, None] - tok_pos).astype(jnp.float32)
    qg = q.reshape(b, tq, N_KV_HEADS, Q_PER_KV, HEAD_DIM)
    s = jnp.einsum('bqkgd,bkqmd->bkgqm', qg, sel[..., 0, :]).astype(jnp.float32) * (HEAD_DIM ** -0.5)
    p = masked_softmax(s - slopes[None, :, :, None, None] * dist[:, :, None], mask[:, :, None])
    o = jnp.einsum('bkgqm,bkqmd->bqkgd', p.astype(sel.dtype), sel[..., 1, :])
    return o.reshape(b, tq, N_HEADS, HEAD_DIM)

def selected_branch(q, q_pos, kv_slc, idx, valid, slopes):
    b, tq = q.shape[:2]
    blk = pad_to_blocks(kv_slc)
    nb = blk.shape[1]
    kv_blocks = blk.transpose(0, 4, 1, 2, 3, 5).reshape(b, N_KV_HEADS, nb, CMP_BLOCK * 2 * HEAD_DIM)
    if tq > SLC_QBLK and tq % SLC_QBLK == 0:
        n_q = tq // SLC_QBLK
        n_sel = idx.shape[-1]
        qb = q.reshape(b, n_q, SLC_QBLK, N_HEADS, HEAD_DIM).swapaxes(0, 1)
        pb = q_pos.reshape(n_q, SLC_QBLK)
        ib = idx.reshape(b, N_KV_HEADS, n_q, SLC_QBLK, n_sel).transpose(2, 0, 1, 3, 4)
        vb = valid.reshape(b, N_KV_HEADS, n_q, SLC_QBLK, n_sel).transpose(2, 0, 1, 3, 4)
        o = lax.map(lambda a: selected_attention(a[0], a[1], kv_blocks, a[2], a[3], slopes), (qb, pb, ib, vb))
        return o.swapaxes(0, 1).reshape(b, tq, N_HEADS, HEAD_DIM)
    return selected_attention(q, q_pos, kv_blocks, idx, valid, slopes)

def compressed_and_selected(q, q_pos, kv_cmp, kv_slc, cmp_pos_emb, w_cmp_k, w_cmp_v, k_norm_cmp_g, slopes):
    kc, vc = compress_blocks(kv_cmp, cmp_pos_emb, w_cmp_k, w_cmp_v, k_norm_cmp_g)
    o_cmp, p_kv = compressed_attention(q, q_pos, kc, vc, slopes)
    idx, valid = select_blocks(p_kv, q_pos, kc.shape[1])
    o_slc = selected_branch(q, q_pos, kv_slc, idx, valid, slopes)
    return o_cmp, o_slc

def window_attention(q, q_pos, kv, k_pos, slopes):
    b, tq = q.shape[:2]
    qg = q.reshape(b, tq, N_KV_HEADS, Q_PER_KV, HEAD_DIM)
    s = jnp.einsum('bqkgd,bskd->bkgqs', qg, kv[:, :, 0]).astype(jnp.float32) * (HEAD_DIM ** -0.5)
    dist_i = q_pos[:, None] - k_pos[None, :]
    mask = (dist_i >= 0) & (dist_i < WINDOW) & (k_pos[None, :] >= 0)
    p = masked_softmax(s - slopes[:, :, None, None] * dist_i.astype(jnp.float32), mask)
    o = jnp.einsum('bkgqs,bskd->bqkgd', p.astype(kv.dtype), kv[:, :, 1])
    return o.reshape(b, tq, N_HEADS, HEAD_DIM)

def window_attention_prompt(q, kv, slopes):
    b, s = q.shape[:2]
    n_q = s // WIN_QBLK
    kv_pad = jnp.pad(kv, ((0, 0), (WINDOW, 0), (0, 0), (0, 0), (0, 0)))
    qb = q.reshape(b, n_q, WIN_QBLK, N_HEADS, HEAD_DIM).swapaxes(0, 1)

    def one_block(args):
        i, qi = args
        start = i * WIN_QBLK
        kvi = lax.dynamic_slice_in_dim(kv_pad, start, WIN_QBLK + WINDOW, axis=1)
        q_pos = start + jnp.arange(WIN_QBLK, dtype=jnp.int32)
        k_pos = start - WINDOW + jnp.arange(WIN_QBLK + WINDOW, dtype=jnp.int32)
        return window_attention(qi, q_pos, kvi, k_pos, slopes)

    o = lax.map(one_block, (jnp.arange(n_q, dtype=jnp.int32), qb))
    return o.swapaxes(0, 1).reshape(b, s, N_HEADS, HEAD_DIM)

def gate_merge(o_cmp, o_slc, o_win, gates):
    o = gates[..., 0:1] * o_cmp + gates[..., 1:2] * o_slc + gates[..., 2:3] * o_win
    b, t = o.shape[:2]
    return o.reshape(b, t, ATTN_WIDTH).astype(o_cmp.dtype)

def pool_mix(u_ext, n_new, pool_w, pool_scale):
    b, n, _ = u_ext.shape
    uf = u_ext.astype(jnp.float32)
    cs = jnp.concatenate([jnp.zeros((b, 1, POOL_WIDTH), jnp.float32), jnp.cumsum(uf, axis=1)], axis=1)
    rows = np.arange(n - n_new, n)
    outs = []
    for gi, w in enumerate(POOL_WINDOWS):
        lo = np.maximum(rows + 1 - w, 0)
        cnt = jnp.asarray((rows + 1 - lo).astype(np.float32))
        sl = slice(gi * POOL_GROUP_WIDTH, (gi + 1) * POOL_GROUP_WIDTH)
        win_sum = cs[:, rows + 1, sl] - cs[:, lo, sl]
        outs.append(win_sum / cnt[None, :, None] - uf[:, n - n_new:, sl])
    d = jnp.stack(outs, axis=2)
    y = jnp.einsum('bngc,gce->bnge', d, pool_w.astype(jnp.float32)).reshape(b, n_new, POOL_WIDTH)
    return (y * pool_scale.astype(jnp.float32)).astype(u_ext.dtype)

def hier_moe(h, w_router_group, w_router_expert, w_gate, w_up, w_down):
    b, t, d = h.shape
    x = h.reshape(b * t, d)
    pg = jax.nn.softmax(jnp.einsum('nd,dg->ng', x, w_router_group).astype(jnp.float32), axis=-1)
    g_val, g_idx = lax.top_k(pg, 1)
    le = jnp.einsum('nd,de->ne', x, w_router_expert).astype(jnp.float32).reshape(
        -1, N_EXPERT_GROUPS, EXPERTS_PER_GROUP)
    le = jnp.einsum('nge,ng->ne', le, jax.nn.one_hot(g_idx[:, 0], N_EXPERT_GROUPS, dtype=jnp.float32))
    e_val, e_idx = lax.top_k(jax.nn.softmax(le, axis=-1), TOP_K_EXPERTS)
    gate = g_val * (e_val / jnp.sum(e_val, axis=-1, keepdims=True))
    expert_id = g_idx * EXPERTS_PER_GROUP + e_idx
    dense_gate = jnp.sum(jax.nn.one_hot(expert_id, N_EXPERTS, dtype=jnp.float32) * gate[..., None], axis=1)
    y = jnp.zeros((b * t, d), jnp.float32)
    for e in range(N_EXPERTS):
        he = jax.nn.silu(x @ w_gate[e]) * (x @ w_up[e])
        y = y + dense_gate[:, e:e + 1] * (he @ w_down[e]).astype(jnp.float32)
    return y.reshape(b, t, d).astype(h.dtype)

def merge_and_ffn(x, a, m, w_out, norm2_g, w_router_group, w_router_expert, w_gate, w_up, w_down):
    h = x + jnp.einsum('btc,cd->btd', jnp.concatenate([a, m], axis=-1), w_out)
    return h + hier_moe(rmsnorm(h, norm2_g), w_router_group, w_router_expert, w_gate, w_up, w_down)

def gather_pages(cache, page_table):
    db, n_pages = page_table.shape
    rows = cache[page_table]
    return rows.reshape(db, n_pages * cache.shape[1], *cache.shape[2:])

def setup_inputs(seed: int = 0) -> dict:
    key = jax.random.key(seed)
    ks = jax.random.split(key, 24)
    n_pages = PAST_LEN // PAGE_SIZE
    n_used = DEC_BATCH * n_pages
    n_pool = n_used + max(1, n_used // 4)
    win_buf = min(WINDOW, PAST_LEN)

    def nrm(k, shape, s):
        return s * jax.random.normal(k, shape, jnp.float32)

    page_table = jax.random.permutation(ks[0], n_pool)[:n_used].reshape(DEC_BATCH, n_pages).astype(jnp.int32)
    kv_shape = (n_pool, PAGE_SIZE, 2, N_KV_HEADS, HEAD_DIM)
    return {
        'x_prompt': nrm(ks[1], (BATCH, SEQ, D_MODEL), 1.0),
        'x_sample': nrm(ks[2], (DEC_BATCH, DEC_SEQ, D_MODEL), 1.0),
        'cache_cmp_kv': nrm(ks[3], kv_shape, 1.0),
        'cache_slc_kv': nrm(ks[4], kv_shape, 1.0),
        'state_win_kv': nrm(ks[5], (DEC_BATCH, win_buf, 2, N_KV_HEADS, HEAD_DIM), 1.0),
        'state_pool': nrm(ks[6], (DEC_BATCH, POOL_BUF, POOL_WIDTH), 1.0),
        'page_table': page_table,
        'norm1_g': 1.0 + nrm(ks[7], (D_MODEL,), 0.02),
        'w_in': nrm(ks[8], (D_MODEL, IN_COLS), D_MODEL ** -0.5),
        'q_norm_g': 1.0 + nrm(ks[9], (HEAD_DIM,), 0.02),
        'k_norm_cmp_g': 1.0 + nrm(ks[10], (HEAD_DIM,), 0.02),
        'k_norm_slc_g': 1.0 + nrm(ks[11], (HEAD_DIM,), 0.02),
        'k_norm_win_g': 1.0 + nrm(ks[12], (HEAD_DIM,), 0.02),
        'cmp_pos_emb': nrm(ks[13], (CMP_BLOCK, HEAD_DIM), 0.1),
        'w_cmp_k': nrm(ks[14], (CMP_BLOCK, HEAD_DIM, HEAD_DIM), (CMP_BLOCK * HEAD_DIM) ** -0.5),
        'w_cmp_v': nrm(ks[15], (CMP_BLOCK, HEAD_DIM, HEAD_DIM), (CMP_BLOCK * HEAD_DIM) ** -0.5),
        'pool_w': nrm(ks[16], (N_POOL_GROUPS, POOL_GROUP_WIDTH, POOL_GROUP_WIDTH), POOL_GROUP_WIDTH ** -0.5),
        'pool_scale': 1.0 + nrm(ks[17], (POOL_WIDTH,), 0.1),
        'w_out': nrm(ks[18], (D_MODEL, D_MODEL), D_MODEL ** -0.5),
        'norm2_g': 1.0 + nrm(ks[19], (D_MODEL,), 0.02),
        'w_router_group': nrm(ks[20], (D_MODEL, N_EXPERT_GROUPS), D_MODEL ** -0.5),
        'w_router_expert': nrm(ks[21], (D_MODEL, N_EXPERTS), D_MODEL ** -0.5),
        'w_gate': nrm(ks[22], (N_EXPERTS, D_MODEL, D_EXPERT), D_MODEL ** -0.5),
        'w_up': nrm(jax.random.fold_in(ks[23], 1), (N_EXPERTS, D_MODEL, D_EXPERT), D_MODEL ** -0.5),
        'w_down': nrm(jax.random.fold_in(ks[23], 2), (N_EXPERTS, D_EXPERT, D_MODEL), D_EXPERT ** -0.5),
    }

def reference(x_prompt, x_sample, cache_cmp_kv, cache_slc_kv, state_win_kv, state_pool, page_table,
              norm1_g, w_in, q_norm_g, k_norm_cmp_g, k_norm_slc_g, k_norm_win_g, cmp_pos_emb, w_cmp_k,
              w_cmp_v, pool_w, pool_scale, w_out, norm2_g, w_router_group, w_router_expert, w_gate,
              w_up, w_down):
    slopes = alibi_slopes()

    s_len = x_prompt.shape[1]
    q_p, kvc_p, kvs_p, kvw_p, g_p, u_p = in_projection(
        x_prompt, norm1_g, w_in, q_norm_g, k_norm_slc_g, k_norm_win_g)
    pos_p = jnp.arange(s_len, dtype=jnp.int32)
    o_cmp_p, o_slc_p = compressed_and_selected(
        q_p, pos_p, kvc_p, kvs_p, cmp_pos_emb, w_cmp_k, w_cmp_v, k_norm_cmp_g, slopes)
    o_win_p = window_attention_prompt(q_p, kvw_p, slopes)
    a_p = gate_merge(o_cmp_p, o_slc_p, o_win_p, g_p)
    m_p = pool_mix(u_p, s_len, pool_w, pool_scale)
    y_prompt = merge_and_ffn(x_prompt, a_p, m_p, w_out, norm2_g, w_router_group, w_router_expert,
                             w_gate, w_up, w_down)

    ds = x_sample.shape[1]
    past = page_table.shape[1] * cache_cmp_kv.shape[1]
    q_s, kvc_s, kvs_s, kvw_s, g_s, u_s = in_projection(
        x_sample, norm1_g, w_in, q_norm_g, k_norm_slc_g, k_norm_win_g)
    pos_s = past + jnp.arange(ds, dtype=jnp.int32)
    full_cmp = jnp.concatenate([gather_pages(cache_cmp_kv, page_table), kvc_s], axis=1)
    full_slc = jnp.concatenate([gather_pages(cache_slc_kv, page_table), kvs_s], axis=1)
    o_cmp_s, o_slc_s = compressed_and_selected(
        q_s, pos_s, full_cmp, full_slc, cmp_pos_emb, w_cmp_k, w_cmp_v, k_norm_cmp_g, slopes)
    win_buf = state_win_kv.shape[1]
    win_ctx = jnp.concatenate([state_win_kv, kvw_s], axis=1)
    k_pos_s = past - win_buf + jnp.arange(win_buf + ds, dtype=jnp.int32)
    o_win_s = window_attention(q_s, pos_s, win_ctx, k_pos_s, slopes)
    a_s = gate_merge(o_cmp_s, o_slc_s, o_win_s, g_s)
    pool_ext = jnp.concatenate([state_pool, u_s], axis=1)
    m_s = pool_mix(pool_ext, ds, pool_w, pool_scale)
    y_sample = merge_and_ffn(x_sample, a_s, m_s, w_out, norm2_g, w_router_group, w_router_expert,
                             w_gate, w_up, w_down)

    win_keep = min(WINDOW, s_len)
    return (y_prompt, y_sample, kvc_p, kvc_s, kvs_p, kvs_s, kvw_p[:, s_len - win_keep:], win_ctx[:, ds:],
            u_p[:, s_len - POOL_BUF:], pool_ext[:, ds:])


_drawn_inputs = setup_inputs


def setup_inputs(seed=0):
    import zlib

    import numpy as np

    out = dict(_drawn_inputs(seed))
    spreads = {}
    factors = {'q_norm_g': 8.0, 'k_norm_cmp_g': 8.0, 'k_norm_slc_g': 3.916, 'k_norm_win_g': 4.412}
    for name, (base, spread) in spreads.items():
        noise = np.random.default_rng([zlib.crc32(name.encode()), seed]).standard_normal(out[name].shape)
        drawn = base * np.exp(spread * noise) if base else spread * noise
        out[name] = jnp.asarray(drawn.astype(out[name].dtype))
    for name, factor in factors.items():
        out[name] = (out[name] * factor).astype(out[name].dtype)
    return out
```

```python
from contextlib import ExitStack

import concourse.bass as bass
import numpy as np
from concourse import mybir

F32 = mybir.dt.float32
I32 = mybir.dt.int32
ACT = mybir.ActivationFunctionType
ALU = mybir.AluOpType
X = mybir.AxisListType.X

P = 128
D = 1024
KC = D // P
SEQ, DB, DS, PAST = 512, 8, 8, 2048
NS = DB * DS
NT = SEQ + NS
TILES = 5
ROWS = [P, P, P, P, NS]
H, HD, KVH, G = 8, 64, 2, 4
PAGES = PAST // P
NPAGES = DB * PAGES
NBS = PAST // 64
NBP = SEQ // 64
COLS = 1816
WC = COLS // 4
CCMP, CSLC, CWIN, CGATE, CU = 512, 768, 1024, 1280, 1304
WINDOWS = (2, 4, 8, 16)
NE, NG, EPG, DE = 16, 4, 4, 512
CAP = 640
MORE = CAP // P - 1
FIRST = NE * P
EPS = 1e-6
NEG = -1e30
TINY = 1.1754943508222875e-38
PAIRS = 4
SLOTS = 68
NBALL = NPAGES * 2 + NBP
CMP_UNITS = [(0, 8), (9, 8), (34, 8), (48, 8)]
SLOPES = [2.0 ** -(h + 1) for h in range(H)]

SMALL = [("bias_c", NBS), ("new_bias", PAIRS * NS), ("win_bias", 512), ("head", 24), ("pc_bias", 4 * H * NBP), ("slope", H), ("inv_slope", H),
         ("prio", NE), ("prio4", NG), ("expert", NE), ("token", TILES),
         ("row", P), ("valid", TILES)]


def place(h):
    return h % G * KVH + h // G


def spread(ap, axis, n):
    shape = list(ap.shape)
    shape[axis] = n
    return ap.broadcast_to(shape)


def prompt_units():
    return [(b, i, h) for b in range(2) for i in range(4) for h in range(H)]


def compress_steps(u):
    for r, (first, count) in enumerate(CMP_UNITS):
        if first <= u < first + count:
            each = -(-HD // count)
            return [(r, d) for d in range((u - first) * each, min(HD, (u - first + 1) * each))]
    return []


AT_SQUARES, AT_NORM, AT_KEYS, AT_LOGITS, AT_PROBS, AT_SUM, AT_MASK, AT_VALUES = 17, 19, 20, 22, 23, 24, 25, 57


def psum_plan():
    plan, used, nxt = {}, [0] * 8, [0]

    def add(name, bank=None, pool=8):
        if bank is None:
            bank = nxt[0] % pool
            nxt[0] = bank + 1
        plan[name] = (bank, used[bank])
        used[bank] += 1

    for i in range(TILES):
        for half in range(2):
            add(("xT", i, half))
        add(("in", 0, i))
    for c in range(1, 4):
        for i in range(TILES):
            add(("in", c, i))
    for g in range(4):
        for name in ("pool_p", "pool_s", "mix_p", "mix_s"):
            add((name, g))
    for i in range(TILES):
        add(("qT", i))
        add(("kT", i))
    add("gate_rows")
    nxt[0] = 0
    units = prompt_units()
    add(("p_s", 0), pool=5)
    for u in range(len(units) + 1):
        if u + 1 < len(units):
            add(("p_s", u + 1), pool=5)
        for r, d in compress_steps(u):
            if d == 0:
                add(("cmp", r), bank=5)
        for at, names in ((AT_NORM, ["key_norm"]), (AT_LOGITS, ["cmp_s", "pc_s"]), (AT_SUM, ["cmp_sum"]), (AT_VALUES, ["vcT"])):
            if u == at:
                for name in names:
                    add(name, bank=5)
        if u < len(units):
            add(("p_T", u), pool=5)
        if u:
            b, i, h = units[u - 1]
            if h == 0:
                add(("p_o", b, i), bank=6 + i % 2)
    nxt[0] = 0
    for t in range(PAIRS + 1):
        if t < PAIRS:
            for c in range(5):
                if c < 4:
                    for s in range(2):
                        add(("slc_k", t, c, s))
                if c:
                    add(("slc_s", t, c - 1))
            add(("new_s", t))
            for s in range(2):
                add(("win_k", t, s))
            add(("win_s", t))
            add(("neww_s", t))
        if t == 0:
            for i in range(4):
                add(("pc_T", i))
                add(("pc_o", i))
            add("cmp_T")
            add("cmp_o")
        if t:
            for c in range(5):
                add(("slc_T", t - 1, c))
            for c in range(2):
                add(("win_T", t - 1, c))
            for name in ("slc_o", "win_o", "bcast"):
                add((name, t - 1))
    for i in range(4):
        add(("aT", i))
    for i in range(TILES + 1):
        if i < TILES:
            for half in range(2):
                add(("h", i, half))
        if i:
            for half in range(2):
                add(("nT", i - 1, half))
            add(("logit", i - 1))
    add("prefix")
    add("idx")
    return plan, used


def hybrid_step(nc, a, out, scratch):
    with ExitStack() as ctx:
        def sb(name, shape, dt=F32):
            return ctx.enter_context(nc.sbuf_tensor(name, shape, dt))

        def sem(name):
            return ctx.enter_context(nc.semaphore(name))

        def sems(name, n):
            return [sem(f"{name}{i}") for i in range(n)]

        bank = [ctx.enter_context(nc.psum_tensor(f"bank{i}", [P, 512], F32)) for i in range(8)]
        plan, used = psum_plan()
        full, free = sems("bank_full", 8), sems("bank_free", 8)

        def ps(name):
            return bank[plan[name][0]]

        def opened(pe, name):
            b, n = plan[name]
            if n:
                pe.wait_ge(free[b], n)

        def filled(eng, name):
            b, n = plan[name]
            eng.wait_ge(full[b], n + 1)

        def taken(eng, name):
            b, n = plan[name]
            eng.wait_ge(free[b], n + 1)

        def written(ins, name):
            ins.then_inc(full[plan[name][0]], 1)

        def read(ins, name):
            ins.then_inc(free[plan[name][0]], 1)

        arena = sb("arena", [P, 2 * KC * WC + 2 * SLOTS * P])
        proj = sb("proj", [P, TILES, COLS])
        xh = sb("xh", [P, TILES, D])
        amT = sb("amT", [P, KC, NT])
        qT = sb("qT", [P, G, SEQ + 0])
        qTs = sb("qTs", [P, G, NS])
        QB = sb("QB", [P, DB, P])
        kTs = sb("kTs", [P, NT])
        kTw = sb("kTw", [P, NT])
        KCT = sb("KCT", [P, NBALL])
        VC = sb("VC", [P, 3, P])
        mats = sb("mats", [P, 5, P])
        slc_bias = sb("slc_bias", [P, PAST])
        small = sb("small", [P, sum(w for _, w in SMALL)])
        gains = sb("gains", [P, 3, HD])
        cols = sb("cols", [P, 5])
        gate = sb("gate", [P, TILES, 24])
        grow = sb("grow", [P, PAIRS, 3])
        rstd = sb("rstd", [P, 2, TILES])
        nrm = sb("nrm", [P, TILES, 12])
        maskb = sb("maskb", [P, PAIRS, NBS + 1])
        st = sb("st", [P, 96])
        posc = sb("posc", [P, 2])
        kpb = sb("kpb", [P, KVH * NBP])

        ident, ones, upper, gsum, eones = (mats[:, i, :] for i in range(5))
        table, at = {}, 0
        for name, w in SMALL:
            table[name] = small[:, at:at + w]
            at += w

        def view(t, o, *shape):
            n = int(np.prod(shape))
            v = t[:, o:o + n]
            if len(shape) == 2:
                v = v.rearrange("p (a b) -> p a b", b=shape[1])
            if len(shape) == 3:
                v = v.rearrange("p (a b c) -> p a b c", b=shape[1], c=shape[2])
            return v

        xflat = xh[:, :, :].rearrange("p a b -> p (a b)")
        aflat = amT[:, 0:4, :].rearrange("p a b -> p (a b)")
        qflat = qT[:, :, :].rearrange("p a b -> p (a b)")
        pflat = proj[:, :, :].rearrange("p a b -> p (a b)")

        w_in = [view(arena, i * KC * WC, KC, WC) for i in range(2)]
        xn = [view(qflat, i * D, D) for i in range(2)]
        g1b = QB[:, :, :].rearrange("p a b -> p (a b)")
        xnT = amT
        bands = view(slc_bias, 0, 3, 4, P)
        bands_s = view(slc_bias, 3 * 4 * P, 2, 4, NS)
        pool_w = view(kTs, 0, 4, P)
        dT = view(aflat, 512, NT)
        sel = view(aflat, 512 + NT, PAIRS, P)
        statep = view(kTw, 0, 512)
        qsq = view(xflat, 0, TILES, 512)
        ksq = view(qflat, 0, TILES, 256)
        qn = view(xflat, 0, TILES, 512)
        wblk = [view(arena, 0, 32, P), view(xflat, 0, 32, P)]
        posr = VC[:, 0, 0:HD]
        kcr, vcr, ktmp = (view(xflat, 4160 + i * 2 * 132, 2 * 132) for i in range(3))
        cache = [view(arena, 2 * KC * WC + i * SLOTS * P, SLOTS * 2, HD) for i in range(2)]
        pages = [view(arena, i * 4096, PAGES, 2 * P) for i in range(4)]
        Z = 4 * 4096
        pS = [view(slc_bias, i * 512, 512) for i in range(3)]
        dist = view(slc_bias, 3 * 512, 512)
        pT = [view(aflat, i * 512, 512) for i in range(2)]
        tmpo = view(aflat, 1672, 512)
        tmpc = view(qflat, 0, 512)
        vct = view(arena, Z + 7168, NBALL)
        zc = view(xflat, 4952, PAIRS, NBS)
        ec = view(xflat, 4160, PAIRS, NBS)
        score = view(xflat, 4288, PAIRS, NBS + 1)
        pw = view(aflat, 0, PAIRS, P)
        cT = view(aflat, 512, PAIRS, P)
        pcz = view(aflat, 1160, 4, H * NBP)
        pcm = view(aflat, 1416, 4, H * NBP)
        Vblk = view(aflat, 1672, 512)
        pcT = view(arena, Z + 7688, 2, P)
        a_tok = proj[:, 0:4, 0:512]
        SW, WW = PAST + NS, 512 + NS
        S = [view(arena, Z + i * SW, SW) for i in range(2)]
        SN = [view(arena, Z + 2 * SW + i * WW, WW) for i in range(2)]
        kb = [view(arena, Z + 2 * SW + 2 * WW + i * 512, 512) for i in range(4)]
        co = view(arena, Z + 2 * SW + 2 * WW + 2048, PAIRS * P)
        PT = proj[:, :, CU:CU + 512]
        PTw = qT[:, 0:2, 0:512]
        wst = [view(xflat, i * D, 4, 2 * P) for i in range(4)]
        diag = view(qflat, 1024, 3 * P)
        bcs = view(qflat, 1024 + 3 * P, 3 * P)
        t1 = view(qflat, 1024 + 6 * P, P)
        t2 = view(qflat, 1024 + 7 * P, P)
        w_out = view(arena, 0, KC, D)
        n2 = [view(qflat, i * D, D) for i in range(2)]
        n2T = QB
        g2b = view(pflat, 8000, D)
        logits = view(kTs, 0, TILES, NG + NE)
        w_r = sb("w_r", [P, KC, NG + NE])
        r16 = [view(kTs, 100 + i * 80, TILES, NE) for i in range(5)]
        pair16 = view(kTw, 96, 2, TILES * NE).rearrange("p k (i e) -> p k i e", e=NE)
        pos, ex = (view(kTw, 256 + i * 10, 2, TILES) for i in range(2))
        slot_f = view(kTw, 276, 2, TILES)
        over_f = view(kTw, 286, 2, TILES)
        r4 = [view(kTw, 400 + i * 20, TILES, NG) for i in range(4)]
        r1 = [view(kTw, 480 + i * 5, TILES) for i in range(10)]
        gates1 = sb("gates1", [P, 2, TILES])
        gates2 = sb("gates2", [P, 2, TILES])
        inside = sb("inside", [P, 2, TILES])
        row_i = sb("row_i", [P, 2, 2, TILES], I32)
        slot_i = sb("slot_i", [P, 2, TILES], I32)
        tokid = sb("tokid", [P, TILES], I32)
        idx = sb("idx", [P, NE], I32)
        chosen = view(kTw, 0, TILES + 1, NE)
        picks = view(pflat, 5632, 2 * TILES, P)
        tok_at = view(pflat, 5632 + 2 * TILES * P, 2, TILES * NE).rearrange("p k (i e) -> p k i e", e=NE)
        nmax = sb("nmax", [1, 1], I32)

        wslot = [view(arena, i * 4096, 4096) for i in range(6)]
        xg = [view(pflat, i * D, D) for i in range(2)]
        xgT = view(pflat, 2 * D, KC, P)
        sg = view(pflat, 3 * D, DE)
        he = view(pflat, 3 * D + DE, DE)
        heT = view(pflat, 4 * D, DE // P, P)
        ytok = view(pflat, 4 * D + DE, D)
        over_yb = [view(arena, 3 * 4096 + k * D, D) for k in range(2)]
        over_idx = sb("over_idx", [P, 1], I32)
        passed = sb("passed", [1, 1], I32)
        yb = [[view(arena, (2 * i + k) * D, D) for k in range(2)] for i in range(2)]

        ld_x = sems("x_loaded", TILES)
        ld_win = sems("w_in_loaded", 2)
        ld_c1 = sem("first_tables_loaded")
        ld_c2 = sem("pool_tables_loaded")
        ld_c3 = sem("slc_bias_loaded")
        ld_sel = sem("sel_loaded")
        ld_pos = sem("pos_loaded")
        ld_wblk = sems("w_cmp_loaded", 2)
        ld_cache = sems("cmp_pages_loaded", 2)
        ld_dist = sem("dist_loaded")
        ld_pages = sems("slc_pages_loaded", 4)
        ld_values = sems("slc_values_loaded", 4)
        ld_win_state = sems("win_state_loaded", 4)
        ld_xr = sem("x_loaded_again")
        ld_wout = sem("w_out_loaded")
        ld_g2 = sem("g2_loaded")
        ld_zero = sem("slot_table_cleared")
        st_out = sem("outputs_stored")
        st_res = sem("results_stored")
        st_win = sems("win_state_stored", 4)
        act_sq = sem("squares_done")
        dve = sem("dve_step")
        act = sem("act_step")
        pool = sem("pool_step")
        xn_ready = sem("xn_ready")
        ms_ready = sem("mean_square_ready")
        rt_ready = sem("root_ready")
        heads_sq = sem("head_squares_ready")
        heads_ms = sem("head_means_ready")
        heads_rt = sem("head_roots_ready")
        q_ready = sem("q_normed")
        k_ready = sem("k_normed")
        k_step = sem("k_scaled")
        g_exp = sem("gate_exp_ready")
        g_ready = sem("gates_ready")
        cleared = sem("memory_cleared")
        extra = sem("cache_extras_ready")
        kc_sq = sem("kc_squares_ready")
        kc_ms = sem("kc_mean_ready")
        kc_rt = sem("kc_root_ready")
        kct_ready = sem("kc_transposed_ready")
        vct_ready = sem("vc_transposed_ready")
        cz = sem("cmp_logits_ready")
        ce = sem("cmp_exp_ready")
        cp = sem("cmp_p_ready")
        pcz_ready = sem("pc_logits_ready")
        pce = sem("pc_exp_ready")
        pcp = sem("pc_p_ready")
        vb = sem("vblk_ready")
        p_e = sem("prompt_exp_ready")
        p_a = sem("prompt_heads_added")
        s_z = sem("slc_logits_ready")
        s_e = sem("slc_exp_ready")
        w_z = sem("win_logits_ready")
        w_e = sem("win_exp_ready")
        diag_ready = sem("diag_ready")
        qb_ready = sem("qb_ready")
        a_ready = sem("a_sample_ready")
        h_ready = sem("h_ready")
        h_sq = sem("h_squares_ready")
        h_ms = sem("h_mean_ready")
        h_rt = sem("h_root_ready")
        n_ready = sem("n2_ready")
        n_stored = sems("n2_stored", 2)
        qb_clear = sem("qb_cleared")
        z_clear = sem("small_areas_cleared")
        ld_w = sems("expert_matrix_loaded", 6)
        product = sem("expert_product_done")
        xg_ld = sems("tokens_gathered", 2)
        xt_full = sem("gathered_transposed")
        xgt_ready = sem("gathered_copied")
        sg_ready = sem("silu_ready")
        he_ready = sem("hidden_ready")
        ht_full = sem("hidden_transposed")
        ht_taken = sem("hidden_copied")
        y_taken = sem("expert_rows_copied")
        st_y = sem("expert_rows_stored")
        y_ld = sems("expert_rows_gathered", 2)
        y_ready = sem("y_ready")
        head_out = sem("sample_heads_scaled")
        o_idx = sem("more_idx_loaded")
        o_passed = sem("more_idx_passed")
        o_xg = sem("more_tokens_gathered")
        o_w = sem("more_matrices_loaded")
        o_x = sem("more_transposed")
        o_xc = sem("more_copied")
        o_gu = sem("more_gate_up_done")
        o_sg = sem("more_silu_ready")
        o_he = sem("more_hidden_ready")
        o_ht = sem("more_hidden_transposed")
        o_hc = sem("more_hidden_copied")
        o_p = sem("more_product_done")
        o_y = sem("more_rows_copied")
        o_st = sem("more_rows_stored")
        o_yl = sem("more_rows_gathered")
        o_add = sem("more_rows_added")
        r_exp_in = sem("router_exp_in")
        r_exp = sem("router_exp_ready")
        oh_ready = sem("onehots_ready")
        slots_ready = sem("slots_ready")
        scattered = sem("tokens_scattered")
        idx_ready = sem("idx_ready")
        picks_ready = sem("slot_onehots_ready")

        def kb_free(eng, t, j):
            n = 10 * t + j - 4
            if n >= 0:
                t0, j0 = n // 10, n % 10
                filled(eng, ("win_s", t0) if j0 >= 8 else ("slc_s", t0, j0 // 2))

        def crowded(eng):
            eng.wait_ge(slots_ready, 1)
            return eng.value_load(nmax[:, :], min_val=0, max_val=NT) > P

        block = ctx.enter_context(nc.Block())

        @block.sync
        def _(sp):
            for i in range(TILES):
                n = ROWS[i]
                src = a["x_prompt"][0, i * P:(i + 1) * P, :] if i < 4 else a["x_sample"].rearrange("b q d -> (b q) d")
                sp.dma_start(xh[0:n, i, :], src).then_inc(ld_x[i], 16)
                if i == 0:
                    sp.dma_start(g1b, spread(a["norm1_g"].rearrange("(a n) -> a n", a=1), 0, P)).then_inc(ld_c1, 16)
                    sp.dma_start(mats[:, :, :], a["c_mats"]).then_inc(ld_c1, 16)

            def load_win(c):
                src = a["w_in"].rearrange("(k p) c -> p k c", p=P)[:, :, c * WC:(c + 1) * WC]
                sp.dma_start(w_in[c % 2], src).then_inc(ld_win[c % 2], 16)

            load_win(0)
            load_win(1)
            sp.dma_start(small[:, :], a["c_small"]).then_inc(ld_c1, 16)
            for j, name in enumerate(("q_norm_g", "k_norm_slc_g", "k_norm_win_g")):
                sp.dma_start(gains[:, j, :], spread(a[name].rearrange("(a n) -> a n", a=1), 0, P)).then_inc(ld_c1, 16)
            for par in range(2):
                sp.dma_start(cols[64 * par:64 * par + 64, 0:1], a["k_norm_cmp_g"].rearrange("(n a) -> n a", a=1)).then_inc(ld_c1, 16)
            for g in range(4):
                sp.dma_start(cols[:, 1 + g:2 + g], a["pool_scale"][g * P:(g + 1) * P].rearrange("(n a) -> n a", a=1)).then_inc(ld_c1, 16)
            sp.dma_start(w_r[:, :, 0:NG], a["w_router_group"].rearrange("(k p) g -> p k g", p=P)).then_inc(ld_c1, 16)
            sp.dma_start(w_r[:, :, NG:NG + NE], a["w_router_expert"].rearrange("(k p) g -> p k g", p=P)).then_inc(ld_c1, 16)
            sp.dma_start(tokid[:, :], a["c_tokid"]).then_inc(ld_c1, 16)
            sp.dma_start(slc_bias[:, :], a["c_bands"]).then_inc(ld_c2, 16)
            sp.dma_start(pool_w, a["pool_w"].rearrange("g c e -> c g e")).then_inc(ld_c2, 16)
            sp.dma_start(statep[0:120, :], a["state_pool"].rearrange("b r c -> (b r) c")).then_inc(ld_c2, 16)

            table_rows = a["page_table"]
            regs = [sp.alloc_register(f"page{k}") for k in range(PAGES)]

            def load_pages(first, count, emit):
                with sp.Fori(first, first + count) as b:
                    sp.load(regs, table_rows[bass.ds(b, 1), :])
                    for k in range(PAGES):
                        emit(b, k, sp.snap(regs[k], min_val=0, max_val=a["cache_cmp_kv"].shape[0] - 1))

            def load_cache(r):
                which, half = r // 2, r % 2
                if r >= 2:
                    filled(sp, ("cmp", r - 2))

                def one(b, k, page):
                    src = a["cache_cmp_kv"][bass.ds(page, 1), :, which, :, :].rearrange("a p h d -> (a p) h d")
                    dst = cache[half][:, bass.ds((b * PAGES + k - half * 64) * 2, 2), :]
                    sp.dma_start(dst, src).then_inc(ld_cache[half], 16)

                load_pages(4 * half, 4, one)

            def load_wblk(which, part):
                w = a["w_cmp_k"] if which == 0 else a["w_cmp_v"]
                for par in range(2):
                    sp.dma_start(wblk[part][64 * par:64 * par + 64, :, 64 * par:64 * par + 64],
                                 w[:, 32 * part:32 * part + 32, :]).then_inc(ld_wblk[part], 16)

            load_cache(0)
            for c in range(2, 4):
                filled(sp, ("in", c - 2, TILES - 1))
                load_win(c)
            load_cache(1)
            for par in range(2):
                sp.dma_start(posr[64 * par:64 * par + 64, :], a["cmp_pos_emb"]).then_inc(ld_pos, 16)
            filled(sp, ("in", 3, TILES - 1))
            sp.dma_start(sel[0:NS, :, :], a["c_sel"]).then_inc(ld_sel, 16)
            sp.wait_ge(cleared, 4)
            load_wblk(0, 0)
            for name in (("pool_p", 3), ("pool_s", 3)):
                filled(sp, name)
            sp.dma_start(dist, a["c_dist"]).then_inc(ld_dist, 16)
            sp.wait_ge(cleared, 5)
            load_wblk(0, 1)
            load_cache(2)
            filled(sp, ("cmp", 1))
            load_wblk(1, 0)
            load_wblk(1, 1)
            load_cache(3)

            def load_slc(b, first, count):
                sp.load(regs, table_rows[b:b + 1, :])
                for k in range(PAGES):
                    page = sp.snap(regs[k], min_val=0, max_val=a["cache_slc_kv"].shape[0] - 1)
                    src = a["cache_slc_kv"][bass.ds(page, 1), :, first:first + count, :, :].rearrange("a p c h d -> (a p) (c h d)")
                    sp.dma_start(pages[b % 4][:, k, first * P:(first + count) * P], src)\
                        .then_inc((ld_values if first else ld_pages)[b % 4], 16)

            def load_wst(b):
                if b >= 4:
                    filled(sp, ("win_o", b // 2 - 2))
                    sp.wait_ge(st_win[b % 4], 32)
                src = a["state_win_kv"][b].rearrange("(n p) c h d -> p n (c h d)", p=P)
                sp.dma_start(wst[b % 4], src).then_inc(ld_win_state[b % 4], 16)

            filled(sp, ("cmp", 2))
            load_slc(1, 0, 2)
            load_slc(2, 0, 2)
            filled(sp, ("cmp", 3))
            load_slc(0, 0, 2)
            for b in range(3):
                load_wst(b)
            load_slc(3, 0, 2)
            load_wst(3)
            filled(sp, ("p_T", len(prompt_units()) - 1))
            sp.dma_start(slc_bias[:, :], a["c_slc_bias"]).then_inc(ld_c3, 16)
            for t in range(2, PAIRS):
                filled(sp, ("slc_k", t - 2, 3, 1))
                for b in (2 * t, 2 * t + 1):
                    load_slc(b, 0, 1)
            for t in range(2, PAIRS):
                filled(sp, ("slc_o", t - 2))
                for b in (2 * t, 2 * t + 1):
                    load_wst(b)
                    load_slc(b, 1, 1)
            filled(sp, ("slc_o", 2))
            for g in range(G):
                for h2 in range(KVH):
                    r0 = (h2 * G + g) * HD
                    sp.dma_start(w_out[64 * h2:64 * h2 + 64, g, :], a["w_out"][r0:r0 + HD, :]).then_inc(ld_wout, 16)
            sp.dma_start(w_out[:, 4:8, :], a["w_out"][512:1024, :].rearrange("(k p) c -> p k c", p=P)).then_inc(ld_wout, 16)
            for t in (2, 3):
                filled(sp, ("win_o", t))
            for i in range(4):
                sp.wait_ge(st_win[i], 64)
            for i in range(TILES):
                n = ROWS[i]
                src = a["x_prompt"][0, i * P:(i + 1) * P, :] if i < 4 else a["x_sample"].rearrange("b q d -> (b q) d")
                sp.dma_start(xh[0:n, i, :], src).then_inc(ld_xr, 16)
            for i in range(4):
                filled(sp, ("aT", i))
            sp.dma_start(g2b, spread(a["norm2_g"].rearrange("(a n) -> a n", a=1), 0, P)).then_inc(ld_g2, 16)

            def load_matrix(e, j, slot):
                if j < 2:
                    w = (a["w_gate"], a["w_up"])[j]
                    dst = wslot[slot].rearrange("p (k f) -> p k f", k=KC)
                    src = w[bass.ds(e, 1), :, :].rearrange("a (k p) f -> p (a k) f", p=P)
                else:
                    dst = wslot[slot].rearrange("p (k f) -> p k f", k=DE // P)
                    src = a["w_down"][bass.ds(e, 1), :, :].rearrange("a (k p) f -> p (a k) f", p=P)
                sp.dma_start(dst, src).then_inc(ld_w[slot], 16)

            load_matrix(0, 0, 2)
            load_matrix(0, 1, 3)
            sp.wait_ge(a_ready, PAIRS)
            load_matrix(0, 2, 4)
            load_matrix(1, 0, 5)
            filled(sp, ("h", TILES - 1, 1))
            load_matrix(1, 1, 0)
            load_matrix(1, 2, 1)
            with sp.Fori(1, NE // 2) as it:
                for j in range(6):
                    sp.wait_ge(product, it * 6 + (j - 5))
                    load_matrix(it * 2 + j // 3, j % 3, (j + 2) % 6)

            with sp.If(crowded(sp)):
                sp.wait_ge(product, 3 * NE)
                with sp.Fori(0, NE) as e:
                    sp.wait_ge(o_p, e * MORE)
                    for j in range(3):
                        if j < 2:
                            dst = wslot[j].rearrange("p (k f) -> p k f", k=KC)
                            src = (a["w_gate"], a["w_up"])[j][bass.ds(e, 1), :, :].rearrange("a (k p) f -> p (a k) f", p=P)
                        else:
                            dst = wslot[j].rearrange("p (k f) -> p k f", k=DE // P)
                            src = a["w_down"][bass.ds(e, 1), :, :].rearrange("a (k p) f -> p (a k) f", p=P)
                        sp.dma_start(dst, src).then_inc(o_w, 16)

            for i in range(TILES):
                n = ROWS[i]
                sp.wait_ge(y_ready, i + 1)
                dst = out["y_prompt"][0, i * P:(i + 1) * P, :] if i < 4 else out["y_sample"].rearrange("b q d -> (b q) d")
                sp.dma_start(dst, xh[0:n, i, :]).then_inc(st_res, 16)
            sp.wait_ge(st_res, 16 * TILES)

        @block.tensor
        def _(pe):
            pe.wait_ge(ld_c1, 32)

            def xT(i):
                n = ROWS[i]
                pe.wait_ge(xn_ready, i + 1)
                for half in range(2):
                    opened(pe, ("xT", i, half))
                    for k in range(4):
                        c = (half * 4 + k) * P
                        last = pe.transpose(ps(("xT", i, half))[:, k * P:k * P + n], xn[i % 2][0:n, c:c + P], ident[0:n, 0:n])
                    written(last, ("xT", i, half))

            for c in range(4):
                for i in range(TILES):
                    n = ROWS[i]
                    if c == 0:
                        xT(i)
                        for half in range(2):
                            taken(pe, ("xT", i, half))
                    if i == 0:
                        pe.wait_ge(ld_win[c % 2], 16 * (c // 2 + 1))
                    opened(pe, ("in", c, i))
                    for k in range(KC):
                        last = pe.matmul(ps(("in", c, i))[0:n, 0:WC], xnT[:, k, i * P:i * P + n], w_in[c % 2][:, k, :],
                                         start=k == 0, stop=k == KC - 1)
                    written(last, ("in", c, i))

            for i in range(TILES):
                taken(pe, ("in", 3, i))
                taken(pe, ("in", 2, i))
            pe.wait_ge(ld_c2, 16 * 3)
            for g in range(4):
                u = lambda i, n: proj[0:n, i, CU + g * P:CU + (g + 1) * P]
                opened(pe, ("pool_p", g))
                for i in range(4):
                    o = ps(("pool_p", g))[:, i * P:(i + 1) * P]
                    last = pe.matmul(o, u(i, P), bands[:, 0 if i == 0 else 1, g, :], start=True, stop=i == 0)
                    if i:
                        last = pe.matmul(o, u(i - 1, P), bands[:, 2, g, :], start=False, stop=True)
                written(last, ("pool_p", g))
                opened(pe, ("pool_s", g))
                o = ps(("pool_s", g))[:, 0:NS]
                pe.matmul(o, u(4, NS), bands_s[0:NS, 0, g, :], start=True, stop=False)
                last = pe.matmul(o, statep[0:120, g * P:(g + 1) * P], bands_s[0:120, 1, g, :], start=False, stop=True)
                written(last, ("pool_s", g))
                taken(pe, ("pool_p", g))
                taken(pe, ("pool_s", g))
                opened(pe, ("mix_p", g))
                written(pe.matmul(ps(("mix_p", g))[:, :], pool_w[:, g, :], dT[:, 0:SEQ], start=True, stop=True), ("mix_p", g))
                opened(pe, ("mix_s", g))
                written(pe.matmul(ps(("mix_s", g))[:, 0:NS], pool_w[:, g, :], dT[:, SEQ:NT], start=True, stop=True), ("mix_s", g))

            def compress(r, d):
                which, half = r // 2, r % 2
                if d == 0:
                    pe.wait_ge(ld_cache[half], (which + 1) * 64 * 16)
                    pe.wait_ge(extra, (1, 2, 2, 3)[r])
                    opened(pe, ("cmp", r))
                if d % 32 == 0:
                    pe.wait_ge(ld_wblk[d // 32], 32 * (which + 1))
                nmov = 130 if half == 0 else 136
                last = pe.matmul(ps(("cmp", r))[:, 0:nmov], wblk[d // 32][:, d % 32, :], cache[half][:, 0:nmov, d],
                                 start=d == 0, stop=d == HD - 1)
                if d == HD - 1:
                    written(last, ("cmp", r))

            pe.wait_ge(q_ready, 1)
            pe.wait_ge(k_ready, 2 * TILES)
            for i in range(TILES):
                n = ROWS[i]
                opened(pe, ("qT", i))
                for j in range(G):
                    last = pe.transpose(ps(("qT", i))[:, j * P:j * P + n], qn[0:n, i, j * P:(j + 1) * P], ident[0:n, 0:n])
                written(last, ("qT", i))
                opened(pe, ("kT", i))
                for j, c in enumerate((CSLC, CWIN)):
                    last = pe.transpose(ps(("kT", i))[:, j * P:j * P + n], proj[0:n, i, c:c + P], ident[0:n, 0:n])
                written(last, ("kT", i))
            pe.wait_ge(g_ready, 1)
            pe.wait_ge(ld_sel, 16)
            opened(pe, "gate_rows")
            for t in range(PAIRS):
                last = pe.matmul(ps("gate_rows")[:, t * 24:t * 24 + 24], sel[0:NS, t, :], gate[0:NS, 4, :], start=True, stop=True)
            written(last, "gate_rows")

            def beside(u):
                if u == AT_NORM:
                    pe.wait_ge(kc_sq, 1)
                    opened(pe, "key_norm")
                    written(pe.matmul(ps("key_norm")[:, 0:264], eones, ktmp, start=True, stop=True), "key_norm")
                if u == AT_LOGITS:
                    pe.wait_ge(kct_ready, 6)
                    pe.wait_ge(qb_ready, 16)
                    opened(pe, "cmp_s")
                    for t in range(PAIRS):
                        for s in range(2):
                            b = 2 * t + s
                            last = pe.matmul(ps("cmp_s")[:, t * NBS:(t + 1) * NBS], QB[:, b, :], KCT[:, b * NBS:(b + 1) * NBS],
                                             start=s == 0, stop=s == 1)
                    written(last, "cmp_s")
                    opened(pe, "pc_s")
                    for i in range(4):
                        for j in range(G):
                            c = i * H * NBP + j * 2 * NBP
                            last = pe.matmul(ps("pc_s")[:, c:c + 2 * NBP], qT[:, j, i * P:(i + 1) * P], kpb[:, :], start=True, stop=True)
                    written(last, "pc_s")
                if u == AT_SUM:
                    pe.wait_ge(cp, 1)
                    opened(pe, "cmp_sum")
                    written(pe.matmul(ps("cmp_sum")[:, 0:P], gsum, zc.rearrange("p a b -> p (a b)"), start=True, stop=True), "cmp_sum")
                if u == AT_VALUES:
                    pe.wait_ge(vct_ready, 4)
                    opened(pe, "vcT")
                    for j, n in enumerate((P, P, NBP)):
                        last = pe.transpose(ps("vcT")[0:n, j * P:(j + 1) * P], vct[:, j * P:j * P + n], ident)
                    written(last, "vcT")

            def cmp_values():
                pe.wait_ge(vb, 16 * H)
                pe.wait_ge(pcp, 1)
                for i in range(4):
                    opened(pe, ("pc_T", i))
                    written(pe.transpose(ps(("pc_T", i))[0:64, 0:P], pcz[:, i, :], ident), ("pc_T", i))
                    taken(pe, ("pc_T", i))
                    opened(pe, ("pc_o", i))
                    written(pe.matmul(ps(("pc_o", i))[:, :], pcT[0:64, i % 2, :], Vblk[0:64, :], start=True, stop=True), ("pc_o", i))
                pe.wait_ge(cp, 2)
                opened(pe, "cmp_T")
                for t in range(PAIRS):
                    last = pe.transpose(ps("cmp_T")[:, t * P:(t + 1) * P], pw[:, t, :], ident)
                written(last, "cmp_T")
                taken(pe, "cmp_T")
                taken(pe, "vcT")
                opened(pe, "cmp_o")
                for t in range(PAIRS):
                    last = pe.matmul(ps("cmp_o")[:, t * P:(t + 1) * P], VC[:, t // 2, :], cT[:, t, :], start=True, stop=True)
                written(last, "cmp_o")

            units = prompt_units()

            def p_scores(u):
                b, i, h = units[u]
                k0, n = 64 * (h // G), (i + 1) * P
                kt = (kTs, kTw)[b]
                opened(pe, ("p_s", u))
                written(pe.matmul(ps(("p_s", u))[:, 0:n], qT[k0:k0 + 64, h % G, i * P:(i + 1) * P], kt[k0:k0 + 64, 0:n],
                                  start=True, stop=True), ("p_s", u))

            p_scores(0)
            for u in range(len(units) + 1):
                if u + 1 < len(units):
                    p_scores(u + 1)
                for r, d in compress_steps(u):
                    compress(r, d)
                beside(u)
                if u < len(units):
                    b, i, h = units[u]
                    pe.wait_ge(p_e, u + 1)
                    opened(pe, ("p_T", u))
                    for c in range(i + 1):
                        last = pe.transpose(ps(("p_T", u))[:, c * P:(c + 1) * P], pS[u % 3][:, c * P:(c + 1) * P], ident)
                    written(last, ("p_T", u))
                if u:
                    b, i, h = units[u - 1]
                    taken(pe, ("p_T", u - 1))
                    if h == 0:
                        opened(pe, ("p_o", b, i))
                    v0 = (CSLC, CWIN)[b] + P + 64 * (h // G)
                    for c in range(i + 1):
                        last = pe.matmul(ps(("p_o", b, i))[:, place(h) * HD:(place(h) + 1) * HD], pT[(u - 1) % 2][:, c * P:(c + 1) * P],
                                         proj[:, c, v0:v0 + HD], start=c == 0, stop=c == i)
                    if h == H - 1:
                        written(last, ("p_o", b, i))

            def s_scores(t):
                for c in range(5):
                    if c < 4:
                        for s in range(2):
                            b = 2 * t + s
                            if c == 0:
                                pe.wait_ge(ld_pages[b % 4], 16 * PAGES * (b // 4 + 1))
                            name = ("slc_k", t, c, s)
                            opened(pe, name)
                            for k in range(4):
                                last = pe.transpose(ps(name)[:, k * P:(k + 1) * P], pages[b % 4][:, 4 * c + k, 0:P], ident)
                            written(last, name)
                    if c:
                        name = ("slc_s", t, c - 1)
                        opened(pe, name)
                        for s in range(2):
                            taken(pe, ("slc_k", t, c - 1, s))
                            last = pe.matmul(ps(name)[:, :], QB[:, 2 * t + s, :], kb[(10 * t + 2 * (c - 1) + s) % 4],
                                             start=s == 0, stop=s == 1)
                        written(last, name)
                name = ("new_s", t)
                opened(pe, name)
                for s in range(2):
                    last = pe.matmul(ps(name)[:, 0:NS], QB[:, 2 * t + s, :], kTs[:, SEQ:NT], start=s == 0, stop=s == 1)
                written(last, name)
                for s in range(2):
                    b = 2 * t + s
                    pe.wait_ge(ld_win_state[b % 4], 16 * (b // 4 + 1))
                    name = ("win_k", t, s)
                    opened(pe, name)
                    for k in range(4):
                        last = pe.transpose(ps(name)[:, k * P:(k + 1) * P], wst[b % 4][:, k, 0:P], ident)
                    written(last, name)
                name = ("win_s", t)
                opened(pe, name)
                for s in range(2):
                    taken(pe, ("win_k", t, s))
                    last = pe.matmul(ps(name)[:, :], QB[:, 2 * t + s, :], kb[(10 * t + 8 + s) % 4], start=s == 0, stop=s == 1)
                written(last, name)
                name = ("neww_s", t)
                opened(pe, name)
                for s in range(2):
                    last = pe.matmul(ps(name)[:, 0:NS], QB[:, 2 * t + s, :], kTw[:, SEQ:NT], start=s == 0, stop=s == 1)
                written(last, name)

            def s_values(t):
                for b in (2 * t, 2 * t + 1):
                    if b >= 4:
                        pe.wait_ge(ld_values[b % 4], 16 * PAGES)
                pe.wait_ge(s_e, t + 1)
                for c in range(5):
                    name = ("slc_T", t, c)
                    opened(pe, name)
                    if c < 4:
                        for k in range(4):
                            o = (4 * c + k) * P
                            last = pe.transpose(ps(name)[:, k * P:(k + 1) * P], S[t % 2][:, o:o + P], ident)
                    else:
                        last = pe.transpose(ps(name)[0:NS, 0:P], S[t % 2][:, PAST:SW], ident)
                    written(last, name)
                pe.wait_ge(w_e, t + 1)
                for c in range(2):
                    name = ("win_T", t, c)
                    opened(pe, name)
                    if c == 0:
                        for k in range(4):
                            last = pe.transpose(ps(name)[:, k * P:(k + 1) * P], SN[t % 2][:, k * P:(k + 1) * P], ident)
                    else:
                        last = pe.transpose(ps(name)[0:NS, 0:P], SN[t % 2][:, 512:WW], ident)
                    written(last, name)
                name = ("slc_o", t)
                opened(pe, name)
                for c in range(5):
                    taken(pe, ("slc_T", t, c))
                for s in range(2):
                    o = ps(name)[:, 64 * s:64 * s + 64]
                    for k in range(PAGES):
                        c0 = (k % 4) * P + 64 * s
                        pe.matmul(o, pages[(2 * t + s) % 4][:, k, P:2 * P], PT[:, k // 4, c0:c0 + 64], start=k == 0, stop=False)
                    last = pe.matmul(o, proj[0:NS, 4, CSLC + P:CSLC + 2 * P], PT[0:NS, 4, 64 * s:64 * s + 64],
                                     start=False, stop=True)
                written(last, name)
                name = ("win_o", t)
                opened(pe, name)
                for c in range(2):
                    taken(pe, ("win_T", t, c))
                for s in range(2):
                    o = ps(name)[:, 64 * s:64 * s + 64]
                    for k in range(4):
                        c0 = k * P + 64 * s
                        pe.matmul(o, wst[(2 * t + s) % 4][:, k, P:2 * P], PTw[:, 0, c0:c0 + 64], start=k == 0, stop=False)
                    last = pe.matmul(o, proj[0:NS, 4, CWIN + P:CWIN + 2 * P], PTw[0:NS, 1, 64 * s:64 * s + 64],
                                     start=False, stop=True)
                written(last, name)
                pe.wait_ge(diag_ready, t + 1)
                name = ("bcast", t)
                opened(pe, name)
                written(pe.matmul(ps(name)[:, 0:3 * P], ones, diag, start=True, stop=True), name)

            for t in range(PAIRS + 1):
                if t < PAIRS:
                    s_scores(t)
                if t == 0:
                    cmp_values()
                if t:
                    s_values(t - 1)

            pe.wait_ge(p_a, 12)
            pe.wait_ge(a_ready, PAIRS)
            for i in range(4):
                opened(pe, ("aT", i))
                for j in range(G):
                    last = pe.transpose(ps(("aT", i))[:, j * P:(j + 1) * P], a_tok[:, i, j * P:(j + 1) * P], ident)
                written(last, ("aT", i))
            pe.wait_ge(ld_wout, 16 * 9)
            for i in range(TILES + 1):
                if i < TILES:
                    n = ROWS[i]
                    if i < 4:
                        taken(pe, ("aT", i))
                    for half in range(2):
                        opened(pe, ("h", i, half))
                        for k in range(KC):
                            last = pe.matmul(ps(("h", i, half))[0:n, :], amT[:, k, i * P:i * P + n],
                                             w_out[:, k, half * 512:(half + 1) * 512], start=k == 0, stop=k == KC - 1)
                        written(last, ("h", i, half))
                if i:
                    n = ROWS[i - 1]
                    pe.wait_ge(n_ready, i)
                    for half in range(2):
                        opened(pe, ("nT", i - 1, half))
                        for k in range(4):
                            c = (half * 4 + k) * P
                            last = pe.transpose(ps(("nT", i - 1, half))[:, k * P:k * P + n], n2[(i - 1) % 2][0:n, c:c + P],
                                                ident[0:n, 0:n])
                        written(last, ("nT", i - 1, half))
                    for half in range(2):
                        taken(pe, ("nT", i - 1, half))
                    opened(pe, ("logit", i - 1))
                    for k in range(KC):
                        last = pe.matmul(ps(("logit", i - 1))[0:n, 0:NG + NE], n2T[:, k, 0:n], w_r[:, k, :],
                                         start=k == 0, stop=k == KC - 1)
                    written(last, ("logit", i - 1))
            pe.wait_ge(oh_ready, 1)
            opened(pe, "prefix")
            both = chosen[:, :, :].rearrange("p a b -> p (a b)")
            n = (TILES + 1) * NE
            pe.matmul(ps("prefix")[:, 0:n], upper, both, start=True, stop=False)
            for k in range(1, TILES + 1):
                last = pe.matmul(ps("prefix")[:, k * NE:n], ones, both[:, 0:n - k * NE], start=False, stop=k == TILES)
            written(last, "prefix")
            opened(pe, "idx")
            for n in range(2 * TILES):
                i, k = n // 2, n % 2
                pe.wait_ge(picks_ready, n + 1)
                last = pe.matmul(ps("idx")[:, 0:NE], picks[:, n, :], tok_at[:, k, i, :], start=n == 0, stop=n == 2 * TILES - 1)
            written(last, "idx")

            for b in range(8):
                pe.wait_ge(free[b], used[b])
            BG, BU, BX, BH, BY = bank[0], bank[1], (bank[2], bank[3]), bank[4], (bank[5], bank[6])

            def gathered_T(slot, turn):
                pe.wait_ge(xg_ld[slot], turn)
                for half in range(2):
                    for k in range(4):
                        c = (half * 4 + k) * P
                        last = pe.transpose(BX[half][:, k * P:(k + 1) * P], xg[slot][:, c:c + P], ident)
                last.then_inc(xt_full, 1)

            def expert(it, s, last_one):
                e = it * 2 + s
                pe.wait_ge(xgt_ready, e * 2 + 2)
                for j in range(2):
                    slot = (3 * s + j + 2) % 6
                    pe.wait_ge(ld_w[slot], it * 16 + 16)
                    pe.wait_ge((sg_ready, he_ready)[j], e)
                    for k in range(KC):
                        ins = pe.matmul((BG, BU)[j][:, :], xgT[:, k, :], wslot[slot][:, k * DE:(k + 1) * DE],
                                        start=k == 0, stop=k == KC - 1)
                    ins.then_inc(product, 1)
                if not last_one:
                    gathered_T((s + 1) % 2, (it + (s + 1) // 2) * 16 + 16)
                pe.wait_ge(he_ready, e + 1)
                for k in range(DE // P):
                    ins = pe.transpose(BH[:, k * P:(k + 1) * P], he[:, k * P:(k + 1) * P], ident)
                ins.then_inc(ht_full, 1)
                slot = (3 * s + 4) % 6
                pe.wait_ge(ld_w[slot], it * 16 + 16)
                pe.wait_ge(ht_taken, e + 1)
                pe.wait_ge(y_taken, e * 2)
                for half in range(2):
                    for k in range(DE // P):
                        c = k * D + half * 512
                        ins = pe.matmul(BY[half][:, :], heT[:, k, :], wslot[slot][:, c:c + 512], start=k == 0, stop=k == DE // P - 1)
                ins.then_inc(product, 1)

            gathered_T(0, 16)
            with pe.Fori(0, NE // 2 - 1) as it:
                for s in range(2):
                    expert(it, s, False)
            for s in range(2):
                expert(NE // 2 - 1, s, s == 1)

            with pe.If(crowded(pe)):
                pe.wait_ge(y_taken, 2 * NE)
                with pe.Fori(0, NE) as e:
                    with pe.Fori(0, MORE) as t:
                        n = e * MORE + t
                        pe.wait_ge(o_xg, n * 16 + 16)
                        for k in range(KC):
                            ins = pe.transpose(BX[k // 4][:, k % 4 * P:(k % 4 + 1) * P], xg[0][:, k * P:(k + 1) * P], ident)
                        ins.then_inc(o_x, 1)
                        pe.wait_ge(o_w, e * 48 + 48)
                        pe.wait_ge(o_xc, n * 2 + 2)
                        for j in range(2):
                            for k in range(KC):
                                ins = pe.matmul((BG, BU)[j][:, :], xgT[:, k, :], wslot[j][:, k * DE:(k + 1) * DE],
                                                start=k == 0, stop=k == KC - 1)
                        ins.then_inc(o_gu, 1)
                        pe.wait_ge(o_he, n + 1)
                        for k in range(DE // P):
                            ins = pe.transpose(BH[:, k * P:(k + 1) * P], he[:, k * P:(k + 1) * P], ident)
                        ins.then_inc(o_ht, 1)
                        pe.wait_ge(o_hc, n + 1)
                        for half in range(2):
                            for k in range(DE // P):
                                c = k * D + half * 512
                                ins = pe.matmul(BY[half][:, :], heT[:, k, :], wslot[2][:, c:c + 512], start=k == 0, stop=k == DE // P - 1)
                        ins.then_inc(o_p, 1)

        @block.scalar
        def _(sc):
            def copy4(name, dst, n):
                filled(sc, name)
                return sc.activation(dst, ps(name)[:, :].rearrange("p (k t) -> p k t", k=4)[:, :, 0:n], ACT.Copy)

            sc.wait_ge(cleared, 2)
            for i in range(TILES):
                n = ROWS[i]
                sc.wait_ge(ld_x[i], 16)
                if i:
                    sc.wait_ge(act_sq, i)
                sc.activation(view(pflat, 0, D)[0:n, :], xh[0:n, i, :], ACT.Square, accum_out=st[0:n, i:i + 1]).then_inc(act_sq, 1)
            sc.wait_ge(ms_ready, 1)
            sc.activation(st[:, 16:21], st[:, 8:13], ACT.Sqrt).then_inc(rt_ready, 1)

            for c in range(4):
                for i in range(TILES):
                    n = ROWS[i]
                    if c == 0:
                        read(copy4(("xT", i, 0), xnT[:, 0:4, i * P:i * P + n], n), ("xT", i, 0))
                    if (c * TILES + i) % 2 == 0:
                        filled(sc, ("in", c, i))
                        read(sc.activation(proj[0:n, i, c * WC:(c + 1) * WC], ps(("in", c, i))[0:n, 0:WC], ACT.Copy), ("in", c, i))
                if c == 2:
                    for i in range(TILES):
                        for c in range(3):
                            taken(sc, ("in", c, i))
                    sc.activation(qsq, proj[:, :, 0:512], ACT.Square).then_inc(heads_sq, 1)
                    sc.activation(ksq[:, :, 0:P], proj[:, :, CSLC:CSLC + P], ACT.Square).then_inc(heads_sq, 1)
                    sc.activation(ksq[:, :, P:2 * P], proj[:, :, CWIN:CWIN + P], ACT.Square).then_inc(heads_sq, 1)
                    sc.wait_ge(heads_ms, 1)
                    sc.activation(nrm[:, :, :], nrm[:, :, :], ACT.Sqrt).then_inc(heads_rt, 1)
                    sc.activation(gate[:, :, :], proj[:, :, CGATE:CGATE + 24], ACT.Exp, scale=-1.0).then_inc(g_exp, 1)

            for g in range(4):
                if g:
                    filled(sc, ("mix_p", g - 1))
                filled(sc, ("pool_p", g))
                read(sc.activation(dT[:, 0:SEQ], ps(("pool_p", g))[:, :], ACT.Copy), ("pool_p", g))
                filled(sc, ("mix_p", g))
                read(sc.activation(amT[:, 4 + g, 0:SEQ], ps(("mix_p", g))[:, :], ACT.Copy, scale=cols[:, 1 + g:2 + g]), ("mix_p", g))

            for i in range(TILES):
                n = ROWS[i]
                dst = qT[:, :, i * P:(i + 1) * P] if i < 4 else qTs[:, :, :]
                read(copy4(("qT", i), dst, n), ("qT", i))

            units = prompt_units()

            def p_exp(u):
                b, i, h = units[u]
                n = (i + 1) * P
                d = 40 + 8 * (i % 2) + place(h)
                taken(sc, ("p_s", u))
                if h == 0 and 4 * b + i >= 2:
                    sc.wait_ge(p_a, 4 * b + i - 1)
                z = pS[u % 3][:, 0:n]
                sc.activation(z, z, ACT.Exp, bias=st[:, 32 + u % 4:33 + u % 4], scale=-1.0, accum_out=st[:, d:d + 1]).then_inc(p_e, 1)

            p_exp(0)
            for u in range(len(units)):
                if u + 1 < len(units):
                    p_exp(u + 1)
                if u % 2 == 0:
                    n = (units[u][1] + 1) * P
                    filled(sc, ("p_T", u))
                    read(sc.activation(pT[u % 2][:, 0:n], ps(("p_T", u))[:, 0:n], ACT.Copy), ("p_T", u))
                if u == AT_NORM:
                    sc.wait_ge(kc_ms, 1)
                    sc.activation(ktmp, ktmp, ACT.Sqrt).then_inc(kc_rt, 1)
                if u == AT_LOGITS:
                    sc.wait_ge(cz, 1)
                    sc.activation(ec, zc, ACT.Exp).then_inc(ce, 1)
                    sc.wait_ge(pcz_ready, 1)
                    sc.activation(pcm, pcz, ACT.Exp).then_inc(pce, 1)
                if u == AT_VALUES:
                    filled(sc, "vcT")
                    sc.activation(VC[:, 0:2, :], ps("vcT")[:, 0:2 * P].rearrange("p (a b) -> p a b", a=2), ACT.Copy)
                    read(sc.activation(VC[0:NBP, 2, :], ps("vcT")[0:NBP, 2 * P:3 * P], ACT.Copy), "vcT")

            for t in range(PAIRS + 1):
                if t < PAIRS:
                    for c in range(4):
                        kb_free(sc, t, 2 * c)
                        filled(sc, ("slc_k", t, c, 0))
                        read(sc.activation(kb[(10 * t + 2 * c) % 4], ps(("slc_k", t, c, 0))[:, :], ACT.Copy), ("slc_k", t, c, 0))
                    kb_free(sc, t, 8)
                    filled(sc, ("win_k", t, 0))
                    read(sc.activation(kb[(10 * t + 8) % 4], ps(("win_k", t, 0))[:, :], ACT.Copy), ("win_k", t, 0))
                    d = 72 + 2 * (t % 2)
                    sc.wait_ge(s_z, t + 1)
                    sc.activation(S[t % 2], S[t % 2], ACT.Exp, bias=st[:, 80:81], scale=-1.0, accum_out=st[:, d:d + 1]).then_inc(s_e, 1)
                    sc.wait_ge(w_z, t + 1)
                    sc.activation(SN[t % 2], SN[t % 2], ACT.Exp, bias=st[:, 81:82], scale=-1.0, accum_out=st[:, d + 1:d + 2]).then_inc(w_e, 1)
                if t == 0:
                    for i in range(4):
                        if i >= 2:
                            filled(sc, ("pc_o", i - 2))
                        filled(sc, ("pc_T", i))
                        read(sc.activation(pcT[0:64, i % 2, :], ps(("pc_T", i))[0:64, 0:P], ACT.Copy), ("pc_T", i))
                    filled(sc, "cmp_T")
                    read(sc.activation(cT, ps("cmp_T")[:, :].rearrange("p (a b) -> p a b", b=P), ACT.Copy), "cmp_T")
                    filled(sc, "cmp_o")
                    read(sc.activation(co, ps("cmp_o")[:, :], ACT.Copy), "cmp_o")
                if t:
                    p = t - 1
                    if p:
                        filled(sc, ("slc_o", p - 1))
                        filled(sc, ("win_o", p - 1))
                    for c in (0, 2):
                        filled(sc, ("slc_T", p, c))
                        read(sc.activation(PT[:, c, :], ps(("slc_T", p, c))[:, :], ACT.Copy), ("slc_T", p, c))
                    filled(sc, ("slc_T", p, 4))
                    read(sc.activation(PT[0:NS, 4, 0:P], ps(("slc_T", p, 4))[0:NS, 0:P], ACT.Copy), ("slc_T", p, 4))
                    filled(sc, ("win_T", p, 1))
                    read(sc.activation(PTw[0:NS, 1, 0:P], ps(("win_T", p, 1))[0:NS, 0:P], ACT.Copy), ("win_T", p, 1))
                    if p:
                        sc.wait_ge(a_ready, p)
                    filled(sc, ("bcast", p))
                    read(sc.activation(bcs, ps(("bcast", p))[:, 0:3 * P], ACT.Copy), ("bcast", p))

            for i in (0, 2):
                read(copy4(("aT", i), amT[:, 0:4, i * P:(i + 1) * P], P), ("aT", i))
            for i in range(TILES):
                n = ROWS[i]
                sc.wait_ge(h_ready, i + 1)
                if i:
                    sc.wait_ge(h_sq, i)
                sc.activation(view(pflat, 0, D)[0:n, :], xh[0:n, i, :], ACT.Square, accum_out=st[0:n, 8 + i:9 + i]).then_inc(h_sq, 1)
                sc.wait_ge(h_ms, i + 1)
                sc.activation(st[0:n, 16 + i:17 + i], st[0:n, 24 + i:25 + i], ACT.Sqrt).then_inc(h_rt, 1)
                sc.wait_ge(n_ready, i + 1)
                sc.dma_start(scratch["n2"][i * P:i * P + n, :], n2[i % 2][0:n, :]).then_inc(n_stored[i % 2], 16)
                if i:
                    filled(sc, ("logit", i - 1))
                read(copy4(("nT", i, 0), n2T[:, 0:4, 0:n], n), ("nT", i, 0))
            sc.wait_ge(r_exp_in, 1)
            sc.activation(r4[1], r4[0], ACT.Exp)
            sc.activation(r1[7], r1[6], ACT.Exp).then_inc(r_exp, 1)

            BX, BG, BY = bank[2], bank[0], (bank[5], bank[6])

            def gathered(n):
                sc.wait_ge(xt_full, n)
                sc.activation(xgT[:, 0:4, :], BX[:, :].rearrange("p (k t) -> p k t", k=4), ACT.Copy).then_inc(xgt_ready, 1)

            def expert(it, s, last_one):
                e = it * 2 + s
                sc.wait_ge(product, e * 3 + 1)
                sc.wait_ge(he_ready, e)
                sc.activation(sg, BG[:, :], ACT.Silu).then_inc(sg_ready, 1)
                if not last_one:
                    gathered(e + 2)
                sc.wait_ge(product, e * 3 + 3)
                sc.wait_ge(st_y, e * 16)
                for half in range(2):
                    sc.activation(ytok[:, half * 512:(half + 1) * 512], BY[half][:, :], ACT.Copy).then_inc(y_taken, 1)
                sc.wait_ge(y_taken, e * 2 + 2)
                sc.dma_start(scratch["y"].rearrange("(r e) d -> r e d", e=NE)[0:P, bass.ds(e, 1), :], ytok.rearrange("p (a d) -> p a d", a=1)).then_inc(st_y, 16)

            gathered(1)
            with sc.Fori(0, NE // 2 - 1) as it:
                for s in range(2):
                    expert(it, s, False)
            for s in range(2):
                expert(NE // 2 - 1, s, s == 1)

            with sc.If(crowded(sc)):
                with sc.Fori(0, NE) as e:
                    with sc.Fori(0, MORE) as t:
                        n = e * MORE + t
                        sc.wait_ge(o_x, n + 1)
                        sc.activation(xgT[:, 0:4, :], BX[:, :].rearrange("p (k t) -> p k t", k=4), ACT.Copy).then_inc(o_xc, 1)
                        sc.wait_ge(o_gu, n + 1)
                        sc.activation(sg, BG[:, :], ACT.Silu).then_inc(o_sg, 1)
                        sc.wait_ge(o_p, n + 1)
                        sc.wait_ge(st_y, 16 * NE)
                        sc.wait_ge(o_st, n * 16)
                        for half in range(2):
                            sc.activation(ytok[:, half * 512:(half + 1) * 512], BY[half][:, :], ACT.Copy).then_inc(o_y, 1)
                        sc.wait_ge(o_y, n * 2 + 2)
                        dst = scratch["more_y"].rearrange("(r e) d -> r e d", e=NE)[bass.ds(t * P, P), bass.ds(e, 1), :]
                        sc.dma_start(dst, ytok.rearrange("p (a d) -> p a d", a=1)).then_inc(o_st, 16)

        @block.vector
        def _(ve):
            steps = [0]

            def link(ins):
                steps[0] += 1
                ins.then_inc(dve, 1)
                ve.wait_ge(dve, steps[0])

            def bc(ap, n):
                return spread(ap.rearrange("p (a b) -> p a b", b=1), 2, n)

            ve.wait_ge(act_sq, TILES)
            ve.tensor_scalar(st[:, 8:13], st[:, 0:5], 1.0 / D, EPS, ALU.mult, ALU.add).then_inc(ms_ready, 1)
            ve.wait_ge(rt_ready, 1)
            link(ve.reciprocal(rstd[:, 0, :], st[:, 16:21]))
            ve.wait_ge(ld_c1, 32)
            for c in range(4):
                for i in range(TILES):
                    n = ROWS[i]
                    if c == 0:
                        if i >= 2:
                            filled(ve, ("xT", i - 2, 1))
                        ve.scalar_tensor_tensor(xn[i % 2][0:n, :], xh[0:n, i, :], rstd[0:n, 0, i:i + 1], g1b[0:n, :],
                                                ALU.mult, ALU.mult).then_inc(xn_ready, 1)
                        filled(ve, ("xT", i, 1))
                        src = ps(("xT", i, 1))[:, :].rearrange("p (k t) -> p k t", k=4)[:, :, 0:n]
                        read(ve.tensor_copy(xnT[:, 4:8, i * P:i * P + n], src), ("xT", i, 1))
                    if (c * TILES + i) % 2 == 1:
                        filled(ve, ("in", c, i))
                        read(ve.tensor_copy(proj[0:n, i, c * WC:(c + 1) * WC], ps(("in", c, i))[0:n, 0:WC]), ("in", c, i))
                if c == 2:
                    ve.wait_ge(ld_c1, N_C1)
                    link(ve.tensor_scalar(gains[:, 0, :], gains[:, 0, :], HD ** -0.5, None, ALU.mult))
                    ve.wait_ge(heads_sq, 3)
                    ve.tensor_reduce(nrm[:, :, 0:8], qsq.rearrange("p t (h d) -> p t h d", d=HD), X, ALU.add)
                    link(ve.tensor_reduce(nrm[:, :, 8:12], ksq.rearrange("p t (h d) -> p t h d", d=HD), X, ALU.add))
                    ve.tensor_scalar(nrm[:, :, :], nrm[:, :, :], 1.0 / HD, EPS, ALU.mult, ALU.add).then_inc(heads_ms, 1)
                    ve.wait_ge(heads_rt, 1)
                    ve.reciprocal(nrm[:, :, :], nrm[:, :, :]).then_inc(heads_rt, 1)
                    ve.wait_ge(heads_rt, 2)
                    inv = spread(table["inv_slope"].rearrange("p (a h) -> p a h", a=1), 1, 4)
                    link(ve.tensor_tensor(nrm[:, 0:4, 0:8], nrm[:, 0:4, 0:8], inv, ALU.mult))
                    for i in range(TILES):
                        qh = proj[:, i, 0:512].rearrange("p (h d) -> p h d", d=HD)
                        link(ve.tensor_tensor(qh, qh, bc(nrm[:, i, 0:8], HD), ALU.mult))
                    gq = spread(spread(gains[:, 0, :].rearrange("p (a b d) -> p a b d", a=1, b=1), 1, KVH), 2, G)
                    for i in range(TILES):
                        qh = proj[:, i, 0:512].rearrange("p (h d) -> p h d", d=HD).rearrange("p (k j) d -> p k j d", j=G)
                        o = qn[:, i, :].rearrange("p (j k d) -> p k j d", k=KVH, j=G)
                        last = ve.tensor_tensor(o, qh, gq, ALU.mult)
                    last.then_inc(q_ready, 1)
                    ve.wait_ge(g_exp, 1)
                    link(ve.tensor_scalar(gate[:, :, :], gate[:, :, :], 1.0, None, ALU.add))
                    ve.reciprocal(gate[:, :, :], gate[:, :, :]).then_inc(g_ready, 1)

            for g in range(4):
                if g:
                    filled(ve, ("mix_s", g - 1))
                filled(ve, ("pool_s", g))
                read(ve.tensor_copy(dT[:, SEQ:NT], ps(("pool_s", g))[:, 0:NS]), ("pool_s", g))
                filled(ve, ("mix_s", g))
                read(ve.tensor_scalar(amT[:, 4 + g, SEQ:NT], ps(("mix_s", g))[:, 0:NS], cols[:, 1 + g:2 + g], None, ALU.mult),
                     ("mix_s", g))

            def raw(r, dst, col):
                half = r % 2
                filled(ve, ("cmp", r))
                n = (P, 136)[half]
                if half == 0:
                    link(ve.tensor_copy(posc[:, col:col + 1], ps(("cmp", r))[:, P:P + 1]))
                read(ve.tensor_scalar(dst[:, half * P:half * P + n], ps(("cmp", r))[:, 0:n], posc[:, col:col + 1], None, ALU.add),
                     ("cmp", r))

            for i in range(TILES):
                n = ROWS[i]
                filled(ve, ("kT", i))
                ve.tensor_copy(kTs[:, i * P:i * P + n], ps(("kT", i))[:, 0:n])
                read(ve.tensor_copy(kTw[:, i * P:i * P + n], ps(("kT", i))[:, P:P + n]), ("kT", i))
            filled(ve, "gate_rows")
            tmp24 = st[:, 0:96].rearrange("p (t c) -> p t c", c=24)
            hm = spread(table["head"].rearrange("p (a c) -> p a c", a=1), 1, PAIRS)
            ve.wait_ge(dve, steps[0])
            read(ve.tensor_tensor(tmp24, ps("gate_rows")[:, 0:96].rearrange("p (t c) -> p t c", c=24), hm, ALU.mult), "gate_rows")
            taken(ve, "gate_rows")
            link(ve.tensor_reduce(grow[:, :, :], tmp24.rearrange("p t (h b) -> p t b h", b=3), X, ALU.add))
            def gates_of(i, b):
                return gate[:, i, :].rearrange("p (k j b) -> p j k b", k=KVH, j=G)[:, :, :, b]

            def heads(ap):
                return ap.rearrange("p (j k d) -> p j k d", j=G, k=KVH)

            def bc3(ap):
                return spread(ap.rearrange("p j (k a) -> p j k a", a=1), 3, HD)

            def turned(src, dst, signal):
                s3 = src.rearrange("p (n h) -> p n h", h=2)
                d3 = dst.rearrange("p (n r) -> p n r", r=2)
                for h in range(2):
                    for par in range(2):
                        ve.tensor_copy(d3[64 * h:64 * h + 64, :, par], s3[64 * par:64 * par + 64, :, h]).then_inc(signal, 1)

            pz = pcz.rearrange("p i (h n) -> p (i h) n", n=NBP)
            pflt = pcz.rearrange("p i c -> p (i c)")
            pmax, psum = st[:, 56:88], st[:, 56:88]

            def beside(u):
                if u == AT_NORM:
                    filled(ve, "key_norm")
                    read(ve.tensor_scalar(ktmp, ps("key_norm")[:, 0:264], 1.0 / HD, EPS, ALU.mult, ALU.add), "key_norm")
                    taken(ve, "key_norm")
                    ve.sem_inc(kc_ms, 1)
                if u == AT_KEYS:
                    ve.wait_ge(kc_rt, 1)
                    link(ve.reciprocal(ktmp, ktmp))
                    link(ve.scalar_tensor_tensor(kcr, kcr, cols[:, 0:1], ktmp, ALU.mult, ALU.mult))
                    ve.memset(kpb[:, :], 0.0)
                    turned(kcr, KCT[:, :], kct_ready)
                    ve.wait_ge(kct_ready, 4)
                    for h in range(KVH):
                        ve.tensor_copy(kpb[64 * h:64 * h + 64, h * NBP:(h + 1) * NBP], KCT[64 * h:64 * h + 64, DB * NBS:NBALL])\
                            .then_inc(kct_ready, 1)
                if u == AT_LOGITS:
                    filled(ve, "cmp_s")
                    bcb = spread(table["bias_c"].rearrange("p (a n) -> p a n", a=1), 1, PAIRS)
                    read(ve.tensor_tensor(zc, ps("cmp_s")[:, 0:P].rearrange("p (t n) -> p t n", n=NBS), bcb, ALU.add), "cmp_s")
                    taken(ve, "cmp_s")
                    link(ve.tensor_reduce(st[:, 0:4], zc, X, ALU.max))
                    ve.tensor_tensor(zc, zc, bc(st[:, 0:4], NBS), ALU.subtract).then_inc(cz, 1)
                    filled(ve, "pc_s")
                    read(ve.tensor_tensor(pflt, ps("pc_s")[:, 0:4 * H * NBP], table["pc_bias"], ALU.add), "pc_s")
                    taken(ve, "pc_s")
                    link(ve.tensor_reduce(pmax, pz, X, ALU.max))
                    link(ve.tensor_tensor(pz, pz, bc(pmax, NBP), ALU.subtract))
                    slopes = spread(spread(table["slope"].rearrange("p (a h b) -> p a h b", a=1, b=1), 1, 4), 3, NBP)
                    pz4 = pcz.rearrange("p i (h n) -> p i h n", n=NBP)
                    ve.tensor_tensor(pz4, pz4, slopes, ALU.mult).then_inc(pcz_ready, 1)
                if u == AT_PROBS:
                    ve.wait_ge(ce, 1)
                    link(ve.scalar_tensor_tensor(zc, ec, TINY, ec, ALU.is_ge, ALU.mult))
                    link(ve.tensor_reduce(st[:, 4:8], zc, X, ALU.add))
                    link(ve.reciprocal(st[:, 8:12], st[:, 4:8]))
                    link(ve.tensor_tensor(ec, zc, bc(st[:, 8:12], NBS), ALU.mult))
                    ve.scalar_tensor_tensor(zc, ec, TINY, ec, ALU.is_ge, ALU.mult).then_inc(cp, 1)
                    ve.wait_ge(pce, 1)
                    link(ve.scalar_tensor_tensor(pflt, table["pc_bias"], NEG / 10, pcm.rearrange("p i c -> p (i c)"), ALU.is_gt, ALU.mult))
                    link(ve.tensor_reduce(psum, pz, X, ALU.add))
                    link(ve.scalar_tensor_tensor(psum, psum, 0.0, psum, ALU.is_equal, ALU.add))
                    link(ve.reciprocal(psum, psum))
                    ve.tensor_tensor(pz, pz, bc(psum, NBP), ALU.mult).then_inc(pcp, 1)
                if u == AT_SUM:
                    filled(ve, "cmp_sum")
                    ve.wait_ge(z_clear, 1)
                    read(ve.tensor_copy(score[:, :, 1:NBS], ps("cmp_sum")[:, 0:P].rearrange("p (t n) -> p t n", n=NBS)[:, :, 1:NBS]), "cmp_sum")
                    taken(ve, "cmp_sum")
                if AT_MASK <= u < AT_MASK + PAIRS:
                    t = u - AT_MASK
                    for k in range(2):
                        link(ve.max(st[:, 64:72], score[:, t, :]))
                        link(ve.match_replace(score[:, t, :], st[:, 64:72], score[:, t, :], -2.0))
                    if t == PAIRS - 1:
                        link(ve.tensor_scalar(maskb[:, :, :], score, -1.5, NEG, ALU.is_gt, ALU.mult))

            units = prompt_units()
            ve.wait_ge(g_ready, 1)
            ve.wait_ge(ld_dist, 16)

            def logits_of(u):
                b, i, h = units[u]
                n = (i + 1) * P
                if u >= 3:
                    filled(ve, ("p_T", u - 3))
                filled(ve, ("p_s", u))
                read(ve.tensor_tensor_reduce(pS[u % 3][:, 0:n], ps(("p_s", u))[:, 0:n], dist[:, SEQ - n:SEQ], -SLOPES[h], 3e38, ALU.add,
                                             ALU.min, st[:, 32 + u % 4:33 + u % 4]), ("p_s", u))

            def add_heads(b, i):
                d = 40 + 8 * (i % 2)
                filled(ve, ("p_o", b, i))
                link(ve.reciprocal(st[:, d:d + 8], st[:, d:d + 8]))
                w = st[:, d:d + 8].rearrange("p (j k) -> p j k", k=KVH)
                link(ve.tensor_tensor(w, w, gates_of(i, b + 1), ALU.mult))
                o = a_tok[:, i, :] if b == 0 else tmpo
                read(ve.tensor_tensor(heads(o), heads(ps(("p_o", b, i))[:, :]), bc3(w), ALU.mult), ("p_o", b, i))
                taken(ve, ("p_o", b, i))
                if b == 0:
                    ve.sem_inc(p_a, 1)
                    return
                ve.tensor_tensor(a_tok[:, i, :], a_tok[:, i, :], tmpo, ALU.add).then_inc(p_a, 1)
                ve.wait_ge(p_a, 4 * b + i + 1)

            logits_of(0)
            for u in range(len(units) + 1):
                if u + 1 < len(units):
                    logits_of(u + 1)
                if u < len(units) and u % 2:
                    n = (units[u][1] + 1) * P
                    filled(ve, ("p_T", u))
                    read(ve.tensor_copy(pT[u % 2][:, 0:n], ps(("p_T", u))[:, 0:n]), ("p_T", u))
                if u and units[u - 1][2] == H - 1:
                    add_heads(units[u - 1][0], units[u - 1][1])
                for r, (first, count) in enumerate(CMP_UNITS):
                    if u == first + count:
                        raw(r, (kcr, kcr, vcr, vcr)[r], r // 2)
                        taken(ve, ("cmp", r))
                        if r == 1:
                            ve.tensor_tensor(ktmp, kcr, kcr, ALU.mult).then_inc(kc_sq, 1)
                        if r == 3:
                            turned(vcr, vct, vct_ready)
                beside(u)

            ve.wait_ge(z_clear, 3)
            ve.wait_ge(cp, 1)
            for s in range(2):
                for tp in range(2):
                    c0 = (2 * tp + s) * NBS
                    last = ve.tensor_copy(pw[64 * s:64 * s + 64, tp::2, c0:c0 + NBS], zc[64 * s:64 * s + 64, tp::2, :])
            last.then_inc(cp, 1)
            ve.wait_ge(ld_c3, 16)
            for t in range(PAIRS + 1):
                if t < PAIRS:
                    Sb, Wb = S[t % 2], SN[t % 2]
                    if t >= 2:
                        filled(ve, ("slc_T", t - 2, 4))
                        filled(ve, ("win_T", t - 2, 1))

                    def chunk(c):
                        name = ("slc_s", t, c)
                        filled(ve, name)
                        z = Sb[:, c * 512:(c + 1) * 512]
                        read(ve.tensor_tensor(z, ps(name)[:, :], slc_bias[:, c * 512:(c + 1) * 512], ALU.add), name)
                        taken(ve, name)
                        z3 = z.rearrange("p (n l) -> p n l", l=64)
                        ve.tensor_tensor_reduce(z3, z3, bc(maskb[:, t, 8 * c:8 * c + 8], 64), -1.0, 3e38, ALU.add, ALU.min,
                                                st[:, 84 + c:85 + c])

                    for c in range(5):
                        if c < 4:
                            kb_free(ve, t, 2 * c + 1)
                            filled(ve, ("slc_k", t, c, 1))
                            read(ve.tensor_copy(kb[(10 * t + 2 * c + 1) % 4], ps(("slc_k", t, c, 1))[:, :]), ("slc_k", t, c, 1))
                        if c:
                            chunk(c - 1)
                    nb = table["new_bias"][:, t * NS:(t + 1) * NS]
                    filled(ve, ("new_s", t))
                    read(ve.tensor_tensor_reduce(Sb[:, PAST:SW], ps(("new_s", t))[:, 0:NS], nb, -1.0, 3e38, ALU.add, ALU.min,
                                                 st[:, 88:89]), ("new_s", t))
                    taken(ve, ("new_s", t))
                    if t:
                        ve.wait_ge(s_e, t)
                        ve.wait_ge(w_e, t)
                    ve.tensor_reduce(st[:, 80:81], st[:, 84:89], X, ALU.min).then_inc(s_z, 1)
                    kb_free(ve, t, 9)
                    filled(ve, ("win_k", t, 1))
                    read(ve.tensor_copy(kb[(10 * t + 9) % 4], ps(("win_k", t, 1))[:, :]), ("win_k", t, 1))
                    filled(ve, ("win_s", t))
                    read(ve.tensor_tensor_reduce(Wb[:, 0:512], ps(("win_s", t))[:, :], table["win_bias"], -1.0, 3e38, ALU.add,
                                                 ALU.min, st[:, 90:91]), ("win_s", t))
                    filled(ve, ("neww_s", t))
                    read(ve.tensor_tensor_reduce(Wb[:, 512:WW], ps(("neww_s", t))[:, 0:NS], nb, -1.0, 3e38, ALU.add, ALU.min,
                                                 st[:, 91:92]), ("neww_s", t))
                    taken(ve, ("neww_s", t))
                    ve.tensor_reduce(st[:, 81:82], st[:, 90:92], X, ALU.min).then_inc(w_z, 1)
                if t == 0:
                    for i in range(4):
                        filled(ve, ("pc_o", i))
                        read(ve.tensor_tensor(heads(tmpc), heads(ps(("pc_o", i))[:, :]), bc3(gates_of(i, 0)), ALU.mult), ("pc_o", i))
                        taken(ve, ("pc_o", i))
                        ve.tensor_tensor(a_tok[:, i, :], a_tok[:, i, :], tmpc, ALU.add).then_inc(p_a, 1)
                        ve.wait_ge(p_a, 8 + i + 1)
                if t:
                    p = t - 1
                    if p:
                        filled(ve, ("slc_o", p - 1))
                        filled(ve, ("win_o", p - 1))
                    for c in (1, 3):
                        filled(ve, ("slc_T", p, c))
                        read(ve.tensor_copy(PT[:, c, :], ps(("slc_T", p, c))[:, :]), ("slc_T", p, c))
                    filled(ve, ("win_T", p, 0))
                    read(ve.tensor_copy(PTw[:, 0, :], ps(("win_T", p, 0))[:, :]), ("win_T", p, 0))
                    d = 72 + 2 * (p % 2)
                    ve.wait_ge(w_e, p + 1)
                    link(ve.reciprocal(st[:, d:d + 2], st[:, d:d + 2]))
                    if p:
                        filled(ve, ("bcast", p - 1))
                    ve.tensor_scalar(diag[:, 0:P], ident, grow[:, p, 0:1], None, ALU.mult)
                    ve.tensor_scalar(diag[:, P:2 * P], ident, grow[:, p, 1:2], st[:, d:d + 1], ALU.mult, ALU.mult)
                    ve.tensor_scalar(diag[:, 2 * P:3 * P], ident, grow[:, p, 2:3], st[:, d + 1:d + 2], ALU.mult, ALU.mult)\
                        .then_inc(diag_ready, 1)
                    taken(ve, ("bcast", p))
                    taken(ve, "cmp_o")
                    ve.tensor_tensor(t1, co[:, p * P:(p + 1) * P], bcs[:, 0:P], ALU.mult)
                    filled(ve, ("slc_o", p))
                    read(ve.tensor_tensor(t2, ps(("slc_o", p))[:, 0:P], bcs[:, P:2 * P], ALU.mult), ("slc_o", p))
                    taken(ve, ("slc_o", p))
                    link(ve.tensor_tensor(t1, t1, t2, ALU.add))
                    filled(ve, ("win_o", p))
                    read(ve.tensor_tensor(t2, ps(("win_o", p))[:, 0:P], bcs[:, 2 * P:3 * P], ALU.mult), ("win_o", p))
                    taken(ve, ("win_o", p))
                    for h in range(KVH):
                        q = slice(64 * h, 64 * h + 64)
                        o = amT[q, 0:4, SEQ + 16 * p:SEQ + 16 * p + 16].rearrange("p g (s q) -> p s g q", s=2)
                        i0, i1 = (x[q, :].rearrange("p (s k g q) -> p k s g q", s=2, k=2, g=4)[:, h] for x in (t1, t2))
                        last = ve.tensor_tensor(o, i0, i1, ALU.add)
                    last.then_inc(a_ready, 1)
                    ve.wait_ge(a_ready, p + 1)

            for i in (1, 3):
                filled(ve, ("aT", i))
                read(ve.tensor_copy(amT[:, 0:4, i * P:(i + 1) * P], ps(("aT", i))[:, :].rearrange("p (k t) -> p k t", k=4)), ("aT", i))
            ve.wait_ge(ld_xr, 16 * TILES)
            link(ve.memset(logits, 0.0))
            for i in range(TILES):
                n = ROWS[i]
                for half in range(2):
                    filled(ve, ("h", i, half))
                    x = xh[0:n, i, half * 512:(half + 1) * 512]
                    read(ve.tensor_tensor(x, ps(("h", i, half))[0:n, :], x, ALU.add), ("h", i, half))
                taken(ve, ("h", i, 1))
                ve.sem_inc(h_ready, 1)
                ve.wait_ge(h_sq, i + 1)
                ve.tensor_scalar(st[0:n, 24 + i:25 + i], st[0:n, 8 + i:9 + i], 1.0 / D, EPS, ALU.mult, ALU.add).then_inc(h_ms, 1)
                ve.wait_ge(h_rt, i + 1)
                link(ve.reciprocal(rstd[0:n, 1, i:i + 1], st[0:n, 16 + i:17 + i]))
                if i == 0:
                    ve.wait_ge(ld_g2, 16)
                if i >= 2:
                    filled(ve, ("nT", i - 2, 1))
                    ve.wait_ge(n_stored[i % 2], 16 * (i // 2))
                ve.scalar_tensor_tensor(n2[i % 2][0:n, :], xh[0:n, i, :], rstd[0:n, 1, i:i + 1], g2b[0:n, :], ALU.mult, ALU.mult)\
                    .then_inc(n_ready, 1)
                if i:
                    filled(ve, ("logit", i - 1))
                    read(ve.tensor_copy(logits[0:ROWS[i - 1], i - 1, :], ps(("logit", i - 1))[0:ROWS[i - 1], 0:20]), ("logit", i - 1))
                filled(ve, ("nT", i, 1))
                read(ve.tensor_copy(n2T[:, 4:8, 0:n], ps(("nT", i, 1))[:, :].rearrange("p (k t) -> p k t", k=4)[:, :, 0:n]), ("nT", i, 1))
            filled(ve, ("logit", 4))
            read(ve.tensor_copy(logits[0:NS, 4, :], ps(("logit", 4))[0:NS, 0:20]), ("logit", 4))
            taken(ve, ("logit", 4))
            for i in range(4):
                taken(ve, ("logit", i))

            lg, le = logits[:, :, 0:NG], logits[:, :, NG:NG + NE]
            over4 = lambda x: bc(x, NG)
            over16 = lambda x: bc(x, NE)
            wide = lambda name, n: spread(table[name].rearrange("p (a n) -> p a n", a=1), 1, TILES)
            link(ve.tensor_reduce(r1[0], lg, X, ALU.max))
            link(ve.tensor_tensor(r4[0], lg, over4(r1[0]), ALU.subtract))
            link(ve.tensor_tensor(r4[2], lg, over4(r1[0]), ALU.is_equal))
            link(ve.tensor_tensor(r4[2], r4[2], wide("prio4", NG), ALU.mult))
            link(ve.tensor_reduce(r1[3], r4[2], X, ALU.max))
            link(ve.tensor_tensor(r4[3], r4[2], over4(r1[3]), ALU.is_equal))
            link(ve.tensor_scalar(r4[2], r4[3], -NEG, NEG, ALU.mult, ALU.add))
            ge = lambda x: x.rearrange("p t (g e) -> p t g e", g=NG)
            pen = spread(r4[2].rearrange("p t (g a) -> p t g a", a=1), 3, EPG)
            link(ve.tensor_tensor(ge(r16[0]), ge(le), pen, ALU.add))

            def first_max(z, m, oh):
                link(ve.tensor_reduce(m, z, X, ALU.max))
                link(ve.tensor_tensor(oh, z, over16(m), ALU.is_equal))
                link(ve.tensor_tensor(oh, oh, wide("prio", NE), ALU.mult))
                link(ve.tensor_reduce(r1[5], oh, X, ALU.max))
                link(ve.tensor_tensor(oh, oh, over16(r1[5]), ALU.is_equal))

            flat = lambda x: x.rearrange("p a b -> p (a b)")
            first_max(r16[0], r1[4], r16[2])
            link(ve.scalar_tensor_tensor(flat(r16[1]), flat(r16[2]), NEG, flat(r16[0]), ALU.mult, ALU.add))
            first_max(r16[1], r1[6], r16[3])
            hot = view(kTs, 100 + 2 * 80, 2, TILES * NE).rearrange("p k (i e) -> p k i e", e=NE)
            link(ve.memset(chosen[:, TILES, :], 0.0))
            link(ve.tensor_tensor(chosen[:, 0:TILES, :], r16[2], r16[3], ALU.add))
            ve.tensor_tensor(chosen[:, 0:TILES, :], chosen[:, 0:TILES, :], over16(table["valid"]), ALU.mult).then_inc(oh_ready, 1)
            ve.tensor_tensor(r1[6], r1[6], r1[4], ALU.subtract).then_inc(r_exp_in, 1)
            over_k = lambda x: spread(x.rearrange("p (a i) e -> p a i e", a=1), 1, 2)
            link(ve.tensor_tensor(hot, hot, over_k(over16(table["valid"])), ALU.mult))
            for k in range(2):
                ve.tensor_tensor(tok_at[:, k], hot[:, k], over16(table["token"]), ALU.mult)
            link(ve.tensor_tensor(pair16, hot, over_k(wide("expert", NE)), ALU.mult))
            link(ve.tensor_reduce(ex, pair16, X, ALU.add))
            filled(ve, "prefix")
            link(ve.tensor_tensor(pair16, hot, over_k(ps("prefix")[:, 0:TILES * NE].rearrange("p (i e) -> p i e", e=NE)), ALU.mult))
            link(ve.tensor_reduce(pos, pair16, X, ALU.add))
            for i in range(TILES):
                for k in range(2):
                    ve.tensor_scalar(picks[:, 2 * i + k, :], table["row"], pos[:, k, i:i + 1], None, ALU.is_equal).then_inc(picks_ready, 1)
            read(ve.tensor_reduce(r1[5][:, 0:1], ps("prefix")[:, TILES * NE:(TILES + 1) * NE], X, ALU.max), "prefix")
            taken(ve, "prefix")
            link(ve.tensor_copy(nmax[:, :], r1[5][0:1, 0:1]))
            filled(ve, "idx")
            read(ve.tensor_copy(idx[:, :], ps("idx")[:, 0:NE]), "idx")
            taken(ve, "idx")
            ve.sem_inc(idx_ready, 1)
            link(ve.scalar_tensor_tensor(slot_f, pos, float(NE), ex, ALU.mult, ALU.add))
            link(ve.tensor_copy(slot_i[:, :, :], slot_f))
            link(ve.tensor_scalar(row_i[:, 0], slot_f, FIRST - 1.0, None, ALU.min))
            link(ve.tensor_scalar(over_f, slot_f, -float(FIRST), None, ALU.add))
            link(ve.tensor_scalar(row_i[:, 1], over_f, 0.0, None, ALU.max))
            link(ve.tensor_scalar(inside[:, :, :], over_f, 0.0, None, ALU.is_lt))
            ve.sem_inc(slots_ready, 1)
            ve.wait_ge(r_exp, 1)
            link(ve.tensor_reduce(r1[1], r4[1], X, ALU.add))
            link(ve.reciprocal(r1[2], r1[1]))
            link(ve.tensor_scalar(r1[3], r1[7], 1.0, None, ALU.add))
            link(ve.reciprocal(r1[5], r1[3]))
            link(ve.tensor_tensor(gates2[:, 0, :], r1[2], r1[5], ALU.mult))
            link(ve.tensor_tensor(gates2[:, 1, :], gates2[:, 0, :], r1[7], ALU.mult))
            link(ve.tensor_tensor(gates1[:, :, :], gates2[:, :, :], inside[:, :, :], ALU.mult))
            link(ve.tensor_tensor(gates2[:, :, :], gates2[:, :, :], gates1[:, :, :], ALU.subtract))

            BX, BU, BH = bank[3], bank[1], bank[4]

            def gathered(n):
                ve.wait_ge(xt_full, n)
                ve.tensor_copy(xgT[:, 4:8, :], BX[:, :].rearrange("p (k t) -> p k t", k=4)).then_inc(xgt_ready, 1)

            def expert(it, s, last_one):
                e = it * 2 + s
                ve.wait_ge(product, e * 3 + 2)
                ve.wait_ge(sg_ready, e + 1)
                ve.wait_ge(ht_full, e)
                ve.tensor_tensor(he, sg, BU[:, :], ALU.mult).then_inc(he_ready, 1)
                if not last_one:
                    gathered(e + 2)
                ve.wait_ge(ht_full, e + 1)
                ve.wait_ge(product, e * 3)
                ve.tensor_copy(heT, BH[:, :].rearrange("p (k t) -> p k t", k=4)).then_inc(ht_taken, 1)

            gathered(1)
            with ve.Fori(0, NE // 2 - 1) as it:
                for s in range(2):
                    expert(it, s, False)
            for s in range(2):
                expert(NE // 2 - 1, s, s == 1)

            with ve.If(crowded(ve)):
                with ve.Fori(0, NE) as e:
                    with ve.Fori(0, MORE) as t:
                        n = e * MORE + t
                        ve.wait_ge(o_x, n + 1)
                        ve.tensor_copy(xgT[:, 4:8, :], BX[:, :].rearrange("p (k t) -> p k t", k=4)).then_inc(o_xc, 1)
                        ve.wait_ge(o_gu, n + 1)
                        ve.wait_ge(o_sg, n + 1)
                        ve.tensor_tensor(he, sg, BU[:, :], ALU.mult).then_inc(o_he, 1)
                        ve.wait_ge(o_ht, n + 1)
                        ve.tensor_copy(heT, BH[:, :].rearrange("p (k t) -> p k t", k=4)).then_inc(o_hc, 1)
                for i in range(TILES):
                    m = ROWS[i]
                    ve.wait_ge(o_yl, 32 * (i + 1))
                    for k in range(2):
                        ve.scalar_tensor_tensor(xh[0:m, i, :], over_yb[k][0:m, :], gates2[0:m, k, i:i + 1], xh[0:m, i, :],
                                                ALU.mult, ALU.add).then_inc(o_add, 1)
                        ve.wait_ge(o_add, 2 * i + k + 1)

            for i in range(TILES):
                n = ROWS[i]
                ve.wait_ge(y_ld[i % 2], 32 * (i // 2 + 1))
                ve.scalar_tensor_tensor(xh[0:n, i, :], yb[i % 2][0][0:n, :], gates1[0:n, 0, i:i + 1], xh[0:n, i, :],
                                        ALU.mult, ALU.add).then_inc(head_out, 1)
                ve.wait_ge(head_out, i + 1)
                ve.scalar_tensor_tensor(xh[0:n, i, :], yb[i % 2][1][0:n, :], gates1[0:n, 1, i:i + 1], xh[0:n, i, :],
                                        ALU.mult, ALU.add).then_inc(y_ready, 1)

        @block.gpsimd
        def _(po):
            counts = {}

            def alone(ins, signal):
                n = counts[id(signal)] = counts.get(id(signal), 0) + 1
                ins.then_inc(signal, 1)
                po.wait_ge(signal, n)

            alone(po.memset(st[:, :], 0.0), cleared)
            alone(po.memset(proj[64:P, 4, :], 0.0), cleared)
            alone(po.memset(idx[:, :], 0), cleared)
            for j in range(5):
                po.dma_start(scratch["tokens"].rearrange("(p c) a -> p (c a)", p=P)[:, 16 * j:16 * j + 16], idx[:, 0:16])\
                    .then_inc(ld_zero, 16)
            po.wait_ge(xn_ready, TILES)
            alone(po.memset(QB[:, :, :], 0.0), qb_clear)
            po.wait_ge(heads_rt, 2)
            po.wait_ge(ld_c1, N_C1)
            for j, c in enumerate((CSLC, CWIN)):
                kk = proj[:, :, c:c + P].rearrange("p t (h d) -> p t h d", d=HD)
                r = spread(nrm[:, :, 8 + 2 * j:10 + 2 * j].rearrange("p t (h a) -> p t h a", a=1), 3, HD)
                for i in range(TILES):
                    alone(po.tensor_tensor(kk[:, i], kk[:, i], r[:, i], ALU.mult), k_step)
                g = spread(gains[:, 1 + j, :].rearrange("p (a d) -> p a d", a=1), 1, KVH)
                for i in range(TILES):
                    alone(po.tensor_tensor(kk[:, i], kk[:, i], g, ALU.mult), k_ready)
            for i in range(TILES):
                filled(po, ("in", 3, i))
            alone(po.memset(wblk[0], 0.0), cleared)
            po.wait_ge(ld_pos, 32)
            alone(po.tensor_copy(cache[0][:, 128:130, :], spread(posr.rearrange("p (a d) -> p a d", a=1), 1, 2)), extra)

            def prompt_pages(which):
                c = CCMP + P * which
                alone(po.tensor_copy(cache[1][:, 128:136, :].rearrange("p (n h) d -> p n (h d)", h=2), proj[:, 0:4, c:c + P]), extra)

            prompt_pages(0)
            filled(po, ("qT", 4))
            alone(po.memset(wblk[1], 0.0), cleared)
            for i in range(TILES):
                taken(po, ("in", 3, i))
                taken(po, ("in", 2, i))

            def store(dst, src):
                po.dma_start(dst, src).then_inc(st_out, 16)

            kvp = lambda name: out[name].rearrange("b (i p) c h d -> p (b i) (c h d)", p=P)
            kvs = lambda name: out[name].rearrange("b q c h d -> (b q) (c h d)")
            store(kvp("new_cmp_kv_prompt"), proj[:, 0:4, CCMP:CCMP + 256])
            store(kvs("new_cmp_kv_sample"), proj[0:NS, 4, CCMP:CCMP + 256])
            store(out["new_pool_prompt"][0], proj[P - 15:P, 3, CU:CU + 512])
            store(out["new_pool_sample"][:, 0:7, :], a["state_pool"][:, 8:15, :])
            for b in range(DB):
                store(out["new_pool_sample"][b, 7:15, :], proj[8 * b:8 * b + 8, 4, CU:CU + 512])
            po.wait_ge(k_ready, 2 * TILES)
            store(kvp("new_slc_kv_prompt"), proj[:, 0:4, CSLC:CSLC + 256])
            store(kvs("new_slc_kv_sample"), proj[0:NS, 4, CSLC:CSLC + 256])
            store(kvp("new_win_kv_prompt"), proj[:, 0:4, CWIN:CWIN + 256])
            for b in range(DB):
                store(out["new_win_kv_sample"][b, 504:512].rearrange("q c h d -> q (c h d)"), proj[8 * b:8 * b + 8, 4, CWIN:CWIN + 256])

            taken(po, ("qT", 4))
            po.wait_ge(qb_clear, 1)
            for s in range(2):
                for h in range(KVH):
                    for g in range(G):
                        c0 = 64 * s + 32 * h + 8 * g
                        src = qTs[64 * h:64 * h + 64, g, :].rearrange("p (t s q) -> p s t q", s=2, q=DS)[:, s]
                        alone(po.tensor_copy(QB[64 * h:64 * h + 64, s::2, c0:c0 + DS], src), qb_ready)
            filled(po, ("cmp", 1))
            prompt_pages(1)
            filled(po, "gate_rows")
            for name in (("mix_p", 3), ("mix_s", 3)):
                filled(po, name)
            po.wait_ge(kct_ready, 6)
            alone(po.memset(score, 1.0e4), z_clear)
            filled(po, ("p_o", 1, 3))
            po.wait_ge(p_a, 8)
            alone(po.memset(pw, 0.0), z_clear)
            alone(po.memset(Vblk[0:64, :], 0.0), z_clear)
            taken(po, "vcT")
            for h in range(H):
                po.dma_start(Vblk[8 * place(h):8 * place(h) + 8, 64 * place(h):64 * place(h) + 64], VC[0:8, 2, 64 * (h // G):64 * (h // G) + 64]).then_inc(vb, 16)
            for b in range(DB):
                po.wait_ge(ld_win_state[b % 4], 16 * (b // 4 + 1))
                dst = out["new_win_kv_sample"][b].rearrange("q c h d -> q (c h d)")
                po.dma_start(dst[0:120, :], wst[b % 4][8:P, 0, :]).then_inc(st_win[b % 4], 16)
                po.dma_start(dst[120:504, :].rearrange("(n p) c -> p n c", p=P), wst[b % 4][:, 1:4, :]).then_inc(st_win[b % 4], 16)

            po.wait_ge(idx_ready, 1)
            po.wait_ge(n_stored[0], 48)
            po.wait_ge(n_stored[1], 32)
            for e in range(NE):
                if e >= 2:
                    po.wait_ge(xt_full, e - 1)
                po.indirect_dma_start(xg[e % 2], None, scratch["n2"], bass.IndirectOffsetOnAxis(idx[:, e:e + 1], 0))\
                    .then_inc(xg_ld[e % 2], 16)

            with po.If(crowded(po)):
                po.wait_ge(ld_zero, 16 * 5)
                po.wait_ge(ld_c1, N_C1)
                for i in range(TILES):
                    n = ROWS[i]
                    for k in range(2):
                        po.indirect_dma_start(scratch["tokens"], bass.IndirectOffsetOnAxis(slot_i[0:n, k, i:i + 1], 0),
                                              tokid[0:n, i:i + 1], None).then_inc(scattered, 16)
                po.wait_ge(scattered, 16 * 2 * TILES)
                with po.Fori(0, NE) as e:
                    with po.Fori(0, MORE) as t:
                        n = e * MORE + t
                        po.wait_ge(o_x, n)
                        po.wait_ge(o_passed, n)
                        src = scratch["tokens"].rearrange("(r e) a -> r (e a)", e=NE)[bass.ds(t * P + P, P), bass.ds(e, 1)]
                        po.dma_start(over_idx[:, :], src, allow_slow_non_contiguous=True).then_inc(o_idx, 16)
                        po.wait_ge(o_idx, n * 16 + 16)
                        po.tensor_tensor(passed[:, :], over_idx[0:1, :], over_idx[0:1, :], ALU.add).then_inc(o_passed, 1)
                        po.wait_ge(xt_full, NE)
                        po.indirect_dma_start(xg[0], None, scratch["n2"], bass.IndirectOffsetOnAxis(over_idx[:, :], 0))\
                            .then_inc(o_xg, 16)
                po.wait_ge(o_p, NE * MORE)
                po.wait_ge(o_st, 16 * NE * MORE)
                for i in range(TILES):
                    m = ROWS[i]
                    if i:
                        po.wait_ge(o_add, 2 * i)
                    for k in range(2):
                        po.indirect_dma_start(over_yb[k][0:m, :], None, scratch["more_y"],
                                              bass.IndirectOffsetOnAxis(row_i[0:m, 1, k, i:i + 1], 0)).then_inc(o_yl, 16)

            po.wait_ge(st_y, 16 * NE)
            po.wait_ge(product, 3 * NE)
            for i in range(TILES):
                n = ROWS[i]
                if i >= 2:
                    po.wait_ge(y_ready, i - 1)
                for k in range(2):
                    po.indirect_dma_start(yb[i % 2][k][0:n, :], None, scratch["y"], bass.IndirectOffsetOnAxis(row_i[0:n, 0, k, i:i + 1], 0))\
                        .then_inc(y_ld[i % 2], 16)
            for s in st_win:
                po.wait_ge(s, 64)
            po.wait_ge(st_out, 16 * N_OUT)


N_C1 = 16 * (2 + 1 + 3 + 2 + 4 + 2 + 1)
N_OUT = 4 + DB + 3 + DB


def tables():
    f = np.float32
    p, r = np.arange(P), np.arange(P)
    mats = np.zeros((P, 5, P), f)
    mats[:, 0] = np.eye(P)
    mats[:, 1] = 1
    mats[:, 2] = p[:, None] < p[None, :]
    seq, kvh, grp, q = r // 64, r // 32 % 2, r // 8 % 4, r % 8
    mats[:, 3] = (seq[:, None] == seq) & (kvh[:, None] == kvh) & (q[:, None] == q)
    mats[:, 4] = (p[:, None] // 64) == (p // 64)
    slope = np.array(SLOPES, f)[kvh * G + grp]

    small = {}
    n = np.arange(NBS)
    small["bias_c"] = -slope[:, None] * (PAST + q[:, None] - (64 * n + 63))
    tok = np.arange(NS)
    nb = np.zeros((P, PAIRS, NS), f)
    for t in range(PAIRS):
        ok = (tok[None] // 8 == 2 * t + seq[:, None]) & (tok[None] % 8 <= q[:, None])
        nb[:, t] = np.where(ok, -slope[:, None] * (q[:, None] - tok[None] % 8), NEG)
    small["new_bias"] = nb
    c = np.arange(512)
    dist = 512 + q[:, None] - c
    small["win_bias"] = np.where(dist < 512, -slope[:, None] * dist, NEG)
    head = np.zeros((P, H, 3), f)
    head[r, kvh * G + grp] = 1
    small["head"] = head
    pcb = np.zeros((P, 4, H, NBP), f)
    for i in range(4):
        d = (128 * i + p)[:, None] - (64 * np.arange(NBP) + 63)
        for h in range(H):
            pcb[:, i, place(h)] = np.where(d >= 0, -d, NEG)
    small["pc_bias"] = pcb
    small["slope"] = np.broadcast_to([SLOPES[h] for g in range(G) for h in (g, g + G)], (P, H))
    small["inv_slope"] = np.broadcast_to([1.0 / s for s in SLOPES], (P, H))
    small["prio"] = np.broadcast_to(16.0 - np.arange(NE), (P, NE))
    small["prio4"] = np.broadcast_to(4.0 - np.arange(NG), (P, NG))
    small["expert"] = np.broadcast_to(np.arange(NE), (P, NE))
    small["token"] = P * np.arange(TILES)[None] + p[:, None]
    small["row"] = np.broadcast_to(np.arange(P), (P, P))
    small["valid"] = np.array([[1.0 if x < ROWS[i] else 0.0 for i in range(TILES)] for x in range(P)])

    bands = np.zeros((P, 3, 4, P), f)
    bands_s = np.zeros((P, 2, 4, NS), f)
    for g, w in enumerate(WINDOWS):
        d = p[None, :] - p[:, None]
        cnt = np.minimum(w, p + 1)[None, :]
        bands[:, 0, g] = np.where((d >= 0) & (d < w), 1.0 / cnt, 0) - (d == 0)
        bands[:, 1, g] = np.where((d >= 0) & (d < w), 1.0 / w, 0) - (d == 0)
        bands[:, 2, g] = np.where(d + P < w, 1.0 / w, 0)
        ds = tok[None, :] % 8 - tok[:, None] % 8
        same = tok[None, :] // 8 == tok[:, None] // 8
        bands_s[0:NS, 0, g] = np.where(same & (ds >= 0) & (ds < w), 1.0 / w, 0) - (tok[None, :] == tok[:, None])
        row = np.arange(120)
        dd = 15 + tok[None, :] % 8 - row[:, None] % 15
        bands_s[0:120, 1, g] = np.where((row[:, None] // 15 == tok[None, :] // 8) & (dd < w), 1.0 / w, 0)
    sel = np.zeros((NS, PAIRS, P), f)
    for t in range(PAIRS):
        sel[(2 * t + seq) * 8 + q, t, r] = 1
    x = np.arange(SEQ)
    dd = p[:, None] + 384 - x
    return {
        "c_mats": mats,
        "c_small": np.concatenate([np.asarray(small[k], f).reshape(P, w) for k, w in SMALL], 1),
        "c_bands": np.concatenate([bands.reshape(P, -1), bands_s.reshape(P, -1)], 1),
        "c_sel": sel,
        "c_slc_bias": (-slope[:, None] * (PAST + q[:, None] - np.arange(PAST))).astype(f),
        "c_dist": np.where(dd >= 0, -dd, NEG).astype(f),
        "c_tokid": (128 * np.arange(TILES)[None] + p[:, None]).astype(np.int32),
    }


_INS = ["x_prompt", "x_sample", "cache_cmp_kv", "cache_slc_kv", "state_win_kv", "state_pool", "page_table", "norm1_g", "w_in",
        "q_norm_g", "k_norm_cmp_g", "k_norm_slc_g", "k_norm_win_g", "cmp_pos_emb", "w_cmp_k", "w_cmp_v", "pool_w", "pool_scale",
        "w_out", "norm2_g", "w_router_group", "w_router_expert", "w_gate", "w_up", "w_down"]
_OUTS = [("y_prompt", (1, SEQ, D)), ("y_sample", (DB, DS, D)),
         ("new_cmp_kv_prompt", (1, SEQ, 2, KVH, HD)), ("new_cmp_kv_sample", (DB, DS, 2, KVH, HD)),
         ("new_slc_kv_prompt", (1, SEQ, 2, KVH, HD)), ("new_slc_kv_sample", (DB, DS, 2, KVH, HD)),
         ("new_win_kv_prompt", (1, SEQ, 2, KVH, HD)), ("new_win_kv_sample", (DB, 512, 2, KVH, HD)),
         ("new_pool_prompt", (1, 15, 512)), ("new_pool_sample", (DB, 15, 512))]


def kernel(**inputs):
    import concourse.bacc as bacc
    from concourse.bass_utils import run_bass_kernel_spmd

    nc = bacc.Bacc("TRN2", target_bir_lowering=False, num_devices=1, dynamic_dma_scratch_size=8192)
    arrays, ins, outs = {}, {}, {}
    for name, value in [(n, inputs[n]) for n in _INS] + list(tables().items()):
        value = np.ascontiguousarray(value)
        arrays[f"in_{name}"] = value
        ins[name] = nc.dram_tensor(f"in_{name}", value.shape, mybir.dt.from_np(value.dtype), kind="ExternalInput").ap()
    for name, shape in _OUTS:
        outs[name] = nc.dram_tensor(f"out_{name}", shape, F32, kind="ExternalOutput").ap()
    scratch = {"n2": nc.dram_tensor("normed_rows", (NT, D), F32).ap(),
               "tokens": nc.dram_tensor("token_of_slot", (NE * CAP, 1), I32).ap(),
               "y": nc.dram_tensor("expert_rows", (FIRST, D), F32).ap(),
               "more_y": nc.dram_tensor("more_expert_rows", (NE * MORE * P, D), F32).ap()}
    hybrid_step(nc, ins, outs, scratch)
    r = run_bass_kernel_spmd(nc, [arrays], core_ids=[0])
    return tuple(r.results[0][f"out_{name}"] for name, _ in _OUTS)
```

```python
from contextlib import ExitStack

import concourse.bass as bass
import numpy as np
from concourse import mybir

F32 = mybir.dt.float32
I32 = mybir.dt.int32
ACT = mybir.ActivationFunctionType
ALU = mybir.AluOpType
X = mybir.AxisListType.X

P = 128
D = 1024
KC = D // P
SEQ, DB, DS, PAST = 512, 8, 8, 2048
NS = DB * DS
NT = SEQ + NS
TILES = 5
ROWS = [P, P, P, P, NS]
H, HD, KVH, G = 8, 64, 2, 4
PAGES = PAST // P
NPAGES = DB * PAGES
NBS = PAST // 64
NBP = SEQ // 64
COLS = 1816
WC = COLS // 4
CCMP, CSLC, CWIN, CGATE, CU = 512, 768, 1024, 1280, 1304
WINDOWS = (2, 4, 8, 16)
NE, NG, EPG, DE = 16, 4, 4, 512
HALF = DE // 2
CAP = 640
MORE = CAP // P - 1
FIRST = NE * P
EARLY = (NE - 1) * P
EPS = 1e-6
NEG = -1e30
FINAL = (0, 1, 2, 3, 4, 7, 5)
AHEAD = 3
TINY = 1.1754943508222875e-38
PAIRS = 4
SLOTS = 68
NBALL = NPAGES * 2 + NBP
CMP_UNITS = [(0, 8), (9, 8), (34, 8), (44, 8)]
SLOPES = [2.0 ** -(h + 1) for h in range(H)]

SMALL = [("bias_c", NBS), ("new_bias", PAIRS * NS), ("win_bias", 512), ("head", 24), ("pc_bias", 4 * H * NBP), ("slope", H), ("inv_slope", H),
         ("prio", NE), ("prio4", NG), ("expert", NE), ("token", TILES),
         ("row", P), ("tile", TILES), ("valid", TILES)]


def place(h):
    return h % G * KVH + h // G


def spread(ap, axis, n):
    shape = list(ap.shape)
    shape[axis] = n
    return ap.broadcast_to(shape)


def prompt_units():
    return [(b, i, h) for b in range(2) for i in range(4) for h in range(H)]


def compress_steps(u):
    for r, (first, count) in enumerate(CMP_UNITS):
        if first <= u < first + count:
            each = -(-HD // count)
            return [(r, d) for d in range((u - first) * each, min(HD, (u - first + 1) * each))]
    return []


AT_NORM, AT_KEYS, AT_LOGITS, AT_PROBS, AT_SUM, AT_MASK, AT_VALUES, AT_TURNED = \
    19, 20, 22, 23, 24, 25, 57, 59


def psum_plan():
    plan, used, nxt = {}, [0] * 8, [0]

    def add(name, bank=None, pool=8):
        if bank is None:
            bank = nxt[0] % pool
            nxt[0] = bank + 1
        plan[name] = (bank, used[bank])
        used[bank] += 1

    for i in range(TILES + 1):
        if i < TILES:
            for half in range(2):
                add(("xT", i, half))
        if i:
            add(("in", 0, i - 1))
    for c in range(1, 4):
        for i in range(TILES):
            add(("in", c, i))
    for g in range(4):
        for name in ("pool_p", "pool_s", "mix_p", "mix_s"):
            add((name, g))
    for i in range(TILES):
        add(("qT", i))
        add(("kT", i))
    add("gate_rows")
    nxt[0] = 0
    units = prompt_units()
    for u in range(AHEAD):
        add(("p_s", u), pool=5)
    for u in range(len(units) + 1):
        if u + AHEAD < len(units):
            add(("p_s", u + AHEAD), pool=5)
        for r, d in compress_steps(u):
            if d == 0:
                add(("cmp", r), bank=5)
        for at, names in ((AT_NORM, ["key_norm"]), (AT_LOGITS, ["cmp_s", "pc_s"]), (AT_SUM, ["cmp_sum"]), (AT_VALUES, ["vcT"]), (AT_TURNED, ["pc_T"])):
            if u == at:
                for name in names:
                    add(name, bank=5)
        if u < len(units):
            add(("p_T", u), pool=5)
        if u:
            b, i, h = units[u - 1]
            if h == 0:
                add(("p_o", b, i), bank=6 + i % 2)
    nxt[0] = 0
    for t in range(PAIRS + 1):
        if t < PAIRS:
            for c in range(5):
                if c < 4:
                    for s in range(2):
                        add(("slc_k", t, c, s))
                if c:
                    add(("slc_s", t, c - 1))
            add(("new_s", t))
            for s in range(2):
                add(("win_k", t, s))
            add(("win_s", t))
            add(("neww_s", t))
        if t == 1:
            add("cmp_T")
            for i in range(4):
                add(("pc_o", i))
            add("cmp_o")
        if t == PAIRS:
            for i in range(4):
                add(("aT", i))
        if t:
            for c in range(5):
                add(("slc_T", t - 1, c))
            for c in range(2):
                add(("win_T", t - 1, c))
            for name in ("slc_o", "win_o", "bcast"):
                add((name, t - 1))
    for i in range(TILES + 1):
        for half in range(2):
            if i < TILES:
                add(("h", i, half))
            if i and half == 0:
                for other in range(2):
                    add(("nT", i - 1, other))
            if i and half == 1:
                add(("logit", i - 1))
    add("prefix")
    add("idx")
    return plan, used


def hybrid_step(nc, a, out, scratch):
    with ExitStack() as ctx:
        def sb(name, shape, dt=F32):
            return ctx.enter_context(nc.sbuf_tensor(name, shape, dt))

        def sem(name):
            return ctx.enter_context(nc.semaphore(name))

        def sems(name, n):
            return [sem(f"{name}{i}") for i in range(n)]

        bank = [ctx.enter_context(nc.psum_tensor(f"bank{i}", [P, 512], F32)) for i in range(8)]
        EXPERT_BANKS = bank[0], (bank[1], bank[7]), (bank[2], bank[3]), (bank[4], bank[0]), (bank[5], bank[6])
        plan, used = psum_plan()
        full, free = sems("bank_full", 8), sems("bank_free", 8)

        def ps(name):
            return bank[plan[name][0]]

        def opened(pe, name):
            b, n = plan[name]
            if n:
                pe.wait_ge(free[b], n)

        def filled(eng, name):
            b, n = plan[name]
            eng.wait_ge(full[b], n + 1)

        def taken(eng, name):
            b, n = plan[name]
            eng.wait_ge(free[b], n + 1)

        def written(ins, name):
            ins.then_inc(full[plan[name][0]], 1)

        def read(ins, name):
            ins.then_inc(free[plan[name][0]], 1)

        arena = sb("arena", [P, 2 * KC * WC + 2 * SLOTS * P])
        proj = sb("proj", [P, TILES, COLS])
        xh = sb("xh", [P, TILES, D])
        amT = sb("amT", [P, KC, NT])
        qT = sb("qT", [P, G, SEQ + 0])
        qTs = sb("qTs", [P, G, NS])
        QB = sb("QB", [P, DB, P])
        kTs = sb("kTs", [P, NT])
        kTw = sb("kTw", [P, NT])
        KCT = sb("KCT", [P, NBALL])
        VC = sb("VC", [P, 3, P])
        mats = sb("mats", [P, 5, P])
        slc_bias = sb("slc_bias", [P, PAST])
        small = sb("small", [P, sum(w for _, w in SMALL)])
        gains = sb("gains", [P, 3, HD])
        cols = sb("cols", [P, 5])
        gate = sb("gate", [P, TILES, 24])
        grow = sb("grow", [P, PAIRS, 3])
        rstd = sb("rstd", [P, 2, TILES])
        nrm = sb("nrm", [P, TILES, 12])
        maskb = sb("maskb", [P, PAIRS, NBS + 1])
        st = sb("st", [P, 96])
        posc = sb("posc", [P, 2])
        kpb = sb("kpb", [P, KVH * NBP])

        ident, ones, upper, gsum, eones = (mats[:, i, :] for i in range(5))
        table, at = {}, 0
        for name, w in SMALL:
            table[name] = small[:, at:at + w]
            at += w

        def view(t, o, *shape):
            n = int(np.prod(shape))
            v = t[:, o:o + n]
            if len(shape) == 2:
                v = v.rearrange("p (a b) -> p a b", b=shape[1])
            if len(shape) == 3:
                v = v.rearrange("p (a b c) -> p a b c", b=shape[1], c=shape[2])
            return v

        xflat = xh[:, :, :].rearrange("p a b -> p (a b)")
        aflat = amT[:, 0:4, :].rearrange("p a b -> p (a b)")
        qflat = qT[:, :, :].rearrange("p a b -> p (a b)")
        pflat = proj[:, :, :].rearrange("p a b -> p (a b)")

        w_in = [view(arena, i * KC * WC, KC, WC) for i in range(2)]
        g1 = sb("g1", [P, KC])
        g2 = sb("g2", [P, KC])
        xnT = amT
        bands = view(slc_bias, 0, 3, 4, P)
        bands_s = view(slc_bias, 3 * 4 * P, 2, 4, NS)
        pool_w = view(kTs, 0, 4, P)
        dT = view(aflat, 512, NT)
        sel = view(aflat, 512 + NT, PAIRS, P)
        statep = view(kTw, 0, 512)
        qsq = view(xflat, 0, TILES, 512)
        ksq = view(qflat, 0, TILES, 256)
        qn = view(xflat, 0, TILES, 512)
        wblk = [view(arena, 0, 32, P), view(xflat, 0, 32, P)]
        posr = VC[:, 0, 0:HD]
        kcr, vcr, ktmp = (view(xflat, 4160 + i * 2 * 132, 2 * 132) for i in range(3))
        cache = [view(arena, 2 * KC * WC + i * SLOTS * P, SLOTS * 2, HD) for i in range(2)]
        pages = [view(arena, i * 4096, PAGES, 2 * P) for i in range(4)]
        Z = 4 * 4096
        pS = [view(slc_bias, i * 512, 512) for i in range(3)] + [proj[:, 0, CU:CU + 512]]
        dist = view(slc_bias, 3 * 512, 512)
        pT = [view(aflat, i * 512, 512) for i in range(2)]
        tmpo = view(aflat, 1672, 512)
        tmpc = view(qflat, 0, 512)
        vct = view(arena, Z + 7168, NBALL)
        zc = view(xflat, 4952, PAIRS, NBS)
        ec = view(xflat, 4160, PAIRS, NBS)
        score = view(xflat, 4288, PAIRS, NBS + 1)
        pw = view(aflat, 0, PAIRS, P)
        cT = view(aflat, 512, PAIRS, P)
        pcz = view(aflat, 1160, 4, H * NBP)
        pcm = view(aflat, 1416, 4, H * NBP)
        Vblk = view(aflat, 1672, 512)
        pcT = view(arena, Z + 7688, 4, P)
        a_tok = proj[:, 0:4, 0:512]
        SW, WW = PAST + NS, 512 + NS
        S = [view(arena, Z + i * SW, SW) for i in range(2)]
        SN = [view(arena, Z + 2 * SW + i * WW, WW) for i in range(2)]
        kb = [view(arena, Z + 2 * SW + 2 * WW + i * 512, 512) for i in range(4)]
        co = view(arena, Z + 2 * SW + 2 * WW + 2048, PAIRS * P)
        PT = proj[:, :, CU:CU + 512]
        PTw = qT[:, 0:2, 0:512]
        wst = [view(xflat, i * D, 4, 2 * P) for i in range(4)]
        diag = view(qflat, 1024, 3 * P)
        bcs = view(qflat, 1024 + 3 * P, 3 * P)
        t1 = view(qflat, 1024 + 6 * P, P)
        t2 = view(qflat, 1024 + 7 * P, P)
        w_out = view(arena, 0, KC, D)
        n2 = [view(qflat, i * D, D) for i in range(2)]
        n2T = QB
        g2b = view(pflat, 8000, D)
        logits = view(kTs, 0, TILES, NG + NE)
        w_r = sb("w_r", [P, KC, NG + NE])
        r16 = [view(kTs, 100 + i * 80, TILES, NE) for i in range(5)]
        pair16 = view(kTw, 96, 2, TILES * NE).rearrange("p k (i e) -> p k i e", e=NE)
        pos, ex = (view(kTw, 256 + i * 10, 2, TILES) for i in range(2))
        slot_f = view(kTw, 276, 2, TILES)
        last_hot = view(kTw, 300, 2, TILES)
        is_last = view(kTw, 310, 2, TILES)
        last_token, last_share = view(kTw, 320, 1), view(kTw, 321, 1)
        last_at = view(kTw, 322, TILES)
        over_f = view(kTw, 286, 2, TILES)
        r4 = [view(kTw, 400 + i * 20, TILES, NG) for i in range(4)]
        r1 = [view(kTw, 480 + i * 5, TILES) for i in range(10)]
        gates1 = sb("gates1", [P, 2, TILES])
        gates2 = sb("gates2", [P, 2, TILES])
        inside = sb("inside", [P, 2, TILES])
        row_i = sb("row_i", [P, 2, 2, TILES], I32)
        slot_i = sb("slot_i", [P, 2, TILES], I32)
        tokid = sb("tokid", [P, TILES], I32)
        idx = sb("idx", [P, NE], I32)
        chosen = view(kTw, 0, TILES + 1, NE)
        picks = view(pflat, 5632, 2 * TILES, P)
        tok_at = view(pflat, 5632 + 2 * TILES * P, 2, TILES * NE).rearrange("p k (i e) -> p k i e", e=NE)
        nmax = sb("nmax", [1, 1], I32)

        wslot = [view(arena, i * 4096, 4096) for i in range(6)]
        xg = [view(pflat, i * D, D) for i in range(2)]
        xgT = view(pflat, 2 * D, KC, P)
        sg = view(pflat, 3 * D, DE)
        he = view(pflat, 3 * D + DE, DE)
        heT = view(pflat, 4 * D, DE // P, P)
        ytok = view(pflat, 4 * D + DE, D)
        over_yb = [view(arena, 3 * 4096 + k * D, D) for k in range(2)]
        over_idx = sb("over_idx", [P, 1], I32)
        passed = sb("passed", [1, 1], I32)
        yb = [[view(arena, 2 * 4096 + (2 * i + k) * D, D) for k in range(2)] for i in range(TILES)]
        spot = view(arena, 2 * 4096 + 2 * TILES * D, TILES, P)
        more_rows = view(arena, 5 * 4096, D)

        ld_x = sems("x_loaded", TILES)
        ld_win = sems("w_in_loaded", 2)
        ld_half = sem("first_half_of_w_in_loaded")
        ld_c0 = sem("matrices_and_g1_loaded")
        ld_c1 = sem("first_tables_loaded")
        ld_c2 = sem("pool_tables_loaded")
        ld_c3 = sem("slc_bias_loaded")
        ld_sel = sem("sel_loaded")
        ld_pos = sem("pos_loaded")
        ld_wblk = sems("w_cmp_loaded", 2)
        ld_cache = sems("cmp_pages_loaded", 2)
        ld_dist = sem("dist_loaded")
        ld_pages = sems("slc_pages_loaded", 4)
        ld_values = sems("slc_values_loaded", 4)
        ld_win_state = sems("win_state_loaded", 4)
        ld_xr = sem("x_loaded_again")
        ld_wout = sem("w_out_loaded")
        ld_g2 = sem("g2_loaded")
        ld_zero = sem("slot_table_cleared")
        st_out = sem("outputs_stored")
        st_res = sem("results_stored")
        st_win = sems("win_state_stored", 4)
        act_sq = sem("squares_done")
        dve = sem("dve_step")
        rstd_ready = sem("roots_inverted")
        ms_ready = sem("mean_square_ready")
        rt_ready = sem("root_ready")
        heads_sq = sem("head_squares_ready")
        heads_ms = sem("head_means_ready")
        heads_rt = sem("head_roots_ready")
        q_ready = sem("q_normed")
        k_ready = sem("k_normed")
        k_step = sem("k_scaled")
        g_exp = sem("gate_exp_ready")
        g_ready = sem("gates_ready")
        cleared = sem("memory_cleared")
        extra = sem("cache_extras_ready")
        kc_sq = sem("kc_squares_ready")
        kc_ms = sem("kc_mean_ready")
        kc_rt = sem("kc_root_ready")
        kct_ready = sem("kc_transposed_ready")
        vct_ready = sem("vc_transposed_ready")
        cz = sem("cmp_logits_ready")
        ce = sem("cmp_exp_ready")
        cp = sem("cmp_p_ready")
        pcz_ready = sem("pc_logits_ready")
        pce = sem("pc_exp_ready")
        pcp = sem("pc_p_ready")
        vb = sem("vblk_ready")
        p_e = sem("prompt_exp_ready")
        p_a = sem("prompt_heads_added")
        s_z = sem("slc_logits_ready")
        s_e = sem("slc_exp_ready")
        w_z = sem("win_logits_ready")
        w_e = sem("win_exp_ready")
        diag_ready = sem("diag_ready")
        qb_ready = sem("qb_ready")
        a_ready = sem("a_sample_ready")
        h_ready = sem("h_ready")
        h_sq = sem("h_squares_ready")
        h_ms = sem("h_mean_ready")
        h_rt = sem("h_root_ready")
        n_ready = sem("n2_ready")
        n_stored = sems("n2_stored", 2)
        qb_clear = sem("qb_cleared")
        z_clear = sem("small_areas_cleared")
        ld_w = sems("expert_matrix_loaded", 6)
        product = sem("expert_product_done")
        down_half = sem("half_of_down_done")
        up_half = sem("half_of_up_done")
        xg_ld = sems("tokens_gathered", 2)
        xt_full = sem("gathered_transposed")
        xgt_ready = sem("gathered_copied")
        sg_ready = sem("silu_ready")
        he_ready = sem("hidden_ready")
        ht_full = sem("hidden_transposed")
        ht_taken = sem("hidden_copied")
        y_taken = sem("expert_rows_copied")
        st_y = sem("expert_rows_stored")
        y_ld = sems("expert_rows_gathered", TILES)
        y_ready = sem("result_halves_ready")
        o_idx = sem("more_idx_loaded")
        o_passed = sem("more_idx_passed")
        o_xg = sem("more_tokens_gathered")
        o_w = sem("more_matrices_loaded")
        o_x = sem("more_transposed")
        o_xc = sem("more_copied")
        o_gu = sem("more_gate_up_done")
        o_sg = sem("more_silu_ready")
        o_he = sem("more_hidden_ready")
        o_ht = sem("more_hidden_transposed")
        o_hc = sem("more_hidden_copied")
        o_p = sem("more_product_done")
        o_y = sem("more_rows_copied")
        o_st = sem("more_rows_stored")
        o_yl = sem("more_rows_gathered")
        o_add = sem("more_rows_added")
        r_exp_in = sem("router_exp_in")
        r_exp = sem("router_exp_ready")
        oh_ready = sem("onehots_ready")
        slots_ready = sem("slots_ready")
        scattered = sem("tokens_scattered")
        idx_ready = sem("idx_ready")
        picks_ready = sem("slot_onehots_ready")
        counted = sem("tokens_counted")
        early_added = sem("gathered_rows_added")
        last_in = sem("last_gates_ready")
        last_full = sem("last_shares_full")
        last_ready = sem("last_spread_ready")
        fin_full = sem("last_products_done")

        def kb_free(eng, t, j):
            n = 10 * t + j - 4
            if n >= 0:
                t0, j0 = n // 10, n % 10
                filled(eng, ("win_s", t0) if j0 >= 8 else ("slc_s", t0, j0 // 2))

        def crowded(eng):
            eng.wait_ge(counted, 1)
            return eng.value_load(nmax[:, :], min_val=0, max_val=NT) > P

        block = ctx.enter_context(nc.Block())

        @block.sync
        def _(sp):
            def load_x(i, signal):
                src = a["x_prompt"][0, i * P:(i + 1) * P, :] if i < 4 else a["x_sample"].rearrange("b q d -> (b q) d")
                sp.dma_start(xh[0:ROWS[i], i, :], src).then_inc(signal, 16)

            load_x(0, ld_x[0])
            sp.dma_start(mats[:, :, :], a["c_mats"]).then_inc(ld_c0, 16)
            sp.dma_start(g1[:, :], a["norm1_g"].rearrange("(k p) -> p k", p=P), allow_slow_non_contiguous=True).then_inc(ld_c0, 16)

            def load_win(c, k0=0, k1=KC, signal=None):
                src = a["w_in"].rearrange("(k p) c -> p k c", p=P)[:, k0:k1, c * WC:(c + 1) * WC]
                sp.dma_start(w_in[c % 2][:, k0:k1, :], src).then_inc(signal or ld_win[c % 2], 16)

            load_win(0, 0, KC // 2, ld_half)
            load_win(0, KC // 2, KC)
            for i in range(1, TILES):
                load_x(i, ld_x[i])
            load_win(1)
            sp.dma_start(small[:, :], a["c_small"]).then_inc(ld_c1, 16)
            for j, name in enumerate(("q_norm_g", "k_norm_slc_g", "k_norm_win_g")):
                sp.dma_start(gains[:, j, :], spread(a[name].rearrange("(a n) -> a n", a=1), 0, P)).then_inc(ld_c1, 16)
            for par in range(2):
                sp.dma_start(cols[64 * par:64 * par + 64, 0:1], a["k_norm_cmp_g"].rearrange("(n a) -> n a", a=1)).then_inc(ld_c1, 16)
            for g in range(4):
                sp.dma_start(cols[:, 1 + g:2 + g], a["pool_scale"][g * P:(g + 1) * P].rearrange("(n a) -> n a", a=1)).then_inc(ld_c1, 16)
            sp.dma_start(w_r[:, :, 0:NG], a["w_router_group"].rearrange("(k p) g -> p k g", p=P)).then_inc(ld_c1, 16)
            sp.dma_start(w_r[:, :, NG:NG + NE], a["w_router_expert"].rearrange("(k p) g -> p k g", p=P)).then_inc(ld_c1, 16)
            sp.dma_start(tokid[:, :], a["c_tokid"]).then_inc(ld_c1, 16)
            sp.dma_start(g2[:, :], a["norm2_g"].rearrange("(k p) -> p k", p=P), allow_slow_non_contiguous=True).then_inc(ld_c1, 16)
            sp.dma_start(slc_bias[:, :], a["c_bands"]).then_inc(ld_c2, 16)
            sp.dma_start(pool_w, a["pool_w"].rearrange("g c e -> c g e")).then_inc(ld_c2, 16)
            sp.dma_start(statep[0:120, :], a["state_pool"].rearrange("b r c -> (b r) c")).then_inc(ld_c2, 16)

            table_rows = a["page_table"]
            regs = [sp.alloc_register(f"page{k}") for k in range(PAGES)]

            def load_pages(first, count, emit):
                with sp.Fori(first, first + count) as b:
                    sp.load(regs, table_rows[bass.ds(b, 1), :])
                    for k in range(PAGES):
                        emit(b, k, sp.snap(regs[k], min_val=0, max_val=a["cache_cmp_kv"].shape[0] - 1))

            def load_cache(r):
                which, half = r // 2, r % 2
                if r >= 2:
                    filled(sp, ("cmp", r - 2))

                def one(b, k, page):
                    src = a["cache_cmp_kv"][bass.ds(page, 1), :, which, :, :].rearrange("a p h d -> (a p) h d")
                    dst = cache[half][:, bass.ds((b * PAGES + k - half * 64) * 2, 2), :]
                    sp.dma_start(dst, src).then_inc(ld_cache[half], 16)

                load_pages(4 * half, 4, one)

            def load_wblk(which, part):
                w = a["w_cmp_k"] if which == 0 else a["w_cmp_v"]
                for par in range(2):
                    sp.dma_start(wblk[part][64 * par:64 * par + 64, :, 64 * par:64 * par + 64],
                                 w[:, 32 * part:32 * part + 32, :]).then_inc(ld_wblk[part], 16)

            load_cache(0)
            for c in range(2, 4):
                filled(sp, ("in", c - 2, TILES - 1))
                load_win(c)
            load_cache(1)
            for par in range(2):
                sp.dma_start(posr[64 * par:64 * par + 64, :], a["cmp_pos_emb"]).then_inc(ld_pos, 16)
            filled(sp, ("in", 3, TILES - 1))
            sp.dma_start(sel[0:NS, :, :], a["c_sel"]).then_inc(ld_sel, 16)
            sp.wait_ge(cleared, 4)
            load_wblk(0, 0)
            for name in (("pool_p", 3), ("pool_s", 3)):
                filled(sp, name)
            sp.dma_start(dist, a["c_dist"]).then_inc(ld_dist, 16)
            sp.wait_ge(cleared, 5)
            load_wblk(0, 1)
            load_cache(2)
            filled(sp, ("cmp", 1))
            load_wblk(1, 0)
            load_wblk(1, 1)
            load_cache(3)

            def load_slc(b, first, count):
                sp.load(regs, table_rows[b:b + 1, :])
                for k in range(PAGES):
                    page = sp.snap(regs[k], min_val=0, max_val=a["cache_slc_kv"].shape[0] - 1)
                    src = a["cache_slc_kv"][bass.ds(page, 1), :, first:first + count, :, :].rearrange("a p c h d -> (a p) (c h d)")
                    sp.dma_start(pages[b % 4][:, k, first * P:(first + count) * P], src)\
                        .then_inc((ld_values if first else ld_pages)[b % 4], 16)

            def load_wst(b):
                if b >= 4:
                    filled(sp, ("win_o", b // 2 - 2))
                    sp.wait_ge(st_win[b % 4], 32)
                src = a["state_win_kv"][b].rearrange("(n p) c h d -> p n (c h d)", p=P)
                sp.dma_start(wst[b % 4], src).then_inc(ld_win_state[b % 4], 16)

            filled(sp, ("cmp", 2))
            load_slc(1, 0, 2)
            load_slc(2, 0, 2)
            filled(sp, ("cmp", 3))
            load_slc(0, 0, 2)
            load_wst(0)
            load_wst(1)
            load_slc(3, 0, 2)
            load_wst(2)
            load_wst(3)
            filled(sp, ("p_T", len(prompt_units()) - 1))
            sp.dma_start(slc_bias[:, :], a["c_slc_bias"]).then_inc(ld_c3, 16)
            for t in range(2, PAIRS):
                filled(sp, ("slc_k", t - 2, 3, 1))
                for b in (2 * t, 2 * t + 1):
                    load_slc(b, 0, 1)
            for t in range(2, PAIRS):
                filled(sp, ("slc_o", t - 2))
                for b in (2 * t, 2 * t + 1):
                    load_wst(b)
                for b in (2 * t, 2 * t + 1):
                    load_slc(b, 1, 1)
            filled(sp, ("slc_o", 2))
            for g in range(G):
                for h2 in range(KVH):
                    r0 = (h2 * G + g) * HD
                    sp.dma_start(w_out[64 * h2:64 * h2 + 64, g, :], a["w_out"][r0:r0 + HD, :]).then_inc(ld_wout, 16)
            sp.dma_start(w_out[:, 4:8, :], a["w_out"][512:1024, :].rearrange("(k p) c -> p k c", p=P)).then_inc(ld_wout, 16)
            for t in (2, 3):
                filled(sp, ("win_o", t))
            for i in range(4):
                sp.wait_ge(st_win[i], 64)
            for i in range(TILES):
                load_x(i, ld_xr)
            for i in range(4):
                filled(sp, ("aT", i))
            sp.dma_start(g2b, spread(a["norm2_g"].rearrange("(a n) -> a n", a=1), 0, P)).then_inc(ld_g2, 16)

            def load_matrix(e, j, slot):
                if j < 2:
                    w = (a["w_gate"], a["w_up"])[j]
                    dst = wslot[slot].rearrange("p (k f) -> p k f", k=KC)
                    src = w[bass.ds(e, 1), :, :].rearrange("a (k p) f -> p (a k) f", p=P)
                else:
                    dst = wslot[slot].rearrange("p (k f) -> p k f", k=DE // P)
                    src = a["w_down"][bass.ds(e, 1), :, :].rearrange("a (k p) f -> p (a k) f", p=P)
                sp.dma_start(dst, src).then_inc(ld_w[slot], 16)

            load_matrix(0, 0, 2)
            load_matrix(0, 1, 3)
            sp.wait_ge(a_ready, PAIRS)
            load_matrix(0, 2, 4)
            load_matrix(1, 0, 5)
            filled(sp, ("h", TILES - 1, 1))
            load_matrix(1, 1, 0)
            load_matrix(1, 2, 1)
            with sp.Fori(1, NE // 2) as it:
                for j in range(6):
                    sp.wait_ge(product, it * 6 + (j - 5))
                    load_matrix(it * 2 + j // 3, j % 3, (j + 2) % 6)

            with sp.If(crowded(sp)):
                sp.wait_ge(product, 3 * NE)
                sp.wait_ge(early_added, 1)
                with sp.Fori(0, NE) as e:
                    sp.wait_ge(o_p, e * MORE)
                    for j in range(3):
                        if j < 2:
                            dst = wslot[j].rearrange("p (k f) -> p k f", k=KC)
                            src = (a["w_gate"], a["w_up"])[j][bass.ds(e, 1), :, :].rearrange("a (k p) f -> p (a k) f", p=P)
                        else:
                            dst = wslot[j].rearrange("p (k f) -> p k f", k=DE // P)
                            src = a["w_down"][bass.ds(e, 1), :, :].rearrange("a (k p) f -> p (a k) f", p=P)
                        sp.dma_start(dst, src).then_inc(o_w, 16)

            for n in range(2 * TILES):
                i, c = n % TILES, slice(n // TILES * 512, (n // TILES + 1) * 512)
                sp.wait_ge(y_ready, n + 1)
                dst = out["y_prompt"][0, i * P:(i + 1) * P, c] if i < 4 else out["y_sample"].rearrange("b q d -> (b q) d")[:, c]
                sp.dma_start(dst, xh[0:ROWS[i], i, c]).then_inc(st_res, 16)
            sp.wait_ge(st_res, 32 * TILES)

        @block.tensor
        def _(pe):
            pe.wait_ge(ld_c0, 32)

            def xT(i):
                n = ROWS[i]
                pe.wait_ge(ld_x[i], 16)
                for half in range(2):
                    opened(pe, ("xT", i, half))
                    for k in range(4):
                        c = (half * 4 + k) * P
                        last = pe.transpose(ps(("xT", i, half))[:, k * P:k * P + n], xh[0:n, i, c:c + P], ident[0:n, 0:n])
                    written(last, ("xT", i, half))

            xT(0)
            for c in range(4):
                for i in range(TILES):
                    n = ROWS[i]
                    if c == 0:
                        if i + 1 < TILES:
                            xT(i + 1)
                        for half in range(2):
                            taken(pe, ("xT", i, half))
                    if c == i == 0:
                        pe.wait_ge(ld_half, 16)
                    elif i == 0:
                        pe.wait_ge(ld_win[c % 2], 16 * (c // 2 + 1))
                    opened(pe, ("in", c, i))
                    for k in range(KC):
                        if c == i == 0 and k == KC // 2:
                            pe.wait_ge(ld_win[0], 16)
                        last = pe.matmul(ps(("in", c, i))[0:n, 0:WC], xnT[:, k, i * P:i * P + n], w_in[c % 2][:, k, :],
                                         start=k == 0, stop=k == KC - 1)
                    written(last, ("in", c, i))

            for i in range(TILES):
                taken(pe, ("in", 3, i))
                taken(pe, ("in", 2, i))
            pe.wait_ge(ld_c2, 16 * 3)
            for g in range(4):
                u = lambda i, n: proj[0:n, i, CU + g * P:CU + (g + 1) * P]
                opened(pe, ("pool_p", g))
                for i in range(4):
                    o = ps(("pool_p", g))[:, i * P:(i + 1) * P]
                    last = pe.matmul(o, u(i, P), bands[:, 0 if i == 0 else 1, g, :], start=True, stop=i == 0)
                    if i:
                        last = pe.matmul(o, u(i - 1, P), bands[:, 2, g, :], start=False, stop=True)
                written(last, ("pool_p", g))
                opened(pe, ("pool_s", g))
                o = ps(("pool_s", g))[:, 0:NS]
                pe.matmul(o, u(4, NS), bands_s[0:NS, 0, g, :], start=True, stop=False)
                last = pe.matmul(o, statep[0:120, g * P:(g + 1) * P], bands_s[0:120, 1, g, :], start=False, stop=True)
                written(last, ("pool_s", g))
                taken(pe, ("pool_p", g))
                taken(pe, ("pool_s", g))
                opened(pe, ("mix_p", g))
                written(pe.matmul(ps(("mix_p", g))[:, :], pool_w[:, g, :], dT[:, 0:SEQ], start=True, stop=True), ("mix_p", g))
                opened(pe, ("mix_s", g))
                written(pe.matmul(ps(("mix_s", g))[:, 0:NS], pool_w[:, g, :], dT[:, SEQ:NT], start=True, stop=True), ("mix_s", g))

            def compress(r, d):
                which, half = r // 2, r % 2
                if d == 0:
                    pe.wait_ge(ld_cache[half], (which + 1) * 64 * 16)
                    pe.wait_ge(extra, (1, 2, 2, 3)[r])
                    opened(pe, ("cmp", r))
                if d % 32 == 0:
                    pe.wait_ge(ld_wblk[d // 32], 32 * (which + 1))
                nmov = 130 if half == 0 else 136
                last = pe.matmul(ps(("cmp", r))[:, 0:nmov], wblk[d // 32][:, d % 32, :], cache[half][:, 0:nmov, d],
                                 start=d == 0, stop=d == HD - 1)
                if d == HD - 1:
                    written(last, ("cmp", r))

            pe.wait_ge(q_ready, 1)
            pe.wait_ge(k_ready, 2 * TILES)
            for i in range(TILES):
                n = ROWS[i]
                opened(pe, ("qT", i))
                for j in range(G):
                    last = pe.transpose(ps(("qT", i))[:, j * P:j * P + n], qn[0:n, i, j * P:(j + 1) * P], ident[0:n, 0:n])
                written(last, ("qT", i))
                opened(pe, ("kT", i))
                for j, c in enumerate((CSLC, CWIN)):
                    last = pe.transpose(ps(("kT", i))[:, j * P:j * P + n], proj[0:n, i, c:c + P], ident[0:n, 0:n])
                written(last, ("kT", i))
            pe.wait_ge(g_ready, 1)
            pe.wait_ge(ld_sel, 16)
            opened(pe, "gate_rows")
            for t in range(PAIRS):
                last = pe.matmul(ps("gate_rows")[:, t * 24:t * 24 + 24], sel[0:NS, t, :], gate[0:NS, 4, :], start=True, stop=True)
            written(last, "gate_rows")

            def beside(u):
                if u == AT_NORM:
                    pe.wait_ge(kc_sq, 1)
                    opened(pe, "key_norm")
                    written(pe.matmul(ps("key_norm")[:, 0:264], eones, ktmp, start=True, stop=True), "key_norm")
                if u == AT_LOGITS:
                    pe.wait_ge(kct_ready, 6)
                    pe.wait_ge(qb_ready, 16)
                    opened(pe, "cmp_s")
                    for t in range(PAIRS):
                        for s in range(2):
                            b = 2 * t + s
                            last = pe.matmul(ps("cmp_s")[:, t * NBS:(t + 1) * NBS], QB[:, b, :], KCT[:, b * NBS:(b + 1) * NBS],
                                             start=s == 0, stop=s == 1)
                    written(last, "cmp_s")
                    opened(pe, "pc_s")
                    for i in range(4):
                        for j in range(G):
                            c = i * H * NBP + j * 2 * NBP
                            last = pe.matmul(ps("pc_s")[:, c:c + 2 * NBP], qT[:, j, i * P:(i + 1) * P], kpb[:, :], start=True, stop=True)
                    written(last, "pc_s")
                if u == AT_SUM:
                    pe.wait_ge(cp, 1)
                    opened(pe, "cmp_sum")
                    written(pe.matmul(ps("cmp_sum")[:, 0:P], gsum, zc.rearrange("p a b -> p (a b)"), start=True, stop=True), "cmp_sum")
                if u == AT_VALUES:
                    pe.wait_ge(vct_ready, 4)
                    opened(pe, "vcT")
                    for j, n in enumerate((P, P, NBP)):
                        last = pe.transpose(ps("vcT")[0:n, j * P:(j + 1) * P], vct[:, j * P:j * P + n], ident)
                    written(last, "vcT")

                if u == AT_TURNED:
                    pe.wait_ge(pcp, 1)
                    opened(pe, "pc_T")
                    for i in range(4):
                        last = pe.transpose(ps("pc_T")[0:64, i * P:(i + 1) * P], pcz[:, i, :], ident)
                    written(last, "pc_T")

            def cmp_values():
                pe.wait_ge(cp, 2)
                opened(pe, "cmp_T")
                for t in range(PAIRS):
                    last = pe.transpose(ps("cmp_T")[:, t * P:(t + 1) * P], pw[:, t, :], ident)
                written(last, "cmp_T")
                pe.wait_ge(vb, 16 * H)
                taken(pe, "pc_T")
                for i in range(4):
                    opened(pe, ("pc_o", i))
                    written(pe.matmul(ps(("pc_o", i))[:, :], pcT[0:64, i, :], Vblk[0:64, :], start=True, stop=True), ("pc_o", i))
                taken(pe, "cmp_T")
                taken(pe, "vcT")
                opened(pe, "cmp_o")
                for t in range(PAIRS):
                    last = pe.matmul(ps("cmp_o")[:, t * P:(t + 1) * P], VC[:, t // 2, :], cT[:, t, :], start=True, stop=True)
                written(last, "cmp_o")

            units = prompt_units()

            def p_scores(u):
                b, i, h = units[u]
                k0, n = 64 * (h // G), (i + 1) * P
                kt = (kTs, kTw)[b]
                opened(pe, ("p_s", u))
                written(pe.matmul(ps(("p_s", u))[:, 0:n], qT[k0:k0 + 64, h % G, i * P:(i + 1) * P], kt[k0:k0 + 64, 0:n],
                                  start=True, stop=True), ("p_s", u))

            for u in range(AHEAD):
                p_scores(u)
            for u in range(len(units) + 1):
                if u + AHEAD < len(units):
                    p_scores(u + AHEAD)
                for r, d in compress_steps(u):
                    compress(r, d)
                beside(u)
                if u < len(units):
                    b, i, h = units[u]
                    pe.wait_ge(p_e, u + 1)
                    opened(pe, ("p_T", u))
                    for c in range(i + 1):
                        last = pe.transpose(ps(("p_T", u))[:, c * P:(c + 1) * P], pS[u % 4][:, c * P:(c + 1) * P], ident)
                    written(last, ("p_T", u))
                if u:
                    b, i, h = units[u - 1]
                    taken(pe, ("p_T", u - 1))
                    if h == 0:
                        opened(pe, ("p_o", b, i))
                    v0 = (CSLC, CWIN)[b] + P + 64 * (h // G)
                    for c in range(i + 1):
                        last = pe.matmul(ps(("p_o", b, i))[:, place(h) * HD:(place(h) + 1) * HD], pT[(u - 1) % 2][:, c * P:(c + 1) * P],
                                         proj[:, c, v0:v0 + HD], start=c == 0, stop=c == i)
                    if h == H - 1:
                        written(last, ("p_o", b, i))

            def s_scores(t):
                for c in range(5):
                    if c < 4:
                        for s in range(2):
                            b = 2 * t + s
                            if c == 0:
                                pe.wait_ge(ld_pages[b % 4], 16 * PAGES * (b // 4 + 1))
                            name = ("slc_k", t, c, s)
                            opened(pe, name)
                            for k in range(4):
                                last = pe.transpose(ps(name)[:, k * P:(k + 1) * P], pages[b % 4][:, 4 * c + k, 0:P], ident)
                            written(last, name)
                    if c:
                        name = ("slc_s", t, c - 1)
                        opened(pe, name)
                        for s in range(2):
                            taken(pe, ("slc_k", t, c - 1, s))
                            last = pe.matmul(ps(name)[:, :], QB[:, 2 * t + s, :], kb[(10 * t + 2 * (c - 1) + s) % 4],
                                             start=s == 0, stop=s == 1)
                        written(last, name)
                name = ("new_s", t)
                opened(pe, name)
                for s in range(2):
                    last = pe.matmul(ps(name)[:, 0:NS], QB[:, 2 * t + s, :], kTs[:, SEQ:NT], start=s == 0, stop=s == 1)
                written(last, name)
                for s in range(2):
                    b = 2 * t + s
                    pe.wait_ge(ld_win_state[b % 4], 16 * (b // 4 + 1))
                    name = ("win_k", t, s)
                    opened(pe, name)
                    for k in range(4):
                        last = pe.transpose(ps(name)[:, k * P:(k + 1) * P], wst[b % 4][:, k, 0:P], ident)
                    written(last, name)
                name = ("win_s", t)
                opened(pe, name)
                for s in range(2):
                    taken(pe, ("win_k", t, s))
                    last = pe.matmul(ps(name)[:, :], QB[:, 2 * t + s, :], kb[(10 * t + 8 + s) % 4], start=s == 0, stop=s == 1)
                written(last, name)
                name = ("neww_s", t)
                opened(pe, name)
                for s in range(2):
                    last = pe.matmul(ps(name)[:, 0:NS], QB[:, 2 * t + s, :], kTw[:, SEQ:NT], start=s == 0, stop=s == 1)
                written(last, name)

            def s_values(t):
                for b in (2 * t, 2 * t + 1):
                    if b >= 4:
                        pe.wait_ge(ld_values[b % 4], 16 * PAGES)
                pe.wait_ge(s_e, t + 1)
                for c in range(5):
                    name = ("slc_T", t, c)
                    opened(pe, name)
                    if c < 4:
                        for k in range(4):
                            o = (4 * c + k) * P
                            last = pe.transpose(ps(name)[:, k * P:(k + 1) * P], S[t % 2][:, o:o + P], ident)
                    else:
                        last = pe.transpose(ps(name)[0:NS, 0:P], S[t % 2][:, PAST:SW], ident)
                    written(last, name)
                pe.wait_ge(w_e, t + 1)
                for c in range(2):
                    name = ("win_T", t, c)
                    opened(pe, name)
                    if c == 0:
                        for k in range(4):
                            last = pe.transpose(ps(name)[:, k * P:(k + 1) * P], SN[t % 2][:, k * P:(k + 1) * P], ident)
                    else:
                        last = pe.transpose(ps(name)[0:NS, 0:P], SN[t % 2][:, 512:WW], ident)
                    written(last, name)
                name = ("slc_o", t)
                opened(pe, name)
                for c in range(5):
                    taken(pe, ("slc_T", t, c))
                for s in range(2):
                    o = ps(name)[:, 64 * s:64 * s + 64]
                    for k in range(PAGES):
                        c0 = (k % 4) * P + 64 * s
                        pe.matmul(o, pages[(2 * t + s) % 4][:, k, P:2 * P], PT[:, k // 4, c0:c0 + 64], start=k == 0, stop=False)
                    last = pe.matmul(o, proj[0:NS, 4, CSLC + P:CSLC + 2 * P], PT[0:NS, 4, 64 * s:64 * s + 64],
                                     start=False, stop=True)
                written(last, name)
                name = ("win_o", t)
                opened(pe, name)
                for c in range(2):
                    taken(pe, ("win_T", t, c))
                for s in range(2):
                    o = ps(name)[:, 64 * s:64 * s + 64]
                    for k in range(4):
                        c0 = k * P + 64 * s
                        pe.matmul(o, wst[(2 * t + s) % 4][:, k, P:2 * P], PTw[:, 0, c0:c0 + 64], start=k == 0, stop=False)
                    last = pe.matmul(o, proj[0:NS, 4, CWIN + P:CWIN + 2 * P], PTw[0:NS, 1, 64 * s:64 * s + 64],
                                     start=False, stop=True)
                written(last, name)
                pe.wait_ge(diag_ready, t + 1)
                name = ("bcast", t)
                opened(pe, name)
                written(pe.matmul(ps(name)[:, 0:3 * P], ones, diag, start=True, stop=True), name)

            for t in range(PAIRS + 1):
                if t < PAIRS:
                    s_scores(t)
                if t == 1:
                    cmp_values()
                if t == PAIRS:
                    pe.wait_ge(p_a, 12)
                    for i in range(4):
                        opened(pe, ("aT", i))
                        for j in range(G):
                            last = pe.transpose(ps(("aT", i))[:, j * P:(j + 1) * P], a_tok[:, i, j * P:(j + 1) * P], ident)
                        written(last, ("aT", i))
                if t:
                    s_values(t - 1)

            pe.wait_ge(ld_wout, 16 * 9)
            def projected(i, half):
                n = ROWS[i]
                opened(pe, ("h", i, half))
                for k in range(KC):
                    last = pe.matmul(ps(("h", i, half))[0:n, :], amT[:, k, i * P:i * P + n],
                                     w_out[:, k, half * 512:(half + 1) * 512], start=k == 0, stop=k == KC - 1)
                written(last, ("h", i, half))

            def rows_T(i):
                n = ROWS[i]
                pe.wait_ge(h_ready, i + 1)
                for half in range(2):
                    opened(pe, ("nT", i, half))
                    for k in range(4):
                        c = (half * 4 + k) * P
                        last = pe.transpose(ps(("nT", i, half))[:, k * P:k * P + n], xh[0:n, i, c:c + P], ident[0:n, 0:n])
                    written(last, ("nT", i, half))

            def router_logits(i):
                n = ROWS[i]
                for half in range(2):
                    taken(pe, ("nT", i, half))
                opened(pe, ("logit", i))
                for k in range(KC):
                    last = pe.matmul(ps(("logit", i))[0:n, 0:NG + NE], n2T[:, k, 0:n], w_r[:, k, :], start=k == 0, stop=k == KC - 1)
                written(last, ("logit", i))

            for i in range(TILES + 1):
                if i < 4:
                    taken(pe, ("aT", i))
                if i == 4:
                    pe.wait_ge(a_ready, PAIRS)
                if i < TILES:
                    projected(i, 0)
                if i:
                    rows_T(i - 1)
                if i < TILES:
                    projected(i, 1)
                if i:
                    router_logits(i - 1)
            pe.wait_ge(oh_ready, 1)
            opened(pe, "prefix")
            both = chosen[:, :, :].rearrange("p a b -> p (a b)")
            n = (TILES + 1) * NE
            pe.matmul(ps("prefix")[:, 0:n], upper, both, start=True, stop=False)
            for k in range(1, TILES + 1):
                last = pe.matmul(ps("prefix")[:, k * NE:n], ones, both[:, 0:n - k * NE], start=False, stop=k == TILES)
            written(last, "prefix")
            opened(pe, "idx")
            for n in range(2 * TILES):
                i, k = n // 2, n % 2
                pe.wait_ge(picks_ready, n + 1)
                last = pe.matmul(ps("idx")[:, 0:NE], picks[:, n, :], tok_at[:, k, i, :], start=n == 0, stop=n == 2 * TILES - 1)
            written(last, "idx")

            for b in range(8):
                pe.wait_ge(free[b], used[b])
            BG, BU, BX, BH, BY = EXPERT_BANKS

            def gathered_T(slot, turn, halves):
                pe.wait_ge(xg_ld[slot], turn)
                for half in halves:
                    for k in range(4):
                        c = (half * 4 + k) * P
                        last = pe.transpose(BX[half][:, k * P:(k + 1) * P], xg[slot][:, c:c + P], ident)
                if halves[-1] == 1:
                    last.then_inc(xt_full, 1)

            def expert(it, s, last_one):
                e = it * 2 + s
                pe.wait_ge(xgt_ready, e * 2 + 2)
                slot = (3 * s + 2) % 6
                pe.wait_ge(ld_w[slot], it * 16 + 16)
                pe.wait_ge(sg_ready, e)
                for k in range(KC):
                    ins = pe.matmul(BG[:, :], xgT[:, k, :], wslot[slot][:, k * DE:(k + 1) * DE], start=k == 0, stop=k == KC - 1)
                ins.then_inc(product, 1)
                slot = (3 * s + 3) % 6
                pe.wait_ge(ld_w[slot], it * 16 + 16)
                pe.wait_ge(he_ready, 2 * e)
                for half in range(2):
                    for k in range(KC):
                        c = k * DE + half * HALF
                        ins = pe.matmul(BU[half][:, 0:HALF], xgT[:, k, :], wslot[slot][:, c:c + HALF],
                                        start=k == 0, stop=k == KC - 1)
                    ins.then_inc((up_half, product)[half], 1)
                for half in range(2):
                    if not last_one:
                        gathered_T((s + 1) % 2, (it + (s + 1) // 2) * 16 + 16, [half])
                    pe.wait_ge(he_ready, 2 * e + half + 1)
                    for k in (2 * half, 2 * half + 1):
                        ins = pe.transpose(BH[half][:, k % 2 * P:(k % 2 + 1) * P], he[:, k * P:(k + 1) * P], ident)
                    ins.then_inc(ht_full, 1)
                slot = (3 * s + 4) % 6
                pe.wait_ge(ld_w[slot], it * 16 + 16)
                pe.wait_ge(y_taken, e * 2)
                for half in range(2):
                    for k in range(DE // P):
                        if half == 0 and k % 2 == 0:
                            pe.wait_ge(ht_taken, 2 * e + k // 2 + 1)
                        c = k * D + half * 512
                        ins = pe.matmul(BY[half][:, :], heT[:, k, :], wslot[slot][:, c:c + 512], start=k == 0, stop=k == DE // P - 1)
                    ins.then_inc((down_half, product)[half], 1)

            more = crowded(pe)
            gathered_T(0, 16, [0, 1])
            with pe.Fori(0, NE // 2 - 1) as it:
                for s in range(2):
                    expert(it, s, False)
            expert(NE // 2 - 1, 0, False)
            pe.wait_ge(last_in, 1)
            pe.wait_ge(xgt_ready, 2 * NE)
            for n in range(2 * TILES):
                i, k = n // 2, n % 2
                last = pe.matmul(BX[1][:, 0:1], picks[:, n, :], last_hot[:, k, i:i + 1], start=n == 0, stop=n == 2 * TILES - 1)
            last.then_inc(last_full, 1)
            expert(NE // 2 - 1, 1, True)

            with pe.If(more):
                pe.wait_ge(y_taken, 2 * NE)
                with pe.Fori(0, NE) as e:
                    with pe.Fori(0, MORE) as t:
                        n = e * MORE + t
                        pe.wait_ge(o_xg, n * 16 + 16)
                        for k in range(KC):
                            ins = pe.transpose(BX[k // 4][:, k % 4 * P:(k % 4 + 1) * P], xg[0][:, k * P:(k + 1) * P], ident)
                        ins.then_inc(o_x, 1)
                        pe.wait_ge(o_w, e * 48 + 48)
                        pe.wait_ge(o_xc, n * 2 + 2)
                        for j in range(2):
                            for k in range(KC):
                                ins = pe.matmul((BG, BU[0])[j][:, :], xgT[:, k, :], wslot[j][:, k * DE:(k + 1) * DE],
                                                start=k == 0, stop=k == KC - 1)
                        ins.then_inc(o_gu, 1)
                        pe.wait_ge(o_he, n + 1)
                        for k in range(DE // P):
                            ins = pe.transpose(BH[0][:, k * P:(k + 1) * P], he[:, k * P:(k + 1) * P], ident)
                        ins.then_inc(o_ht, 1)
                        pe.wait_ge(o_hc, n + 1)
                        for half in range(2):
                            for k in range(DE // P):
                                c = k * D + half * 512
                                ins = pe.matmul(BY[half][:, :], heT[:, k, :], wslot[2][:, c:c + 512], start=k == 0, stop=k == DE // P - 1)
                        ins.then_inc(o_p, 1)
                pe.wait_ge(o_y, 2 * NE * MORE)

            pe.wait_ge(last_ready, TILES)
            for n in range(2 * TILES):
                i, half = n % TILES, n // TILES
                if i == 0:
                    pe.wait_ge(y_taken, 2 * NE - 1 + half)
                if n >= 7:
                    pe.wait_ge(y_ready, n - 6)
                pe.matmul(bank[FINAL[n % 7]][0:ROWS[i], :], spot[:, i, 0:ROWS[i]], ytok[:, half * 512:(half + 1) * 512],
                          start=True, stop=True).then_inc(fin_full, 1)

        @block.scalar
        def _(sc):
            def copy4(name, dst, n):
                filled(sc, name)
                return sc.activation(dst, ps(name)[:, :].rearrange("p (k t) -> p k t", k=4)[:, :, 0:n], ACT.Copy)

            sc.wait_ge(cleared, 2)
            for i in range(TILES):
                n = ROWS[i]
                sc.wait_ge(ld_x[i], 16)
                if i:
                    sc.wait_ge(act_sq, i)
                sc.activation(view(pflat, 0, D)[0:n, :], xh[0:n, i, :], ACT.Square, accum_out=st[0:n, i:i + 1]).then_inc(act_sq, 1)
            sc.wait_ge(ms_ready, 1)
            sc.activation(st[:, 16:21], st[:, 8:13], ACT.Sqrt).then_inc(rt_ready, 1)

            sc.wait_ge(rstd_ready, 1)
            for c in range(4):
                for i in range(TILES):
                    n = ROWS[i]
                    if (c * TILES + i) % 2 == 0:
                        filled(sc, ("in", c, i))
                        read(sc.activation(proj[0:n, i, c * WC:(c + 1) * WC], ps(("in", c, i))[0:n, 0:WC], ACT.Copy,
                                           scale=rstd[0:n, 0, i:i + 1]), ("in", c, i))
                if c == 2:
                    for i in range(TILES):
                        for c in range(3):
                            taken(sc, ("in", c, i))
                    sc.activation(qsq, proj[:, :, 0:512], ACT.Square).then_inc(heads_sq, 1)
                    sc.activation(ksq[:, :, 0:P], proj[:, :, CSLC:CSLC + P], ACT.Square).then_inc(heads_sq, 1)
                    sc.activation(ksq[:, :, P:2 * P], proj[:, :, CWIN:CWIN + P], ACT.Square).then_inc(heads_sq, 1)
                    sc.wait_ge(heads_ms, 1)
                    sc.activation(nrm[:, :, :], nrm[:, :, :], ACT.Sqrt).then_inc(heads_rt, 1)
                    sc.activation(gate[:, :, :], proj[:, :, CGATE:CGATE + 24], ACT.Exp, scale=-1.0).then_inc(g_exp, 1)

            for g in range(4):
                if g:
                    filled(sc, ("mix_p", g - 1))
                filled(sc, ("pool_p", g))
                read(sc.activation(dT[:, 0:SEQ], ps(("pool_p", g))[:, :], ACT.Copy), ("pool_p", g))
                filled(sc, ("mix_p", g))
                read(sc.activation(amT[:, 4 + g, 0:SEQ], ps(("mix_p", g))[:, :], ACT.Copy, scale=cols[:, 1 + g:2 + g]), ("mix_p", g))

            for i in range(TILES):
                n = ROWS[i]
                dst = qT[:, :, i * P:(i + 1) * P] if i < 4 else qTs[:, :, :]
                read(copy4(("qT", i), dst, n), ("qT", i))

            units = prompt_units()

            def p_exp(u):
                b, i, h = units[u]
                n = (i + 1) * P
                d = 40 + 8 * (i % 2) + place(h)
                taken(sc, ("p_s", u))
                if h == 0 and 4 * b + i >= 2:
                    sc.wait_ge(p_a, 4 * b + i - 1)
                z = pS[u % 4][:, 0:n]
                sc.activation(z, z, ACT.Exp, bias=st[:, 32 + u % 4:33 + u % 4], scale=-1.0, accum_out=st[:, d:d + 1]).then_inc(p_e, 1)

            for u in range(AHEAD):
                p_exp(u)
            for u in range(len(units)):
                if u + AHEAD < len(units):
                    p_exp(u + AHEAD)
                if u % 2 == 0:
                    n = (units[u][1] + 1) * P
                    filled(sc, ("p_T", u))
                    read(sc.activation(pT[u % 2][:, 0:n], ps(("p_T", u))[:, 0:n], ACT.Copy), ("p_T", u))
                if u == AT_NORM:
                    sc.wait_ge(kc_ms, 1)
                    sc.activation(ktmp, ktmp, ACT.Sqrt).then_inc(kc_rt, 1)
                if u == AT_LOGITS:
                    sc.wait_ge(cz, 1)
                    sc.activation(ec, zc, ACT.Exp).then_inc(ce, 1)
                    sc.wait_ge(pcz_ready, 1)
                    sc.activation(pcm, pcz, ACT.Exp).then_inc(pce, 1)
                if u == AT_VALUES:
                    filled(sc, "vcT")
                    sc.activation(VC[:, 0:2, :], ps("vcT")[:, 0:2 * P].rearrange("p (a b) -> p a b", a=2), ACT.Copy)
                    read(sc.activation(VC[0:NBP, 2, :], ps("vcT")[0:NBP, 2 * P:3 * P], ACT.Copy), "vcT")
                if u == AT_TURNED:
                    filled(sc, "pc_T")
                    read(sc.activation(pcT[0:64, :, :], ps("pc_T")[0:64, :].rearrange("p (i t) -> p i t", t=P), ACT.Copy), "pc_T")

            for t in range(PAIRS + 1):
                if t < PAIRS:
                    for c in range(4):
                        kb_free(sc, t, 2 * c)
                        filled(sc, ("slc_k", t, c, 0))
                        read(sc.activation(kb[(10 * t + 2 * c) % 4], ps(("slc_k", t, c, 0))[:, :], ACT.Copy), ("slc_k", t, c, 0))
                    kb_free(sc, t, 8)
                    filled(sc, ("win_k", t, 0))
                    read(sc.activation(kb[(10 * t + 8) % 4], ps(("win_k", t, 0))[:, :], ACT.Copy), ("win_k", t, 0))
                    d = 72 + 2 * (t % 2)
                    sc.wait_ge(s_z, t + 1)
                    sc.activation(S[t % 2], S[t % 2], ACT.Exp, bias=st[:, 80:81], scale=-1.0, accum_out=st[:, d:d + 1]).then_inc(s_e, 1)
                    sc.wait_ge(w_z, t + 1)
                    sc.activation(SN[t % 2], SN[t % 2], ACT.Exp, bias=st[:, 81:82], scale=-1.0, accum_out=st[:, d + 1:d + 2]).then_inc(w_e, 1)
                if t == 1:
                    filled(sc, "cmp_T")
                    read(sc.activation(cT, ps("cmp_T")[:, :].rearrange("p (a b) -> p a b", b=P), ACT.Copy), "cmp_T")
                    filled(sc, "cmp_o")
                    filled(sc, ("pc_o", 3))
                    read(sc.activation(co, ps("cmp_o")[:, :], ACT.Copy), "cmp_o")
                if t == PAIRS:
                    for i in (0, 2):
                        read(copy4(("aT", i), amT[:, 0:4, i * P:(i + 1) * P], P), ("aT", i))
                if t:
                    p = t - 1
                    if p:
                        filled(sc, ("slc_o", p - 1))
                        filled(sc, ("win_o", p - 1))
                    for c in (0, 2):
                        filled(sc, ("slc_T", p, c))
                        read(sc.activation(PT[:, c, :], ps(("slc_T", p, c))[:, :], ACT.Copy), ("slc_T", p, c))
                    filled(sc, ("slc_T", p, 4))
                    read(sc.activation(PT[0:NS, 4, 0:P], ps(("slc_T", p, 4))[0:NS, 0:P], ACT.Copy), ("slc_T", p, 4))
                    filled(sc, ("win_T", p, 1))
                    read(sc.activation(PTw[0:NS, 1, 0:P], ps(("win_T", p, 1))[0:NS, 0:P], ACT.Copy), ("win_T", p, 1))
                    if p:
                        sc.wait_ge(a_ready, p)
                    filled(sc, ("bcast", p))
                    read(sc.activation(bcs, ps(("bcast", p))[:, 0:3 * P], ACT.Copy), ("bcast", p))

            for i in range(TILES):
                n = ROWS[i]
                sc.wait_ge(h_ready, i + 1)
                if i:
                    sc.wait_ge(h_sq, i)
                sc.activation(view(pflat, 0, D)[0:n, :], xh[0:n, i, :], ACT.Square, accum_out=st[0:n, 8 + i:9 + i]).then_inc(h_sq, 1)
                sc.wait_ge(h_ms, i + 1)
                sc.activation(st[0:n, 16 + i:17 + i], st[0:n, 24 + i:25 + i], ACT.Sqrt).then_inc(h_rt, 1)
                sc.wait_ge(n_ready, i + 1)
                sc.dma_start(scratch["n2"][i * P:i * P + n, :], n2[i % 2][0:n, :]).then_inc(n_stored[i % 2], 16)
            sc.wait_ge(r_exp_in, 1)
            sc.activation(r4[1], r4[0], ACT.Exp)
            sc.activation(r1[7], r1[6], ACT.Exp).then_inc(r_exp, 1)

            BG, BU, (BX, _), BH, BY = EXPERT_BANKS

            def gathered(n):
                sc.wait_ge(xt_full, n)
                sc.activation(xgT[:, 0:4, :], BX[:, :].rearrange("p (k t) -> p k t", k=4), ACT.Copy).then_inc(xgt_ready, 1)

            def expert(it, s, last_one):
                e = it * 2 + s
                sc.wait_ge(product, e * 3 + 1)
                sc.wait_ge(he_ready, 2 * e)
                sc.activation(sg, BG[:, :], ACT.Silu).then_inc(sg_ready, 1)
                if not last_one:
                    gathered(e + 2)
                sc.wait_ge(st_y, e * 16)
                for half in range(2):
                    sc.wait_ge((down_half, product)[half], (e + 1, e * 3 + 3)[half])
                    sc.activation(ytok[:, half * 512:(half + 1) * 512], BY[half][:, :], ACT.Copy).then_inc(y_taken, 1)
                if last_one:
                    return
                sc.wait_ge(y_taken, e * 2 + 2)
                sc.dma_start(scratch["y"].rearrange("(r e) d -> r e d", e=NE - 1)[0:P, bass.ds(e, 1), :], ytok.rearrange("p (a d) -> p a d", a=1)).then_inc(st_y, 16)

            more = crowded(sc)
            gathered(1)
            with sc.Fori(0, NE // 2 - 1) as it:
                for s in range(2):
                    expert(it, s, False)
            for s in range(2):
                expert(NE // 2 - 1, s, s == 1)

            with sc.If(more):
                with sc.Fori(0, NE) as e:
                    with sc.Fori(0, MORE) as t:
                        n = e * MORE + t
                        sc.wait_ge(o_x, n + 1)
                        sc.activation(xgT[:, 0:4, :], BX[:, :].rearrange("p (k t) -> p k t", k=4), ACT.Copy).then_inc(o_xc, 1)
                        sc.wait_ge(o_gu, n + 1)
                        sc.activation(sg, BG[:, :], ACT.Silu).then_inc(o_sg, 1)
                        sc.wait_ge(o_p, n + 1)
                        sc.wait_ge(o_st, n * 16)
                        for half in range(2):
                            sc.activation(more_rows[:, half * 512:(half + 1) * 512], BY[half][:, :], ACT.Copy).then_inc(o_y, 1)
                        sc.wait_ge(o_y, n * 2 + 2)
                        dst = scratch["more_y"].rearrange("(r e) d -> r e d", e=NE)[bass.ds(t * P, P), bass.ds(e, 1), :]
                        sc.dma_start(dst, more_rows.rearrange("p (a d) -> p a d", a=1)).then_inc(o_st, 16)

        @block.vector
        def _(ve):
            steps = [0]

            def link(ins):
                steps[0] += 1
                ins.then_inc(dve, 1)
                ve.wait_ge(dve, steps[0])

            def bc(ap, n):
                return spread(ap.rearrange("p (a b) -> p a b", b=1), 2, n)

            def gained(i):
                n = ROWS[i]
                for half in range(2):
                    filled(ve, ("xT", i, half))
                    src = ps(("xT", i, half))[:, :].rearrange("p (k t) -> p k t", k=4)[:, :, 0:n]
                    read(ve.tensor_tensor(xnT[:, 4 * half:4 * half + 4, i * P:i * P + n], src, bc(g1[:, 4 * half:4 * half + 4], n),
                                          ALU.mult), ("xT", i, half))

            ve.wait_ge(ld_c0, 32)
            gained(0)
            gained(1)
            ve.wait_ge(act_sq, TILES)
            ve.tensor_scalar(st[:, 8:13], st[:, 0:5], 1.0 / D, EPS, ALU.mult, ALU.add).then_inc(ms_ready, 1)
            ve.wait_ge(rt_ready, 1)
            ve.reciprocal(rstd[:, 0, :], st[:, 16:21]).then_inc(rstd_ready, 1)
            ve.wait_ge(rstd_ready, 1)
            for c in range(4):
                for i in range(TILES):
                    n = ROWS[i]
                    if c == 0 and 1 <= i < TILES - 1:
                        gained(i + 1)
                    if (c * TILES + i) % 2 == 1:
                        filled(ve, ("in", c, i))
                        read(ve.tensor_scalar(proj[0:n, i, c * WC:(c + 1) * WC], ps(("in", c, i))[0:n, 0:WC], rstd[0:n, 0, i:i + 1],
                                              None, ALU.mult), ("in", c, i))
                if c == 2:
                    ve.wait_ge(ld_c1, N_C1)
                    link(ve.tensor_scalar(gains[:, 0, :], gains[:, 0, :], HD ** -0.5, None, ALU.mult))
                    ve.wait_ge(heads_sq, 3)
                    ve.tensor_reduce(nrm[:, :, 0:8], qsq.rearrange("p t (h d) -> p t h d", d=HD), X, ALU.add)
                    link(ve.tensor_reduce(nrm[:, :, 8:12], ksq.rearrange("p t (h d) -> p t h d", d=HD), X, ALU.add))
                    ve.tensor_scalar(nrm[:, :, :], nrm[:, :, :], 1.0 / HD, EPS, ALU.mult, ALU.add).then_inc(heads_ms, 1)
                    ve.wait_ge(heads_rt, 1)
                    ve.reciprocal(nrm[:, :, :], nrm[:, :, :]).then_inc(heads_rt, 1)
                    ve.wait_ge(heads_rt, 2)
                    inv = spread(table["inv_slope"].rearrange("p (a h) -> p a h", a=1), 1, 4)
                    link(ve.tensor_tensor(nrm[:, 0:4, 0:8], nrm[:, 0:4, 0:8], inv, ALU.mult))
                    for i in range(TILES):
                        qh = proj[:, i, 0:512].rearrange("p (h d) -> p h d", d=HD)
                        link(ve.tensor_tensor(qh, qh, bc(nrm[:, i, 0:8], HD), ALU.mult))
                    gq = spread(spread(gains[:, 0, :].rearrange("p (a b d) -> p a b d", a=1, b=1), 1, KVH), 2, G)
                    for i in range(TILES):
                        qh = proj[:, i, 0:512].rearrange("p (h d) -> p h d", d=HD).rearrange("p (k j) d -> p k j d", j=G)
                        o = qn[:, i, :].rearrange("p (j k d) -> p k j d", k=KVH, j=G)
                        last = ve.tensor_tensor(o, qh, gq, ALU.mult)
                    last.then_inc(q_ready, 1)
                    ve.wait_ge(g_exp, 1)
                    link(ve.tensor_scalar(gate[:, :, :], gate[:, :, :], 1.0, None, ALU.add))
                    ve.reciprocal(gate[:, :, :], gate[:, :, :]).then_inc(g_ready, 1)

            for g in range(4):
                if g:
                    filled(ve, ("mix_s", g - 1))
                filled(ve, ("pool_s", g))
                read(ve.tensor_copy(dT[:, SEQ:NT], ps(("pool_s", g))[:, 0:NS]), ("pool_s", g))
                filled(ve, ("mix_s", g))
                read(ve.tensor_scalar(amT[:, 4 + g, SEQ:NT], ps(("mix_s", g))[:, 0:NS], cols[:, 1 + g:2 + g], None, ALU.mult),
                     ("mix_s", g))

            def raw(r, dst, col):
                half = r % 2
                filled(ve, ("cmp", r))
                n = (P, 136)[half]
                if half == 0:
                    link(ve.tensor_copy(posc[:, col:col + 1], ps(("cmp", r))[:, P:P + 1]))
                read(ve.tensor_scalar(dst[:, half * P:half * P + n], ps(("cmp", r))[:, 0:n], posc[:, col:col + 1], None, ALU.add),
                     ("cmp", r))

            for i in range(TILES):
                n = ROWS[i]
                filled(ve, ("kT", i))
                ve.tensor_copy(kTs[:, i * P:i * P + n], ps(("kT", i))[:, 0:n])
                read(ve.tensor_copy(kTw[:, i * P:i * P + n], ps(("kT", i))[:, P:P + n]), ("kT", i))
            filled(ve, "gate_rows")
            tmp24 = st[:, 0:96].rearrange("p (t c) -> p t c", c=24)
            hm = spread(table["head"].rearrange("p (a c) -> p a c", a=1), 1, PAIRS)
            ve.wait_ge(dve, steps[0])
            read(ve.tensor_tensor(tmp24, ps("gate_rows")[:, 0:96].rearrange("p (t c) -> p t c", c=24), hm, ALU.mult), "gate_rows")
            taken(ve, "gate_rows")
            link(ve.tensor_reduce(grow[:, :, :], tmp24.rearrange("p t (h b) -> p t b h", b=3), X, ALU.add))
            def gates_of(i, b):
                return gate[:, i, :].rearrange("p (k j b) -> p j k b", k=KVH, j=G)[:, :, :, b]

            def heads(ap):
                return ap.rearrange("p (j k d) -> p j k d", j=G, k=KVH)

            def bc3(ap):
                return spread(ap.rearrange("p j (k a) -> p j k a", a=1), 3, HD)

            def turned(src, dst, signal):
                s3 = src.rearrange("p (n h) -> p n h", h=2)
                d3 = dst.rearrange("p (n r) -> p n r", r=2)
                for h in range(2):
                    for par in range(2):
                        ve.tensor_copy(d3[64 * h:64 * h + 64, :, par], s3[64 * par:64 * par + 64, :, h]).then_inc(signal, 1)

            pz = pcz.rearrange("p i (h n) -> p (i h) n", n=NBP)
            pflt = pcz.rearrange("p i c -> p (i c)")
            pmax, psum = st[:, 56:88], st[:, 56:88]

            def beside(u):
                if u == AT_NORM:
                    filled(ve, "key_norm")
                    read(ve.tensor_scalar(ktmp, ps("key_norm")[:, 0:264], 1.0 / HD, EPS, ALU.mult, ALU.add), "key_norm")
                    taken(ve, "key_norm")
                    ve.sem_inc(kc_ms, 1)
                if u == AT_KEYS:
                    ve.wait_ge(kc_rt, 1)
                    link(ve.reciprocal(ktmp, ktmp))
                    link(ve.scalar_tensor_tensor(kcr, kcr, cols[:, 0:1], ktmp, ALU.mult, ALU.mult))
                    ve.memset(kpb[:, :], 0.0)
                    turned(kcr, KCT[:, :], kct_ready)
                    ve.wait_ge(kct_ready, 4)
                    for h in range(KVH):
                        ve.tensor_copy(kpb[64 * h:64 * h + 64, h * NBP:(h + 1) * NBP], KCT[64 * h:64 * h + 64, DB * NBS:NBALL])\
                            .then_inc(kct_ready, 1)
                if u == AT_LOGITS:
                    filled(ve, "cmp_s")
                    bcb = spread(table["bias_c"].rearrange("p (a n) -> p a n", a=1), 1, PAIRS)
                    read(ve.tensor_tensor(zc, ps("cmp_s")[:, 0:P].rearrange("p (t n) -> p t n", n=NBS), bcb, ALU.add), "cmp_s")
                    taken(ve, "cmp_s")
                    link(ve.tensor_reduce(st[:, 0:4], zc, X, ALU.max))
                    ve.tensor_tensor(zc, zc, bc(st[:, 0:4], NBS), ALU.subtract).then_inc(cz, 1)
                    filled(ve, "pc_s")
                    read(ve.tensor_tensor(pflt, ps("pc_s")[:, 0:4 * H * NBP], table["pc_bias"], ALU.add), "pc_s")
                    taken(ve, "pc_s")
                    link(ve.tensor_reduce(pmax, pz, X, ALU.max))
                    link(ve.tensor_tensor(pz, pz, bc(pmax, NBP), ALU.subtract))
                    slopes = spread(spread(table["slope"].rearrange("p (a h b) -> p a h b", a=1, b=1), 1, 4), 3, NBP)
                    pz4 = pcz.rearrange("p i (h n) -> p i h n", n=NBP)
                    ve.tensor_tensor(pz4, pz4, slopes, ALU.mult).then_inc(pcz_ready, 1)
                if u == AT_PROBS:
                    ve.wait_ge(ce, 1)
                    link(ve.scalar_tensor_tensor(zc, ec, TINY, ec, ALU.is_ge, ALU.mult))
                    link(ve.tensor_reduce(st[:, 4:8], zc, X, ALU.add))
                    link(ve.reciprocal(st[:, 8:12], st[:, 4:8]))
                    link(ve.tensor_tensor(ec, zc, bc(st[:, 8:12], NBS), ALU.mult))
                    ve.scalar_tensor_tensor(zc, ec, TINY, ec, ALU.is_ge, ALU.mult).then_inc(cp, 1)
                    ve.wait_ge(pce, 1)
                    link(ve.scalar_tensor_tensor(pflt, table["pc_bias"], NEG / 10, pcm.rearrange("p i c -> p (i c)"), ALU.is_gt, ALU.mult))
                    link(ve.tensor_reduce(psum, pz, X, ALU.add))
                    link(ve.scalar_tensor_tensor(psum, psum, 0.0, psum, ALU.is_equal, ALU.add))
                    link(ve.reciprocal(psum, psum))
                    ve.tensor_tensor(pz, pz, bc(psum, NBP), ALU.mult).then_inc(pcp, 1)
                if u == AT_SUM:
                    filled(ve, "cmp_sum")
                    ve.wait_ge(z_clear, 1)
                    read(ve.tensor_copy(score[:, :, 1:NBS], ps("cmp_sum")[:, 0:P].rearrange("p (t n) -> p t n", n=NBS)[:, :, 1:NBS]), "cmp_sum")
                    taken(ve, "cmp_sum")
                if AT_MASK <= u < AT_MASK + PAIRS:
                    t = u - AT_MASK
                    for k in range(2):
                        link(ve.max(st[:, 64:72], score[:, t, :]))
                        link(ve.match_replace(score[:, t, :], st[:, 64:72], score[:, t, :], -2.0))
                    if t == PAIRS - 1:
                        link(ve.tensor_scalar(maskb[:, :, :], score, -1.5, NEG, ALU.is_gt, ALU.mult))

            units = prompt_units()
            ve.wait_ge(g_ready, 1)
            ve.wait_ge(ld_dist, 16)

            def logits_of(u):
                b, i, h = units[u]
                n = (i + 1) * P
                if u >= 4:
                    filled(ve, ("p_T", u - 4))
                filled(ve, ("p_s", u))
                read(ve.tensor_tensor_reduce(pS[u % 4][:, 0:n], ps(("p_s", u))[:, 0:n], dist[:, SEQ - n:SEQ], -SLOPES[h], 3e38, ALU.add,
                                             ALU.min, st[:, 32 + u % 4:33 + u % 4]), ("p_s", u))

            def add_heads(b, i):
                d = 40 + 8 * (i % 2)
                filled(ve, ("p_o", b, i))
                link(ve.reciprocal(st[:, d:d + 8], st[:, d:d + 8]))
                w = st[:, d:d + 8].rearrange("p (j k) -> p j k", k=KVH)
                link(ve.tensor_tensor(w, w, gates_of(i, b + 1), ALU.mult))
                o = a_tok[:, i, :] if b == 0 else tmpo
                read(ve.tensor_tensor(heads(o), heads(ps(("p_o", b, i))[:, :]), bc3(w), ALU.mult), ("p_o", b, i))
                taken(ve, ("p_o", b, i))
                if b == 0:
                    ve.sem_inc(p_a, 1)
                    return
                ve.tensor_tensor(a_tok[:, i, :], a_tok[:, i, :], tmpo, ALU.add).then_inc(p_a, 1)
                ve.wait_ge(p_a, 4 * b + i + 1)

            for u in range(AHEAD):
                logits_of(u)
            for u in range(len(units) + 1):
                if u + AHEAD < len(units):
                    logits_of(u + AHEAD)
                if u < len(units) and u % 2:
                    n = (units[u][1] + 1) * P
                    filled(ve, ("p_T", u))
                    read(ve.tensor_copy(pT[u % 2][:, 0:n], ps(("p_T", u))[:, 0:n]), ("p_T", u))
                if u and units[u - 1][2] == H - 1:
                    add_heads(units[u - 1][0], units[u - 1][1])
                for r, (first, count) in enumerate(CMP_UNITS):
                    if u == first + count:
                        raw(r, (kcr, kcr, vcr, vcr)[r], r // 2)
                        taken(ve, ("cmp", r))
                        if r == 1:
                            ve.tensor_tensor(ktmp, kcr, kcr, ALU.mult).then_inc(kc_sq, 1)
                        if r == 3:
                            turned(vcr, vct, vct_ready)
                beside(u)

            for t in range(PAIRS + 1):
                if t < PAIRS:
                    Sb, Wb = S[t % 2], SN[t % 2]
                    if t == 1:
                        ve.wait_ge(z_clear, 3)
                        ve.wait_ge(cp, 1)
                        for s in range(2):
                            for tp in range(2):
                                c0 = (2 * tp + s) * NBS
                                last = ve.tensor_copy(pw[64 * s:64 * s + 64, tp::2, c0:c0 + NBS], zc[64 * s:64 * s + 64, tp::2, :])
                        last.then_inc(cp, 1)
                    if t >= 2:
                        filled(ve, ("slc_T", t - 2, 4))
                        filled(ve, ("win_T", t - 2, 1))

                    def chunk(c):
                        name = ("slc_s", t, c)
                        if t == 0 and c == 0:
                            ve.wait_ge(ld_c3, 16)
                        filled(ve, name)
                        z = Sb[:, c * 512:(c + 1) * 512]
                        read(ve.tensor_tensor(z, ps(name)[:, :], slc_bias[:, c * 512:(c + 1) * 512], ALU.add), name)
                        taken(ve, name)
                        z3 = z.rearrange("p (n l) -> p n l", l=64)
                        ve.tensor_tensor_reduce(z3, z3, bc(maskb[:, t, 8 * c:8 * c + 8], 64), -1.0, 3e38, ALU.add, ALU.min,
                                                st[:, 84 + c:85 + c])

                    for c in range(5):
                        if c < 4:
                            kb_free(ve, t, 2 * c + 1)
                            filled(ve, ("slc_k", t, c, 1))
                            read(ve.tensor_copy(kb[(10 * t + 2 * c + 1) % 4], ps(("slc_k", t, c, 1))[:, :]), ("slc_k", t, c, 1))
                        if c:
                            chunk(c - 1)
                    nb = table["new_bias"][:, t * NS:(t + 1) * NS]
                    filled(ve, ("new_s", t))
                    read(ve.tensor_tensor_reduce(Sb[:, PAST:SW], ps(("new_s", t))[:, 0:NS], nb, -1.0, 3e38, ALU.add, ALU.min,
                                                 st[:, 88:89]), ("new_s", t))
                    taken(ve, ("new_s", t))
                    if t:
                        ve.wait_ge(s_e, t)
                        ve.wait_ge(w_e, t)
                    ve.tensor_reduce(st[:, 80:81], st[:, 84:89], X, ALU.min).then_inc(s_z, 1)
                    kb_free(ve, t, 9)
                    filled(ve, ("win_k", t, 1))
                    read(ve.tensor_copy(kb[(10 * t + 9) % 4], ps(("win_k", t, 1))[:, :]), ("win_k", t, 1))
                    filled(ve, ("win_s", t))
                    read(ve.tensor_tensor_reduce(Wb[:, 0:512], ps(("win_s", t))[:, :], table["win_bias"], -1.0, 3e38, ALU.add,
                                                 ALU.min, st[:, 90:91]), ("win_s", t))
                    filled(ve, ("neww_s", t))
                    read(ve.tensor_tensor_reduce(Wb[:, 512:WW], ps(("neww_s", t))[:, 0:NS], nb, -1.0, 3e38, ALU.add, ALU.min,
                                                 st[:, 91:92]), ("neww_s", t))
                    taken(ve, ("neww_s", t))
                    ve.tensor_reduce(st[:, 81:82], st[:, 90:92], X, ALU.min).then_inc(w_z, 1)
                if t == 1:
                    for i in range(4):
                        filled(ve, ("pc_o", i))
                        read(ve.tensor_tensor(heads(tmpc), heads(ps(("pc_o", i))[:, :]), bc3(gates_of(i, 0)), ALU.mult), ("pc_o", i))
                        taken(ve, ("pc_o", i))
                        ve.tensor_tensor(a_tok[:, i, :], a_tok[:, i, :], tmpc, ALU.add).then_inc(p_a, 1)
                        ve.wait_ge(p_a, 8 + i + 1)
                if t == PAIRS:
                    for i in (1, 3):
                        filled(ve, ("aT", i))
                        src = ps(("aT", i))[:, :].rearrange("p (k t) -> p k t", k=4)
                        read(ve.tensor_copy(amT[:, 0:4, i * P:(i + 1) * P], src), ("aT", i))
                if t:
                    p = t - 1
                    if p:
                        filled(ve, ("slc_o", p - 1))
                        filled(ve, ("win_o", p - 1))
                    for c in (1, 3):
                        filled(ve, ("slc_T", p, c))
                        read(ve.tensor_copy(PT[:, c, :], ps(("slc_T", p, c))[:, :]), ("slc_T", p, c))
                    filled(ve, ("win_T", p, 0))
                    read(ve.tensor_copy(PTw[:, 0, :], ps(("win_T", p, 0))[:, :]), ("win_T", p, 0))
                    d = 72 + 2 * (p % 2)
                    ve.wait_ge(w_e, p + 1)
                    link(ve.reciprocal(st[:, d:d + 2], st[:, d:d + 2]))
                    if p:
                        filled(ve, ("bcast", p - 1))
                    ve.tensor_scalar(diag[:, 0:P], ident, grow[:, p, 0:1], None, ALU.mult)
                    ve.tensor_scalar(diag[:, P:2 * P], ident, grow[:, p, 1:2], st[:, d:d + 1], ALU.mult, ALU.mult)
                    ve.tensor_scalar(diag[:, 2 * P:3 * P], ident, grow[:, p, 2:3], st[:, d + 1:d + 2], ALU.mult, ALU.mult)\
                        .then_inc(diag_ready, 1)
                    taken(ve, ("bcast", p))
                    taken(ve, "cmp_o")
                    ve.tensor_tensor(t1, co[:, p * P:(p + 1) * P], bcs[:, 0:P], ALU.mult)
                    filled(ve, ("slc_o", p))
                    read(ve.tensor_tensor(t2, ps(("slc_o", p))[:, 0:P], bcs[:, P:2 * P], ALU.mult), ("slc_o", p))
                    taken(ve, ("slc_o", p))
                    link(ve.tensor_tensor(t1, t1, t2, ALU.add))
                    filled(ve, ("win_o", p))
                    read(ve.tensor_tensor(t2, ps(("win_o", p))[:, 0:P], bcs[:, 2 * P:3 * P], ALU.mult), ("win_o", p))
                    taken(ve, ("win_o", p))
                    for h in range(KVH):
                        q = slice(64 * h, 64 * h + 64)
                        o = amT[q, 0:4, SEQ + 16 * p:SEQ + 16 * p + 16].rearrange("p g (s q) -> p s g q", s=2)
                        i0, i1 = (x[q, :].rearrange("p (s k g q) -> p k s g q", s=2, k=2, g=4)[:, h] for x in (t1, t2))
                        last = ve.tensor_tensor(o, i0, i1, ALU.add)
                    last.then_inc(a_ready, 1)
                    ve.wait_ge(a_ready, p + 1)

            ve.wait_ge(ld_xr, 16 * TILES)
            link(ve.memset(logits, 0.0))
            for i in range(TILES):
                n = ROWS[i]
                for half in range(2):
                    filled(ve, ("h", i, half))
                    x = xh[0:n, i, half * 512:(half + 1) * 512]
                    read(ve.tensor_tensor(x, ps(("h", i, half))[0:n, :], x, ALU.add), ("h", i, half))
                taken(ve, ("h", i, 1))
                ve.sem_inc(h_ready, 1)
                def rows_of_router():
                    for half in range(2):
                        filled(ve, ("nT", i, half))
                        src = ps(("nT", i, half))[:, :].rearrange("p (k t) -> p k t", k=4)[:, :, 0:n]
                        read(ve.tensor_tensor(n2T[:, 4 * half:4 * half + 4, 0:n], src, bc(g2[:, 4 * half:4 * half + 4], n), ALU.mult),
                             ("nT", i, half))

                def normed_rows():
                    ve.wait_ge(h_sq, i + 1)
                    ve.tensor_scalar(st[0:n, 24 + i:25 + i], st[0:n, 8 + i:9 + i], 1.0 / D, EPS, ALU.mult, ALU.add).then_inc(h_ms, 1)
                    ve.wait_ge(h_rt, i + 1)
                    link(ve.reciprocal(rstd[0:n, 1, i:i + 1], st[0:n, 16 + i:17 + i]))
                    if i == 0:
                        ve.wait_ge(ld_g2, 16)
                    if i >= 2:
                        ve.wait_ge(n_stored[i % 2], 16 * (i // 2))
                    ve.scalar_tensor_tensor(n2[i % 2][0:n, :], xh[0:n, i, :], rstd[0:n, 1, i:i + 1], g2b[0:n, :], ALU.mult, ALU.mult)\
                        .then_inc(n_ready, 1)

                for stage in ((normed_rows, rows_of_router) if i < TILES - 1 else (rows_of_router, normed_rows)):
                    stage()
                filled(ve, ("logit", i))
                read(ve.tensor_scalar(logits[0:n, i, :], ps(("logit", i))[0:n, 0:NG + NE], rstd[0:n, 1, i:i + 1], None, ALU.mult),
                     ("logit", i))
            for i in range(TILES):
                taken(ve, ("logit", i))

            lg, le = logits[:, :, 0:NG], logits[:, :, NG:NG + NE]
            over4 = lambda x: bc(x, NG)
            over16 = lambda x: bc(x, NE)
            wide = lambda name, n: spread(table[name].rearrange("p (a n) -> p a n", a=1), 1, TILES)
            link(ve.tensor_reduce(r1[0], lg, X, ALU.max))
            link(ve.tensor_tensor(r4[0], lg, over4(r1[0]), ALU.subtract))
            link(ve.tensor_tensor(r4[2], lg, over4(r1[0]), ALU.is_equal))
            link(ve.tensor_tensor(r4[2], r4[2], wide("prio4", NG), ALU.mult))
            link(ve.tensor_reduce(r1[3], r4[2], X, ALU.max))
            link(ve.tensor_tensor(r4[3], r4[2], over4(r1[3]), ALU.is_equal))
            link(ve.tensor_scalar(r4[2], r4[3], -NEG, NEG, ALU.mult, ALU.add))
            ge = lambda x: x.rearrange("p t (g e) -> p t g e", g=NG)
            pen = spread(r4[2].rearrange("p t (g a) -> p t g a", a=1), 3, EPG)
            link(ve.tensor_tensor(ge(r16[0]), ge(le), pen, ALU.add))

            def first_max(z, m, oh):
                link(ve.tensor_reduce(m, z, X, ALU.max))
                link(ve.tensor_tensor(oh, z, over16(m), ALU.is_equal))
                link(ve.tensor_tensor(oh, oh, wide("prio", NE), ALU.mult))
                link(ve.tensor_reduce(r1[5], oh, X, ALU.max))
                link(ve.tensor_tensor(oh, oh, over16(r1[5]), ALU.is_equal))

            flat = lambda x: x.rearrange("p a b -> p (a b)")
            first_max(r16[0], r1[4], r16[2])
            link(ve.scalar_tensor_tensor(flat(r16[1]), flat(r16[2]), NEG, flat(r16[0]), ALU.mult, ALU.add))
            first_max(r16[1], r1[6], r16[3])
            hot = view(kTs, 100 + 2 * 80, 2, TILES * NE).rearrange("p k (i e) -> p k i e", e=NE)
            link(ve.memset(chosen[:, TILES, :], 0.0))
            link(ve.tensor_tensor(chosen[:, 0:TILES, :], r16[2], r16[3], ALU.add))
            ve.tensor_tensor(chosen[:, 0:TILES, :], chosen[:, 0:TILES, :], over16(table["valid"]), ALU.mult).then_inc(oh_ready, 1)
            ve.tensor_tensor(r1[6], r1[6], r1[4], ALU.subtract).then_inc(r_exp_in, 1)
            over_k = lambda x: spread(x.rearrange("p (a i) e -> p a i e", a=1), 1, 2)
            link(ve.tensor_tensor(hot, hot, over_k(over16(table["valid"])), ALU.mult))
            for k in range(2):
                ve.tensor_tensor(tok_at[:, k], hot[:, k], over16(table["token"]), ALU.mult)
            link(ve.tensor_tensor(pair16, hot, over_k(wide("expert", NE)), ALU.mult))
            link(ve.tensor_reduce(ex, pair16, X, ALU.add))
            filled(ve, "prefix")
            link(ve.tensor_tensor(pair16, hot, over_k(ps("prefix")[:, 0:TILES * NE].rearrange("p (i e) -> p i e", e=NE)), ALU.mult))
            link(ve.tensor_reduce(pos, pair16, X, ALU.add))
            for i in range(TILES):
                for k in range(2):
                    ve.tensor_scalar(picks[:, 2 * i + k, :], table["row"], pos[:, k, i:i + 1], None, ALU.is_equal).then_inc(picks_ready, 1)
            read(ve.tensor_reduce(r1[5][:, 0:1], ps("prefix")[:, TILES * NE:(TILES + 1) * NE], X, ALU.max), "prefix")
            taken(ve, "prefix")
            link(ve.tensor_copy(nmax[:, :], r1[5][0:1, 0:1]))
            ve.sem_inc(counted, 1)
            filled(ve, "idx")
            link(ve.tensor_copy(last_token, ps("idx")[:, NE - 1:NE]))
            read(ve.tensor_copy(idx[:, :], ps("idx")[:, 0:NE]), "idx")
            taken(ve, "idx")
            ve.sem_inc(idx_ready, 1)
            link(ve.scalar_tensor_tensor(slot_f, pos, float(NE), ex, ALU.mult, ALU.add))
            link(ve.tensor_copy(slot_i[:, :, :], slot_f))
            link(ve.tensor_scalar(is_last, ex, NE - 1.0, None, ALU.is_equal))
            link(ve.scalar_tensor_tensor(over_f, pos, NE - 1.0, ex, ALU.mult, ALU.add))
            link(ve.tensor_tensor(over_f, over_f, is_last, ALU.subtract))
            link(ve.tensor_scalar(row_i[:, 0], over_f, EARLY - 1.0, None, ALU.min))
            link(ve.tensor_scalar(over_f, slot_f, -float(FIRST), None, ALU.add))
            link(ve.tensor_scalar(row_i[:, 1], over_f, 0.0, None, ALU.max))
            link(ve.tensor_scalar(inside[:, :, :], over_f, 0.0, None, ALU.is_lt))
            ve.sem_inc(slots_ready, 1)
            ve.wait_ge(r_exp, 1)
            link(ve.tensor_reduce(r1[1], r4[1], X, ALU.add))
            link(ve.reciprocal(r1[2], r1[1]))
            link(ve.tensor_scalar(r1[3], r1[7], 1.0, None, ALU.add))
            link(ve.reciprocal(r1[5], r1[3]))
            link(ve.tensor_tensor(gates2[:, 0, :], r1[2], r1[5], ALU.mult))
            link(ve.tensor_tensor(gates2[:, 1, :], gates2[:, 0, :], r1[7], ALU.mult))
            link(ve.tensor_tensor(last_hot, gates2[:, :, :], is_last, ALU.mult))
            ve.sem_inc(last_in, 1)
            link(ve.tensor_tensor(gates1[:, :, :], gates2[:, :, :], inside[:, :, :], ALU.mult))
            link(ve.tensor_tensor(gates2[:, :, :], gates2[:, :, :], gates1[:, :, :], ALU.subtract))
            link(ve.tensor_scalar(is_last, is_last, -1.0, 1.0, ALU.mult, ALU.add))
            link(ve.tensor_tensor(gates1[:, :, :], gates1[:, :, :], is_last, ALU.mult))
            link(ve.tensor_scalar(last_at, table["tile"], -1.0, last_token, ALU.mult, ALU.add))

            BG, BU, (_, BX), BH, BY = EXPERT_BANKS

            def gathered(n):
                ve.wait_ge(xt_full, n)
                ve.tensor_copy(xgT[:, 4:8, :], BX[:, :].rearrange("p (k t) -> p k t", k=4)).then_inc(xgt_ready, 1)

            def expert(it, s, last_one):
                e = it * 2 + s
                ve.wait_ge(sg_ready, e + 1)
                ve.wait_ge(ht_full, 2 * e)
                for half in range(2):
                    ve.wait_ge((up_half, product)[half], (e + 1, 3 * e + 2)[half])
                    f = slice(half * HALF, (half + 1) * HALF)
                    ve.tensor_tensor(he[:, f], sg[:, f], BU[half][:, 0:HALF], ALU.mult).then_inc(he_ready, 1)
                ve.wait_ge(product, e * 3)
                for half in range(2):
                    ve.wait_ge(ht_full, 2 * e + half + 1)
                    k = slice(2 * half, 2 * half + 2)
                    ve.tensor_copy(heT[:, k, :], BH[half][:, 0:HALF].rearrange("p (k t) -> p k t", k=2))\
                        .then_inc(ht_taken, 1)
                if not last_one:
                    gathered(e + 2)

            def gathered_rows(i):
                n = ROWS[i]
                ve.wait_ge(y_ld[i], 32)
                for k in range(2):
                    link(ve.scalar_tensor_tensor(xh[0:n, i, :], yb[i][k][0:n, :], gates1[0:n, k, i:i + 1], xh[0:n, i, :],
                                                 ALU.mult, ALU.add))

            more = crowded(ve)
            gathered(1)
            with ve.Fori(0, NE // 2 - 1) as it:
                for s in range(2):
                    expert(it, s, False)
            expert(NE // 2 - 1, 0, False)
            ve.wait_ge(last_full, 1)
            link(ve.tensor_copy(last_share, BX[:, 0:1]))
            ve.wait_ge(product, 3 * (NE - 1))
            for i in range(TILES):
                ve.tensor_scalar(spot[:, i, :], table["row"], last_at[:, i:i + 1], last_share, ALU.is_equal, ALU.mult)\
                    .then_inc(last_ready, 1)
            for i in range(2):
                gathered_rows(i)
            expert(NE // 2 - 1, 1, True)
            for i in range(2, TILES):
                gathered_rows(i)
            ve.sem_inc(early_added, 1)

            with ve.If(more):
                with ve.Fori(0, NE) as e:
                    with ve.Fori(0, MORE) as t:
                        n = e * MORE + t
                        ve.wait_ge(o_x, n + 1)
                        ve.tensor_copy(xgT[:, 4:8, :], BX[:, :].rearrange("p (k t) -> p k t", k=4)).then_inc(o_xc, 1)
                        ve.wait_ge(o_gu, n + 1)
                        ve.wait_ge(o_sg, n + 1)
                        ve.tensor_tensor(he, sg, BU[0][:, :], ALU.mult).then_inc(o_he, 1)
                        ve.wait_ge(o_ht, n + 1)
                        ve.tensor_copy(heT, BH[0][:, :].rearrange("p (k t) -> p k t", k=4)).then_inc(o_hc, 1)
                for i in range(TILES):
                    m = ROWS[i]
                    ve.wait_ge(o_yl, 32 * (i + 1))
                    for k in range(2):
                        ve.scalar_tensor_tensor(xh[0:m, i, :], over_yb[k][0:m, :], gates2[0:m, k, i:i + 1], xh[0:m, i, :],
                                                ALU.mult, ALU.add).then_inc(o_add, 1)
                        ve.wait_ge(o_add, 2 * i + k + 1)

            for n in range(2 * TILES):
                i, half = n % TILES, n // TILES
                x = xh[0:ROWS[i], i, half * 512:(half + 1) * 512]
                ve.wait_ge(fin_full, n + 1)
                ve.tensor_tensor(x, bank[FINAL[n % 7]][0:ROWS[i], :], x, ALU.add).then_inc(y_ready, 1)

        @block.gpsimd
        def _(po):
            counts = {}

            def alone(ins, signal):
                n = counts[id(signal)] = counts.get(id(signal), 0) + 1
                ins.then_inc(signal, 1)
                po.wait_ge(signal, n)

            alone(po.memset(st[:, :], 0.0), cleared)
            alone(po.memset(proj[64:P, 4, :], 0.0), cleared)
            alone(po.memset(idx[:, :], 0), cleared)
            for j in range(5):
                po.dma_start(scratch["tokens"].rearrange("(p c) a -> p (c a)", p=P)[:, 16 * j:16 * j + 16], idx[:, 0:16])\
                    .then_inc(ld_zero, 16)
            alone(po.memset(QB[:, :, :], 0.0), qb_clear)
            po.wait_ge(heads_rt, 2)
            po.wait_ge(ld_c1, N_C1)
            for j, c in enumerate((CSLC, CWIN)):
                kk = proj[:, :, c:c + P].rearrange("p t (h d) -> p t h d", d=HD)
                r = spread(nrm[:, :, 8 + 2 * j:10 + 2 * j].rearrange("p t (h a) -> p t h a", a=1), 3, HD)
                for i in range(TILES):
                    alone(po.tensor_tensor(kk[:, i], kk[:, i], r[:, i], ALU.mult), k_step)
                g = spread(gains[:, 1 + j, :].rearrange("p (a d) -> p a d", a=1), 1, KVH)
                for i in range(TILES):
                    alone(po.tensor_tensor(kk[:, i], kk[:, i], g, ALU.mult), k_ready)
            for i in range(TILES):
                filled(po, ("in", 3, i))
            alone(po.memset(wblk[0], 0.0), cleared)
            po.wait_ge(ld_pos, 32)
            alone(po.tensor_copy(cache[0][:, 128:130, :], spread(posr.rearrange("p (a d) -> p a d", a=1), 1, 2)), extra)

            def prompt_pages(which):
                c = CCMP + P * which
                alone(po.tensor_copy(cache[1][:, 128:136, :].rearrange("p (n h) d -> p n (h d)", h=2), proj[:, 0:4, c:c + P]), extra)

            prompt_pages(0)
            filled(po, ("qT", 4))
            alone(po.memset(wblk[1], 0.0), cleared)
            for i in range(TILES):
                taken(po, ("in", 3, i))
                taken(po, ("in", 2, i))

            def store(dst, src):
                po.dma_start(dst, src).then_inc(st_out, 16)

            kvp = lambda name: out[name].rearrange("b (i p) c h d -> p (b i) (c h d)", p=P)
            kvs = lambda name: out[name].rearrange("b q c h d -> (b q) (c h d)")
            store(kvp("new_cmp_kv_prompt"), proj[:, 0:4, CCMP:CCMP + 256])
            store(kvs("new_cmp_kv_sample"), proj[0:NS, 4, CCMP:CCMP + 256])
            store(out["new_pool_prompt"][0], proj[P - 15:P, 3, CU:CU + 512])
            store(out["new_pool_sample"][:, 0:7, :], a["state_pool"][:, 8:15, :])
            for b in range(DB):
                store(out["new_pool_sample"][b, 7:15, :], proj[8 * b:8 * b + 8, 4, CU:CU + 512])
            po.wait_ge(k_ready, 2 * TILES)
            store(kvp("new_slc_kv_prompt"), proj[:, 0:4, CSLC:CSLC + 256])
            store(kvs("new_slc_kv_sample"), proj[0:NS, 4, CSLC:CSLC + 256])
            store(kvp("new_win_kv_prompt"), proj[:, 0:4, CWIN:CWIN + 256])
            for b in range(DB):
                store(out["new_win_kv_sample"][b, 504:512].rearrange("q c h d -> q (c h d)"), proj[8 * b:8 * b + 8, 4, CWIN:CWIN + 256])

            taken(po, ("qT", 4))
            po.wait_ge(qb_clear, 1)
            for s in range(2):
                for h in range(KVH):
                    for g in range(G):
                        c0 = 64 * s + 32 * h + 8 * g
                        src = qTs[64 * h:64 * h + 64, g, :].rearrange("p (t s q) -> p s t q", s=2, q=DS)[:, s]
                        alone(po.tensor_copy(QB[64 * h:64 * h + 64, s::2, c0:c0 + DS], src), qb_ready)
            filled(po, ("cmp", 1))
            prompt_pages(1)
            filled(po, "gate_rows")
            for name in (("mix_p", 3), ("mix_s", 3)):
                filled(po, name)
            po.wait_ge(kct_ready, 6)
            alone(po.memset(score, 1.0e4), z_clear)
            filled(po, ("p_o", 1, 3))
            po.wait_ge(p_a, 8)
            alone(po.memset(pw, 0.0), z_clear)
            alone(po.memset(Vblk[0:64, :], 0.0), z_clear)
            taken(po, "vcT")
            for h in range(H):
                po.dma_start(Vblk[8 * place(h):8 * place(h) + 8, 64 * place(h):64 * place(h) + 64], VC[0:8, 2, 64 * (h // G):64 * (h // G) + 64]).then_inc(vb, 16)
            for b in range(DB):
                po.wait_ge(ld_win_state[b % 4], 16 * (b // 4 + 1))
                dst = out["new_win_kv_sample"][b].rearrange("q c h d -> q (c h d)")
                po.dma_start(dst[0:120, :], wst[b % 4][8:P, 0, :]).then_inc(st_win[b % 4], 16)
                po.dma_start(dst[120:504, :].rearrange("(n p) c -> p n c", p=P), wst[b % 4][:, 1:4, :]).then_inc(st_win[b % 4], 16)

            po.wait_ge(idx_ready, 1)
            po.wait_ge(n_stored[0], 48)
            po.wait_ge(n_stored[1], 32)
            for e in range(NE):
                if e >= 2:
                    po.wait_ge(xt_full, e - 1)
                po.indirect_dma_start(xg[e % 2], None, scratch["n2"], bass.IndirectOffsetOnAxis(idx[:, e:e + 1], 0))\
                    .then_inc(xg_ld[e % 2], 16)

            po.wait_ge(slots_ready, 1)
            po.wait_ge(st_y, 16 * (NE - 1))
            po.wait_ge(product, 3 * (NE - 1))
            for i in range(TILES):
                n = ROWS[i]
                for k in range(2):
                    po.indirect_dma_start(yb[i][k][0:n, :], None, scratch["y"], bass.IndirectOffsetOnAxis(row_i[0:n, 0, k, i:i + 1], 0))\
                        .then_inc(y_ld[i], 16)

            with po.If(crowded(po)):
                po.wait_ge(ld_zero, 16 * 5)
                po.wait_ge(ld_c1, N_C1)
                for i in range(TILES):
                    n = ROWS[i]
                    for k in range(2):
                        po.indirect_dma_start(scratch["tokens"], bass.IndirectOffsetOnAxis(slot_i[0:n, k, i:i + 1], 0),
                                              tokid[0:n, i:i + 1], None).then_inc(scattered, 16)
                po.wait_ge(scattered, 16 * 2 * TILES)
                with po.Fori(0, NE) as e:
                    with po.Fori(0, MORE) as t:
                        n = e * MORE + t
                        po.wait_ge(o_x, n)
                        po.wait_ge(o_passed, n)
                        src = scratch["tokens"].rearrange("(r e) a -> r (e a)", e=NE)[bass.ds(t * P + P, P), bass.ds(e, 1)]
                        po.dma_start(over_idx[:, :], src, allow_slow_non_contiguous=True).then_inc(o_idx, 16)
                        po.wait_ge(o_idx, n * 16 + 16)
                        po.tensor_tensor(passed[:, :], over_idx[0:1, :], over_idx[0:1, :], ALU.add).then_inc(o_passed, 1)
                        po.wait_ge(xt_full, NE)
                        po.indirect_dma_start(xg[0], None, scratch["n2"], bass.IndirectOffsetOnAxis(over_idx[:, :], 0))\
                            .then_inc(o_xg, 16)
                po.wait_ge(o_p, NE * MORE)
                po.wait_ge(o_st, 16 * NE * MORE)
                for i in range(TILES):
                    m = ROWS[i]
                    if i:
                        po.wait_ge(o_add, 2 * i)
                    for k in range(2):
                        po.indirect_dma_start(over_yb[k][0:m, :], None, scratch["more_y"],
                                              bass.IndirectOffsetOnAxis(row_i[0:m, 1, k, i:i + 1], 0)).then_inc(o_yl, 16)

            for s in st_win:
                po.wait_ge(s, 64)
            po.wait_ge(st_out, 16 * N_OUT)


N_C1 = 16 * (1 + 3 + 2 + 4 + 2 + 1 + 1)
N_OUT = 4 + DB + 3 + DB


def tables():
    f = np.float32
    p, r = np.arange(P), np.arange(P)
    mats = np.zeros((P, 5, P), f)
    mats[:, 0] = np.eye(P)
    mats[:, 1] = 1
    mats[:, 2] = p[:, None] < p[None, :]
    seq, kvh, grp, q = r // 64, r // 32 % 2, r // 8 % 4, r % 8
    mats[:, 3] = (seq[:, None] == seq) & (kvh[:, None] == kvh) & (q[:, None] == q)
    mats[:, 4] = (p[:, None] // 64) == (p // 64)
    slope = np.array(SLOPES, f)[kvh * G + grp]

    small = {}
    n = np.arange(NBS)
    small["bias_c"] = -slope[:, None] * (PAST + q[:, None] - (64 * n + 63))
    tok = np.arange(NS)
    nb = np.zeros((P, PAIRS, NS), f)
    for t in range(PAIRS):
        ok = (tok[None] // 8 == 2 * t + seq[:, None]) & (tok[None] % 8 <= q[:, None])
        nb[:, t] = np.where(ok, -slope[:, None] * (q[:, None] - tok[None] % 8), NEG)
    small["new_bias"] = nb
    c = np.arange(512)
    dist = 512 + q[:, None] - c
    small["win_bias"] = np.where(dist < 512, -slope[:, None] * dist, NEG)
    head = np.zeros((P, H, 3), f)
    head[r, kvh * G + grp] = 1
    small["head"] = head
    pcb = np.zeros((P, 4, H, NBP), f)
    for i in range(4):
        d = (128 * i + p)[:, None] - (64 * np.arange(NBP) + 63)
        for h in range(H):
            pcb[:, i, place(h)] = np.where(d >= 0, -d, NEG)
    small["pc_bias"] = pcb
    small["slope"] = np.broadcast_to([SLOPES[h] for g in range(G) for h in (g, g + G)], (P, H))
    small["inv_slope"] = np.broadcast_to([1.0 / s for s in SLOPES], (P, H))
    small["prio"] = np.broadcast_to(16.0 - np.arange(NE), (P, NE))
    small["prio4"] = np.broadcast_to(4.0 - np.arange(NG), (P, NG))
    small["expert"] = np.broadcast_to(np.arange(NE), (P, NE))
    small["token"] = P * np.arange(TILES)[None] + p[:, None]
    small["tile"] = np.broadcast_to(P * np.arange(TILES), (P, TILES))
    small["row"] = np.broadcast_to(np.arange(P), (P, P))
    small["valid"] = np.array([[1.0 if x < ROWS[i] else 0.0 for i in range(TILES)] for x in range(P)])

    bands = np.zeros((P, 3, 4, P), f)
    bands_s = np.zeros((P, 2, 4, NS), f)
    for g, w in enumerate(WINDOWS):
        d = p[None, :] - p[:, None]
        cnt = np.minimum(w, p + 1)[None, :]
        bands[:, 0, g] = np.where((d >= 0) & (d < w), 1.0 / cnt, 0) - (d == 0)
        bands[:, 1, g] = np.where((d >= 0) & (d < w), 1.0 / w, 0) - (d == 0)
        bands[:, 2, g] = np.where(d + P < w, 1.0 / w, 0)
        ds = tok[None, :] % 8 - tok[:, None] % 8
        same = tok[None, :] // 8 == tok[:, None] // 8
        bands_s[0:NS, 0, g] = np.where(same & (ds >= 0) & (ds < w), 1.0 / w, 0) - (tok[None, :] == tok[:, None])
        row = np.arange(120)
        dd = 15 + tok[None, :] % 8 - row[:, None] % 15
        bands_s[0:120, 1, g] = np.where((row[:, None] // 15 == tok[None, :] // 8) & (dd < w), 1.0 / w, 0)
    sel = np.zeros((NS, PAIRS, P), f)
    for t in range(PAIRS):
        sel[(2 * t + seq) * 8 + q, t, r] = 1
    x = np.arange(SEQ)
    dd = p[:, None] + 384 - x
    return {
        "c_mats": mats,
        "c_small": np.concatenate([np.asarray(small[k], f).reshape(P, w) for k, w in SMALL], 1),
        "c_bands": np.concatenate([bands.reshape(P, -1), bands_s.reshape(P, -1)], 1),
        "c_sel": sel,
        "c_slc_bias": (-slope[:, None] * (PAST + q[:, None] - np.arange(PAST))).astype(f),
        "c_dist": np.where(dd >= 0, -dd, NEG).astype(f),
        "c_tokid": (128 * np.arange(TILES)[None] + p[:, None]).astype(np.int32),
    }


_INS = ["x_prompt", "x_sample", "cache_cmp_kv", "cache_slc_kv", "state_win_kv", "state_pool", "page_table", "norm1_g", "w_in",
        "q_norm_g", "k_norm_cmp_g", "k_norm_slc_g", "k_norm_win_g", "cmp_pos_emb", "w_cmp_k", "w_cmp_v", "pool_w", "pool_scale",
        "w_out", "norm2_g", "w_router_group", "w_router_expert", "w_gate", "w_up", "w_down"]
_OUTS = [("y_prompt", (1, SEQ, D)), ("y_sample", (DB, DS, D)),
         ("new_cmp_kv_prompt", (1, SEQ, 2, KVH, HD)), ("new_cmp_kv_sample", (DB, DS, 2, KVH, HD)),
         ("new_slc_kv_prompt", (1, SEQ, 2, KVH, HD)), ("new_slc_kv_sample", (DB, DS, 2, KVH, HD)),
         ("new_win_kv_prompt", (1, SEQ, 2, KVH, HD)), ("new_win_kv_sample", (DB, 512, 2, KVH, HD)),
         ("new_pool_prompt", (1, 15, 512)), ("new_pool_sample", (DB, 15, 512))]


def kernel(**inputs):
    import concourse.bacc as bacc
    from concourse.bass_utils import run_bass_kernel_spmd

    nc = bacc.Bacc("TRN2", target_bir_lowering=False, num_devices=1, dynamic_dma_scratch_size=8192)
    arrays, ins, outs = {}, {}, {}
    for name, value in [(n, inputs[n]) for n in _INS] + list(tables().items()):
        value = np.ascontiguousarray(value)
        arrays[f"in_{name}"] = value
        ins[name] = nc.dram_tensor(f"in_{name}", value.shape, mybir.dt.from_np(value.dtype), kind="ExternalInput").ap()
    for name, shape in _OUTS:
        outs[name] = nc.dram_tensor(f"out_{name}", shape, F32, kind="ExternalOutput").ap()
    scratch = {"n2": nc.dram_tensor("normed_rows", (NT, D), F32).ap(),
               "tokens": nc.dram_tensor("token_of_slot", (NE * CAP, 1), I32).ap(),
               "y": nc.dram_tensor("expert_rows", (EARLY, D), F32).ap(),
               "more_y": nc.dram_tensor("more_expert_rows", (NE * MORE * P, D), F32).ap()}
    hybrid_step(nc, ins, outs, scratch)
    r = run_bass_kernel_spmd(nc, [arrays], core_ids=[0])
    return tuple(r.results[0][f"out_{name}"] for name, _ in _OUTS)
```
